# Optimizing a Trainium2 kernel written in Bass

```python
import math
import jax, jax.numpy as jnp
from jax import lax
import numpy as np

D_MODEL = 1024
BATCH = 1
SEQ = 512
DEPTH = 2
DEC_BATCH = 8
DEC_SEQ = 1
PAST_LEN = 1024
PAGE_SIZE = 128

N_A_LAYERS = DEPTH // 2
N_B_LAYERS = DEPTH - N_A_LAYERS
A_HEADS = 8
A_DK = D_MODEL // A_HEADS
A_DV = D_MODEL // A_HEADS
CONV_W = 4
CHUNK = 64
A_QKV = 2 * A_HEADS * A_DK + A_HEADS * A_DV
A_IN = A_QKV + A_HEADS * A_DV + 2 * A_HEADS
B_HEADS = 16
B_KV_HEADS = 4
B_HD = D_MODEL // B_HEADS
B_GROUP = B_HEADS // B_KV_HEADS
WINDOW = 128
BLOCK = 128
ROT_DIM = B_HD // 4
ROPE_THETA = 500000.0
D_FF = 2816
N_EXPERTS = 8
TOP_K = 2
D_FF_EXPERT = 1024
N_DENSE = (DEPTH + 1) // 2
N_MOE = DEPTH // 2
EPS = 1e-6

kernel_name = "yoco_gdn_swa_sink_moe_step"

def rms_norm(x, g):
    xf = x.astype(jnp.float32)
    y = xf * lax.rsqrt(jnp.mean(xf * xf, axis=-1, keepdims=True) + EPS)
    return (y * g.astype(jnp.float32)).astype(x.dtype)

def l2_norm(x):
    xf = x.astype(jnp.float32)
    return xf * lax.rsqrt(jnp.sum(xf * xf, axis=-1, keepdims=True) + EPS)

def causal_conv(u, buf, w):
    T = u.shape[1]
    full = jnp.concatenate([buf.astype(u.dtype), u], axis=1)
    out = full[:, 0:T] * w[0]
    for j in range(1, CONV_W):
        out = out + full[:, j:j + T] * w[j]
    return jax.nn.silu(out), full[:, -(CONV_W - 1):]

def gated_delta_chunked(q, k, v, g, beta, S0):
    Bn, T, H, DK = q.shape
    DV = v.shape[-1]
    N = T // CHUNK

    def to_chunks(a):
        a = a.reshape((Bn, N, CHUNK, H) + a.shape[3:])
        return jnp.moveaxis(a, (1, 3), (0, 2))

    qc, kc, vc, gc, bc = (to_chunks(a) for a in (q, k, v, g, beta))
    gcum = jnp.cumsum(gc, axis=-1)
    idx = jnp.arange(CHUNK)
    tril = idx[:, None] >= idx[None, :]
    strict = idx[:, None] > idx[None, :]
    eye = jnp.eye(CHUNK, dtype=jnp.float32)

    def step(S, inp):
        qi, ki, vi, gi, bi = inp
        diff = gi[..., :, None] - gi[..., None, :]
        decay = jnp.where(tril, jnp.exp(jnp.where(tril, diff, 0.0)), 0.0)
        kb = ki * bi[..., None]
        L = jnp.where(strict, jnp.einsum('bhid,bhjd->bhij', kb, ki) * decay, 0.0)
        rhs = jnp.concatenate([vi * bi[..., None], kb * jnp.exp(gi)[..., None]], axis=-1)
        sol = lax.linalg.triangular_solve(L + eye, rhs, left_side=True, lower=True, unit_diagonal=True)
        u, wk = sol[..., :DV], sol[..., DV:]
        v_new = u - jnp.einsum('bhck,bhkv->bhcv', wk, S)
        attn = jnp.where(tril, jnp.einsum('bhid,bhjd->bhij', qi, ki) * decay, 0.0)
        o = (jnp.einsum('bhck,bhkv->bhcv', qi * jnp.exp(gi)[..., None], S)
             + jnp.einsum('bhij,bhjv->bhiv', attn, v_new))
        g_last = gi[..., -1]
        S = (S * jnp.exp(g_last)[..., None, None]
             + jnp.einsum('bhck,bhcv->bhkv', ki * jnp.exp(g_last[..., None] - gi)[..., None], v_new))
        return S, o

    S, o = lax.scan(step, S0, (qc, kc, vc, gcum, bc))
    o = jnp.moveaxis(o, (0, 2), (1, 3)).reshape(Bn, T, H, DV)
    return o, S

def gated_delta_recurrent(q, k, v, g, beta, S0):
    def step(S, inp):
        qt, kt, vt, gt, bt = inp
        S = S * jnp.exp(gt)[..., None, None]
        kv_mem = jnp.einsum('bhk,bhkv->bhv', kt, S)
        delta = (vt - kv_mem) * bt[..., None]
        S = S + jnp.einsum('bhk,bhv->bhkv', kt, delta)
        return S, jnp.einsum('bhk,bhkv->bhv', qt, S)

    xs = tuple(jnp.moveaxis(a, 1, 0) for a in (q, k, v, g, beta))
    S, o = lax.scan(step, S0, xs)
    return jnp.moveaxis(o, 0, 1), S

def deltanet_mixer(hn, conv_buf, S0, w_in, conv_w, A_log, dt_bias, o_norm, w_out, chunked):
    Bn, T, _ = hn.shape
    proj = hn @ w_in
    qkv, z, a, b = jnp.split(proj, [A_QKV, A_QKV + A_HEADS * A_DV, A_QKV + A_HEADS * A_DV + A_HEADS], axis=-1)
    qkv, new_buf = causal_conv(qkv, conv_buf, conv_w)
    q, k, v = jnp.split(qkv, [A_HEADS * A_DK, 2 * A_HEADS * A_DK], axis=-1)
    q = l2_norm(q.reshape(Bn, T, A_HEADS, A_DK)) * (A_DK ** -0.5)
    k = l2_norm(k.reshape(Bn, T, A_HEADS, A_DK))
    v = v.reshape(Bn, T, A_HEADS, A_DV).astype(jnp.float32)
    g = -jnp.exp(A_log.astype(jnp.float32)) * jax.nn.softplus(a.astype(jnp.float32) + dt_bias.astype(jnp.float32))
    beta = jax.nn.sigmoid(b.astype(jnp.float32))
    S0 = S0.astype(jnp.float32)
    if chunked:
        o, S = gated_delta_chunked(q, k, v, g, beta, S0)
    else:
        o, S = gated_delta_recurrent(q, k, v, g, beta, S0)
    zf = z.reshape(Bn, T, A_HEADS, A_DV).astype(jnp.float32)
    o = rms_norm(o, o_norm) * jax.nn.silu(zf)
    o = o.reshape(Bn, T, A_HEADS * A_DV).astype(hn.dtype) @ w_out
    return o, S, new_buf

def partial_rope(x, pos):
    inv = ROPE_THETA ** (-jnp.arange(0, ROT_DIM, 2, dtype=jnp.float32) / ROT_DIM)
    ang = pos.astype(jnp.float32)[:, None] * inv[None, :]
    cos = jnp.cos(ang)[None, :, None, :]
    sin = jnp.sin(ang)[None, :, None, :]
    xf = x.astype(jnp.float32)
    x1 = xf[..., :ROT_DIM // 2]
    x2 = xf[..., ROT_DIM // 2:ROT_DIM]
    out = jnp.concatenate([x1 * cos - x2 * sin, x2 * cos + x1 * sin, xf[..., ROT_DIM:]], axis=-1)
    return out.astype(x.dtype)

def shared_kv(h, kv_norm, w_kv, k_norm, pos):
    Bn, T, _ = h.shape
    kv = rms_norm(h, kv_norm) @ w_kv
    k, v = jnp.split(kv, 2, axis=-1)
    k = partial_rope(rms_norm(k.reshape(Bn, T, B_KV_HEADS, B_HD), k_norm), pos)
    v = v.reshape(Bn, T, B_KV_HEADS, B_HD)
    return k, v

def swa_query(hn, w_q, q_norm, pos):
    Bn, T, _ = hn.shape
    q = rms_norm((hn @ w_q).reshape(Bn, T, B_HEADS, B_HD), q_norm)
    return partial_rope(q, pos)

def sink_attend(s, sinks, v, spec):
    sink = sinks.astype(jnp.float32).reshape(B_KV_HEADS, B_GROUP)[:, :, None, None]
    m = jnp.maximum(jnp.max(s, axis=-1, keepdims=True), sink)
    p = jnp.exp(s - m)
    denom = jnp.sum(p, axis=-1, keepdims=True) + jnp.exp(sink - m)
    return jnp.einsum(spec, (p / denom).astype(v.dtype), v)

def swa_prompt(q, k, v, sinks):
    Bn, T = q.shape[:2]
    nb = T // BLOCK
    qb = q.reshape(Bn, nb, BLOCK, B_KV_HEADS, B_GROUP, B_HD)
    kb = k.reshape(Bn, nb, BLOCK, B_KV_HEADS, B_HD)
    vb = v.reshape(Bn, nb, BLOCK, B_KV_HEADS, B_HD)
    kk = jnp.concatenate([jnp.concatenate([jnp.zeros_like(kb[:, :1]), kb[:, :-1]], axis=1), kb], axis=2)
    vv = jnp.concatenate([jnp.concatenate([jnp.zeros_like(vb[:, :1]), vb[:, :-1]], axis=1), vb], axis=2)
    s = jnp.einsum('bnqhgd,bnkhd->bnhgqk', qb, kk).astype(jnp.float32) * (B_HD ** -0.5)
    blk = jnp.arange(nb)[:, None, None]
    qpos = blk * BLOCK + jnp.arange(BLOCK)[None, :, None]
    kpos = (blk - 1) * BLOCK + jnp.arange(2 * BLOCK)[None, None, :]
    d = qpos - kpos
    mask = (d >= 0) & (d <= WINDOW) & (kpos >= 0)
    s = jnp.where(mask[None, :, None, None], s, -jnp.inf)
    o = sink_attend(s, sinks, vv, 'bnhgqk,bnkhd->bnqhgd')
    return o.reshape(Bn, T, B_HEADS * B_HD)

def swa_sample(q, k_all, v_all, sinks, pos, w_cache):
    Bn, T = q.shape[:2]
    kpos = jnp.concatenate([PAST_LEN - w_cache + jnp.arange(w_cache, dtype=jnp.int32), pos])
    qb = q.reshape(Bn, T, B_KV_HEADS, B_GROUP, B_HD)
    s = jnp.einsum('bqhgd,bkhd->bhgqk', qb, k_all).astype(jnp.float32) * (B_HD ** -0.5)
    d = pos[:, None] - kpos[None, :]
    mask = (d >= 0) & (d <= WINDOW)
    s = jnp.where(mask, s, -jnp.inf)
    o = sink_attend(s, sinks, v_all, 'bhgqk,bkhd->bqhgd')
    return o.reshape(Bn, T, B_HEADS * B_HD)

def swiglu(hn, w_gu, w_down):
    gte, up = jnp.split(hn @ w_gu, 2, axis=-1)
    return (jax.nn.silu(gte) * up) @ w_down

def moe_swiglu(hn, router_w, router_b, w_gu, w_down):
    logits = (hn @ router_w + router_b).astype(jnp.float32)
    top_v, top_i = lax.top_k(logits, TOP_K)
    gates = jax.nn.softmax(top_v, axis=-1)
    combine = jnp.sum(jax.nn.one_hot(top_i, N_EXPERTS, dtype=jnp.float32) * gates[..., None], axis=-2)
    out = jnp.zeros_like(hn)
    for e in range(N_EXPERTS):
        out = out + combine[..., e:e + 1].astype(hn.dtype) * swiglu(hn, w_gu[e], w_down[e])
    return out

def run_group(x, pos, conv_state, delta_state, k_win, v_win, is_prompt, p):
    h = x
    new_conv, new_delta = [], []
    k_sh = v_sh = k_all = v_all = new_k_win = new_v_win = None
    for l in range(DEPTH):
        if l < N_A_LAYERS:
            o, s_new, c_new = deltanet_mixer(
                rms_norm(h, p['a_norm'][l]), conv_state[l], delta_state[l], p['a_w_in'][l], p['a_conv_w'][l],
                p['a_A_log'][l], p['a_dt_bias'][l], p['a_o_norm'][l], p['a_w_out'][l], is_prompt)
            new_conv.append(c_new.astype(conv_state.dtype))
            new_delta.append(s_new.astype(delta_state.dtype))
        else:
            j = l - N_A_LAYERS
            if j == 0:
                k_sh, v_sh = shared_kv(h, p['kv_norm'], p['w_kv'], p['k_norm'], pos)
                if is_prompt:
                    w_p = min(WINDOW, k_sh.shape[1])
                    new_k_win, new_v_win = k_sh[:, -w_p:], v_sh[:, -w_p:]
                else:
                    k_all = jnp.concatenate([k_win.astype(k_sh.dtype), k_sh], axis=1)
                    v_all = jnp.concatenate([v_win.astype(v_sh.dtype), v_sh], axis=1)
                    new_k_win = k_all[:, -k_win.shape[1]:].astype(k_win.dtype)
                    new_v_win = v_all[:, -v_win.shape[1]:].astype(v_win.dtype)
            q = swa_query(rms_norm(h, p['b_norm'][j]), p['b_w_q'][j], p['b_q_norm'][j], pos)
            if is_prompt:
                o = swa_prompt(q, k_sh, v_sh, p['b_sinks'][j])
            else:
                o = swa_sample(q, k_all, v_all, p['b_sinks'][j], pos, k_win.shape[1])
            o = o @ p['b_w_o'][j]
        h = h + o
        hn = rms_norm(h, p['ffn_norm'][l])
        if l % 2 == 0:
            f = swiglu(hn, p['dense_w_gu'][l // 2], p['dense_w_down'][l // 2])
        else:
            f = moe_swiglu(hn, p['moe_router'][l // 2], p['moe_router_b'][l // 2],
                           p['moe_w_gu'][l // 2], p['moe_w_down'][l // 2])
        h = h + f
    return h, jnp.stack(new_conv), jnp.stack(new_delta), new_k_win, new_v_win

def setup_inputs(seed: int = 0) -> dict:
    key = jax.random.key(seed)
    ks = iter(jax.random.split(key, 40))

    def nrm(shape, scale):
        return scale * jax.random.normal(next(ks), shape, jnp.float32)

    def gain(shape):
        return 1.0 + 0.05 * jax.random.normal(next(ks), shape, jnp.float32)

    w_cache = min(WINDOW, PAST_LEN)
    dt = jax.random.uniform(next(ks), (N_A_LAYERS, A_HEADS), jnp.float32, minval=1e-3, maxval=0.1)
    return {
        'x_prompt': nrm((BATCH, SEQ, D_MODEL), 1.0),
        'x_sample': nrm((DEC_BATCH, DEC_SEQ, D_MODEL), 1.0),
        'state_conv': nrm((N_A_LAYERS, DEC_BATCH, CONV_W - 1, A_QKV), 1.0),
        'state_delta': nrm((N_A_LAYERS, DEC_BATCH, A_HEADS, A_DK, A_DV), A_DK ** -0.5),
        'cache_k_win': nrm((DEC_BATCH, w_cache, B_KV_HEADS, B_HD), 1.0),
        'cache_v_win': nrm((DEC_BATCH, w_cache, B_KV_HEADS, B_HD), 1.0),
        'a_norm': gain((N_A_LAYERS, D_MODEL)),
        'a_w_in': nrm((N_A_LAYERS, D_MODEL, A_IN), D_MODEL ** -0.5),
        'a_conv_w': nrm((N_A_LAYERS, CONV_W, A_QKV), CONV_W ** -0.5),
        'a_A_log': jnp.log(jax.random.uniform(next(ks), (N_A_LAYERS, A_HEADS), jnp.float32, minval=1.0, maxval=16.0)),
        'a_dt_bias': dt + jnp.log(-jnp.expm1(-dt)),
        'a_o_norm': gain((N_A_LAYERS, A_DV)),
        'a_w_out': nrm((N_A_LAYERS, A_HEADS * A_DV, D_MODEL), (A_HEADS * A_DV) ** -0.5),
        'kv_norm': gain((D_MODEL,)),
        'w_kv': nrm((D_MODEL, 2 * B_KV_HEADS * B_HD), D_MODEL ** -0.5),
        'k_norm': gain((B_HD,)),
        'b_norm': gain((N_B_LAYERS, D_MODEL)),
        'b_w_q': nrm((N_B_LAYERS, D_MODEL, B_HEADS * B_HD), D_MODEL ** -0.5),
        'b_q_norm': gain((N_B_LAYERS, B_HD)),
        'b_sinks': nrm((N_B_LAYERS, B_HEADS), 0.5),
        'b_w_o': nrm((N_B_LAYERS, B_HEADS * B_HD, D_MODEL), (B_HEADS * B_HD) ** -0.5),
        'ffn_norm': gain((DEPTH, D_MODEL)),
        'dense_w_gu': nrm((N_DENSE, D_MODEL, 2 * D_FF), D_MODEL ** -0.5),
        'dense_w_down': nrm((N_DENSE, D_FF, D_MODEL), D_FF ** -0.5),
        'moe_router': nrm((N_MOE, D_MODEL, N_EXPERTS), D_MODEL ** -0.5),
        'moe_router_b': nrm((N_MOE, N_EXPERTS), 0.01),
        'moe_w_gu': nrm((N_MOE, N_EXPERTS, D_MODEL, 2 * D_FF_EXPERT), D_MODEL ** -0.5),
        'moe_w_down': nrm((N_MOE, N_EXPERTS, D_FF_EXPERT, D_MODEL), D_FF_EXPERT ** -0.5),
    }

def reference(x_prompt, x_sample, state_conv, state_delta, cache_k_win, cache_v_win,
              a_norm, a_w_in, a_conv_w, a_A_log, a_dt_bias, a_o_norm, a_w_out,
              kv_norm, w_kv, k_norm,
              b_norm, b_w_q, b_q_norm, b_sinks, b_w_o,
              ffn_norm, dense_w_gu, dense_w_down, moe_router, moe_router_b, moe_w_gu, moe_w_down):
    p = {
        'a_norm': a_norm, 'a_w_in': a_w_in, 'a_conv_w': a_conv_w, 'a_A_log': a_A_log,
        'a_dt_bias': a_dt_bias, 'a_o_norm': a_o_norm, 'a_w_out': a_w_out,
        'kv_norm': kv_norm, 'w_kv': w_kv, 'k_norm': k_norm,
        'b_norm': b_norm, 'b_w_q': b_w_q, 'b_q_norm': b_q_norm, 'b_sinks': b_sinks, 'b_w_o': b_w_o,
        'ffn_norm': ffn_norm, 'dense_w_gu': dense_w_gu, 'dense_w_down': dense_w_down,
        'moe_router': moe_router, 'moe_router_b': moe_router_b, 'moe_w_gu': moe_w_gu, 'moe_w_down': moe_w_down,
    }
    n_p = x_prompt.shape[0]
    pos_p = jnp.arange(x_prompt.shape[1], dtype=jnp.int32)
    conv0 = jnp.zeros((N_A_LAYERS, n_p, CONV_W - 1, A_QKV), state_conv.dtype)
    delta0 = jnp.zeros((N_A_LAYERS, n_p, A_HEADS, A_DK, A_DV), state_delta.dtype)
    y_prompt, conv_p, delta_p, kw_p, vw_p = run_group(x_prompt, pos_p, conv0, delta0, None, None, True, p)
    pos_s = PAST_LEN + jnp.arange(x_sample.shape[1], dtype=jnp.int32)
    y_sample, conv_s, delta_s, kw_s, vw_s = run_group(
        x_sample, pos_s, state_conv, state_delta, cache_k_win, cache_v_win, False, p)
    return (y_prompt, y_sample, conv_p, conv_s, delta_p, delta_s, kw_p, kw_s, vw_p, vw_s)


_drawn_inputs = setup_inputs


def setup_inputs(seed=0):
    import zlib

    import numpy as np

    out = dict(_drawn_inputs(seed))
    spreads = {}
    factors = {'b_norm': 3.395, 'b_q_norm': 3.149, 'b_sinks': 5.633}
    for name, (base, spread) in spreads.items():
        noise = np.random.default_rng([zlib.crc32(name.encode()), seed]).standard_normal(out[name].shape)
        drawn = base * np.exp(spread * noise) if base else spread * noise
        out[name] = __import__('jax').numpy.asarray(drawn.astype(out[name].dtype))
    for name, factor in factors.items():
        out[name] = (out[name] * factor).astype(out[name].dtype)
    return out
```

```python
from contextlib import ExitStack

import numpy as np
import concourse.bass as bass
from concourse import mybir

F32 = mybir.dt.float32
F32R = mybir.dt.float32r
ALU = mybir.AluOpType
ACT = mybir.ActivationFunctionType
AX = mybir.AxisListType.X
ds = bass.ds

D = 1024
KT = D // 128
TP, TS = 512, 8
NT = TP + TS
HALF = NT // 2
AH, DK = 8, 128
NQKV = 3 * AH
C = 128
NCH = TP // C
FF = 2816
NFF = FF // 128
NE, FE = 8, 1024
BH, BKV, HD = 16, 4, 64
WIN = 128
PAST = 1024
EPS = 1e-6
NEG = -1e30
CHUNK = 2048

CI, CONE, CU, CM16, CBO, CROT, CD0, CD1, CRD0, CRD1, CFOLD = (128 * i for i in range(11))
CCOS = 128 * 11
CSIN = CCOS + NT
CMASK = CSIN + NT
CNEW = CMASK + 256
CEXP = CNEW + 8
CHALF = CEXP + 8
CEPS = CHALF + 2
CHEAD = CEPS + 1
NCST = CHEAD + 16

VA, VKV, VB, VF, VO, VK, VQ = 0, 8, 16, 24, 40, 41, 42
NVEC = 43


def constants():
    t = np.zeros((128, NCST), np.float32)
    i = np.arange(128)
    eye = np.eye(128, dtype=np.float32)
    t[:, CI:CI + 128] = eye
    t[:, CONE:CONE + 128] = 1.0
    t[:, CU:CU + 128] = i[:, None] <= i[None, :]
    t[:, CM16:CM16 + 128] = i[:, None] // 16 == i[None, :] // 16
    t[:, CBO:CBO + 128] = i[:, None] // HD == i[None, :] // HD
    rot_half = HD // 8
    rot = np.zeros((128, 128), np.float32)
    for m in range(128):
        if m % HD < rot_half:
            rot[m + rot_half, m] = -1.0
        elif m % HD < 2 * rot_half:
            rot[m - rot_half, m] = 1.0
    dup = [np.zeros((128, 128), np.float32) for _ in range(2)]
    for m in range(128):
        dup[0][m % HD, m] = 1.0
        dup[1][HD + m % HD, m] = 1.0
    t[:, CROT:CROT + 128] = rot
    t[:, CD0:CD0 + 128] = dup[0]
    t[:, CD1:CD1 + 128] = dup[1]
    t[:, CRD0:CRD0 + 128] = dup[0] @ rot
    t[:, CRD1:CRD1 + 128] = dup[1] @ rot
    t[:, CFOLD:CFOLD + 128] = i[:, None] % HD == i[None, :] % HD
    pos = np.concatenate([np.arange(TP), np.full(TS, PAST)]).astype(np.float32)
    rd = 2 * rot_half
    inv = np.power(np.float32(500000.0), -np.arange(0, rd, 2, dtype=np.float32) / np.float32(rd)).astype(np.float32)
    ang = (pos[None, :] * inv[:, None]).astype(np.float32).astype(np.float64)
    t[:, CCOS:CCOS + NT] = 1.0
    for m in range(128):
        if m % HD < rd:
            t[m, CCOS:CCOS + NT] = np.cos(ang[m % HD % rot_half])
            t[m, CSIN:CSIN + NT] = np.sin(ang[m % HD % rot_half])
    t[:, CMASK:CMASK + 128] = np.where(i[None, :] >= i[:, None], 0.0, NEG)
    t[:, CMASK + 128:CMASK + 256] = np.where(i[None, :] <= i[:, None], 0.0, NEG)
    t[:, CNEW:CNEW + 8] = np.where(np.arange(8)[None, :] == i[:, None] % 8, 0.0, NEG)
    t[:, CEXP:CEXP + 8] = 100 + np.arange(8)[None, :]
    t[:64, CHALF] = 1.0
    t[64:, CHALF + 1] = 1.0
    t[:, CEPS] = EPS
    t[:, CHEAD:CHEAD + 16] = i[:, None] // 8 == np.arange(16)[None, :]
    return {"constants": t}


class Chain:

    def __init__(self, eng, sem, base=0):
        self.eng, self.sem, self.base, self.k = eng, sem, base, 0

    def link(self, ins):
        self.k += 1
        ins.then_inc(self.sem, 1)
        self.eng.wait_ge(self.sem, self.base + self.k)


class Core:
    pass


class Layer:
    pass


def split_buffers(nc, ctx, name):
    return [ctx.enter_context(nc.sbuf_tensor(f"{name}_{part}", [128, KT, NT], F32R)) for part in ("hi", "lo")]


def shared_buffers(nc, ctx):
    c = Core()
    sb = lambda name, shape, dt=F32: ctx.enter_context(nc.sbuf_tensor(name, shape, dt))
    c.sem = lambda name: ctx.enter_context(nc.semaphore(name))
    c.cst = sb("cst", [128, NCST])
    c.vec = sb("vec", [128, NVEC])
    c.h = sb("h", [128, KT, NT])
    c.w_raw = sb("w_raw", [128, 2, CHUNK])
    c.w_hi = sb("w_hi", [128, 2, CHUNK], F32R)
    c.w_lo = sb("w_lo", [128, 2, CHUNK], F32R)
    c.scratch = sb("scratch", [128, 2, NT])
    c.pair = sb("pair", [128, 2, NT])
    c.rstd = c.scratch[:, 0]
    c.P = ctx.enter_context(nc.psum_tensor("P", [128, 8, 512], F32))
    c.raw_loaded = [c.sem("raw_loaded0"), c.sem("raw_loaded1")]
    c.hi_done = c.sem("hi_done")
    c.h_even = c.sem("h_even")
    c.lo_done = c.sem("lo_done")
    c.norm_sems = [c.sem("norm_" + s) for s in ("squared", "summed", "ms_ready", "root_ready", "scaled",
                                                "hi_ready", "low_ready", "own")]
    c.norms = 0
    return c


def cols(c, at, n=128):
    return c.cst[:, at:at + n]


def slot(c, s):
    return c.P[:, 2 * s:2 * s + 2, 0:HALF]


def halves(ap):
    return ap.rearrange("p (b t) -> p b t", b=2)



def load_chunk(c, sp, number, s, src, wait=True):
    if wait:
        sp.wait_ge(c.lo_done, number - 1)
    k_tiles, width = (src[0] if isinstance(src, tuple) else src).shape[1:]
    if isinstance(src, tuple):
        dst = c.w_raw[:, s, 0:k_tiles * 2 * width].rearrange("p (k g f) -> p k g f", k=k_tiles, g=2)
        parts = [(dst[:, :, g], src[g]) for g in range(2)]
    else:
        dst = c.w_raw[:, s, 0:k_tiles * width].rearrange("p (k f) -> p k f", k=k_tiles)
        half = k_tiles // 2
        parts = [(dst[:, 0:half], src[:, 0:half]), (dst[:, half:], src[:, half:])]
    for to, of in parts:
        sp.dma_start(to, of).then_inc(c.raw_loaded[s], 16)


def gate_and_up(w, width):
    w = w.rearrange("(k p) (g f) -> p g k f", p=128, g=2)
    return lambda at: tuple(w[:, g, :, ds(at, width)] for g in range(2))


def three_products(nc, out, w_hi, w_lo, x_hi, x_lo, first, last):
    for n, (w, x) in enumerate(((w_hi, x_hi), (w_hi, x_lo), (w_lo, x_hi))):
        for b in range(2):
            ins = nc.tensor.matmul(out[:, b], w, x[:, b * HALF:(b + 1) * HALF],
                                   start=(first and n == 0), stop=(last and n == 2))
    return ins


class Stream:

    def __init__(self, base, n, src):
        assert base % 2 == 0 and n % 2 == 0
        self.base, self.n, self.src = base, n, src
        self.end = base + n

    def number(self, i, j):
        return i * 2 + (self.base + j)

    def start(self, c, sp, wait=True):
        for j in range(2):
            load_chunk(c, sp, self.base + j, j, self.src(0, j), wait)

    def rest(self, c, sp):
        with sp.Fori(1, self.n // 2) as i:
            for j in range(2):
                load_chunk(c, sp, self.number(i, j), j, self.src(i, j))

    def split_hi(self, nc, c, act, i, j):
        act.wait_ge(c.raw_loaded[j % 2], i * 32 + 32 * ((self.base + j) // 2 + 1))
        nc.scalar.activation(c.w_hi[:, j % 2], c.w_raw[:, j % 2], ACT.Copy).then_inc(c.hi_done, 1)

    def split_lo(self, nc, c, dve, i, j):
        dve.wait_ge(c.hi_done, self.number(i, j) + 1)
        nc.vector.tensor_tensor(c.w_lo[:, j % 2], c.w_raw[:, j % 2], c.w_hi[:, j % 2].bitcast(F32),
                                ALU.subtract).then_inc(c.lo_done, 1)


def over(eng, n, body):
    if n > 1:
        with eng.Fori(0, n - 1) as i:
            body(i, False)
    body(n - 1, True)


def square_tensor(nc, c, pe, st, ready, evacuated):
    def body(i, last):
        for j in range(2):
            pe.wait_ge(c.lo_done, st.number(i, j) + 1)
            for m in range(2):
                g = 2 * j + m
                pe.wait_ge(evacuated, i * 4 + (g + 1))
                for k in range(KT):
                    at = k * 256 + m * 128
                    ins = three_products(nc, slot(c, g), c.w_hi[:, j, at:at + 128], c.w_lo[:, j, at:at + 128],
                                         c.x_hi[:, k], c.x_lo[:, k], k == 0, k == KT - 1)
                ins.then_inc(ready, 1)
    over(pe, st.n // 2, body)


def norm_phase(nc, c, gain):
    squared, summed, ms_ready, root_ready, scaled, hi_ready, low_ready, own = c.norm_sems
    one, all_ = c.norms, c.norms * KT
    c.norms += 1
    with nc.Block() as block:
        @block.scalar
        def _(act):
            for k in range(KT):
                if k >= 2:
                    act.wait_ge(summed, all_ + k - 1)
                nc.scalar.activation(c.pair[:, k % 2], c.h[:, k], ACT.Square).then_inc(squared, 1)
            act.wait_ge(ms_ready, one + 1)
            nc.scalar.activation(c.rstd, c.rstd, ACT.Sqrt).then_inc(root_ready, 1)
            for k in range(KT):
                act.wait_ge(scaled, all_ + k + 1)
                nc.scalar.activation(c.x_hi[:, k], c.pair[:, k % 2], ACT.Copy).then_inc(hi_ready, 1)

        @block.tensor
        def _(pe):
            for k in range(KT):
                pe.wait_ge(squared, all_ + k + 1)
                for b in range(2):
                    ins = pe.matmul(c.P[:, b, 0:HALF], cols(c, CONE), c.pair[:, k % 2, b * HALF:(b + 1) * HALF],
                                    start=(k == 0), stop=(k == KT - 1))
                ins.then_inc(summed, 1)

        @block.vector
        def _(dve):
            dve.wait_ge(summed, all_ + KT)
            nc.vector.tensor_scalar(halves(c.rstd), slot(c, 0), 1.0 / D, EPS, ALU.mult, ALU.add).then_inc(ms_ready, 1)
            dve.wait_ge(root_ready, one + 1)
            nc.vector.reciprocal(c.rstd, c.rstd).then_inc(own, 1)
            dve.wait_ge(own, one + 1)
            for k in range(KT + 1):
                if k < KT:
                    if k >= 2:
                        dve.wait_ge(low_ready, all_ + k - 1)
                    nc.vector.scalar_tensor_tensor(c.pair[:, k % 2], c.h[:, k], c.vec[:, gain + k:gain + k + 1],
                                                   c.rstd, ALU.mult, ALU.mult).then_inc(scaled, 1)
                if k >= 1:
                    dve.wait_ge(hi_ready, all_ + k)
                    nc.vector.tensor_tensor(c.x_lo[:, k - 1], c.pair[:, (k - 1) % 2],
                                            c.x_hi[:, k - 1].bitcast(F32), ALU.subtract).then_inc(low_ready, 1)


def load_phase(nc, c, io, L, sp_work):
    with ExitStack() as ctx:
        xt = ctx.enter_context(nc.sbuf_tensor("x_tokens", [128, 5, D], F32))
        rows = ctx.enter_context(nc.sbuf_tensor("vector_rows", [128, 128], F32))
        crow = ctx.enter_context(nc.sbuf_tensor("conv_rows", [128, 128], F32))
        srow = ctx.enter_context(nc.sbuf_tensor("state_rows", [TS * 3, NQKV * 128], F32))
        in_c, in_v, in_x, in_s = c.sem("in_constants"), c.sem("in_vectors"), c.sem("in_tokens"), c.sem("in_state")
        turned, read = c.sem("load_turned"), c.sem("load_read")
        with nc.Block() as block:
            @block.sync
            def _(sp):
                sp.dma_start(c.cst[:], io["constants"]).then_inc(in_c, 16)
                for t in range(4):
                    sp.dma_start(xt[:, t], io["x_prompt"][0, t * 128:(t + 1) * 128]).then_inc(in_x, 16)
                sp.dma_start(xt[0:TS, 4], io["x_sample"].rearrange("b s d -> (b s) d")).then_inc(in_x, 16)
                sp_work(sp)
                sp.dma_start(srow[:], io["state_conv"][0].rearrange("b j f -> (b j) f")).then_inc(in_s, 16)

            @block.scalar
            def _(act):
                as_rows = lambda v: v.rearrange("(k p) -> k p", p=128)
                parts = [(VA, 8, as_rows(io["a_norm"][0])), (VKV, 8, as_rows(io["kv_norm"])),
                         (VB, 8, as_rows(io["b_norm"][0])), (VF, 8, as_rows(io["ffn_norm"][0])),
                         (VF + 8, 8, as_rows(io["ffn_norm"][1])), (VO, 1, io["a_o_norm"])]
                for at, n, src in parts:
                    act.dma_start(rows[at:at + n, :], src).then_inc(in_v, 16)
                for at, v in ((VK, io["k_norm"].rearrange("(a d) -> a d", a=1)), (VQ, io["b_q_norm"])):
                    for half in range(2):
                        act.dma_start(rows[at:at + 1, half * HD:(half + 1) * HD], v).then_inc(in_v, 16)
                act.dma_start(crow[0:96, :], io["a_conv_w"][0].rearrange("j (m p) -> (j m) p", p=128)).then_inc(in_v, 16)
                act.dma_start(L.a_log[:], io["a_A_log"].rearrange("a h -> h a")).then_inc(in_v, 16)
                act.dma_start(L.dt_bias[:], io["a_dt_bias"].rearrange("a h -> h a")).then_inc(in_v, 16)
                for k in range(1, KT, 2):
                    act.wait_ge(turned, k + 1)
                    nc.scalar.activation(c.h[:, k, 0:TP], c.P[:, k % 4], ACT.Copy).then_inc(read, 1)

            @block.tensor
            def _(pe):
                ident = cols(c, CI)
                pe.wait_ge(in_c, 16)
                pe.wait_ge(in_x, 80)
                for k in range(KT):
                    if k >= 4:
                        pe.wait_ge(c.h_even, (k - 4) // 2 + 1)
                        if k % 2:
                            pe.wait_ge(read, (k - 4) // 2 + 1)
                    for t in range(4):
                        ins = pe.transpose(c.P[:, k % 4, t * 128:(t + 1) * 128], xt[:, t, k * 128:(k + 1) * 128], ident)
                    ins.then_inc(turned, 1)
                for k in range(KT):
                    ins = pe.transpose(c.P[:, 4, k * TS:(k + 1) * TS], xt[0:TS, 4, k * 128:(k + 1) * 128], cols(c, CI)[0:TS, 0:TS])
                ins.then_inc(turned, 1)
                pe.wait_ge(in_v, 16 * 13)
                pe.transpose(c.P[:, 5, 0:NVEC], rows[0:NVEC, :], cols(c, CI)[0:NVEC, 0:NVEC]).then_inc(turned, 1)
                pe.transpose(c.P[:, 6, 0:96], crow[0:96, :], cols(c, CI)[0:96, 0:96]).then_inc(turned, 1)
                pe.wait_ge(in_s, 16)
                for m in range(NQKV):
                    if m == 0:
                        pe.wait_ge(c.h_even, 4)
                        pe.wait_ge(read, 4)
                    ins = pe.transpose(c.P[:, m // AH, (m % AH) * 24:(m % AH) * 24 + 24],
                                       srow[:, m * 128:(m + 1) * 128], cols(c, CI)[0:24, 0:24])
                ins.then_inc(turned, 1)

            @block.vector
            def _(dve):
                for k in range(0, KT, 2):
                    dve.wait_ge(turned, k + 1)
                    nc.vector.tensor_copy(c.h[:, k, 0:TP], c.P[:, k % 4]).then_inc(c.h_even, 1)
                dve.wait_ge(turned, KT + 1)
                nc.vector.tensor_copy(c.h[:, :, TP:NT], c.P[:, 4, 0:KT * TS].rearrange("p (k t) -> p k t", k=KT))
                dve.wait_ge(turned, KT + 2)
                nc.vector.tensor_copy(c.vec[:], c.P[:, 5, 0:NVEC])
                dve.wait_ge(turned, KT + 3)
                nc.vector.tensor_copy(L.conv_w[:], c.P[:, 6, 0:96])
                dve.wait_ge(turned, KT + 4)
                for part in range(3):
                    nc.vector.tensor_copy(L.conv_state[:, part * AH:(part + 1) * AH],
                                          c.P[:, part, 0:192].rearrange("p (m r) -> p m r", m=AH))


def project_in_phase(nc, c, st, sp_next, L):
    sem = lambda s: c.sem(f"in_{s}")
    ready, evacuated, convolved, y_free, own = (sem(s) for s in ("ready", "evacuated", "convolved", "y_free", "own"))
    with nc.Block() as block:
        @block.sync
        def _(sp):
            st.rest(c, sp)
            sp_next(sp)

        @block.tensor
        def _(pe):
            square_tensor(nc, c, pe, st, ready, evacuated)

        @block.scalar
        def _(act):
            act.sem_inc(evacuated, 4)
            act.sem_inc(y_free, 2)
            st.split_hi(nc, c, act, 0, 0)

            def silu(m, y):
                nc.scalar.activation(L.qkv[:, m], L.y[:, y], ACT.Silu).then_inc(y_free, 1)

            def qkv(i, first):
                for j in range(2):
                    st.split_hi(nc, c, act, i, j + 1)
                    for m in range(2):
                        g = 2 * j + m
                        act.wait_ge(ready, i * 4 + (g + 1))
                        nc.scalar.activation(halves(L.u[:, g % 2, 3:3 + NT]), slot(c, g), ACT.Copy).then_inc(evacuated, 1)
                        if not (first and g == 0):
                            act.wait_ge(convolved, i * 4 + g)
                            silu(i * 4 + (g - 1) if g else i * 4 - 1, (g - 1) % 2)
            qkv(0, True)
            with act.Fori(1, NQKV // 4) as i:
                qkv(i, False)
            act.wait_ge(convolved, NQKV)
            silu(NQKV - 1, 1)
            for i in range(NQKV // 4, st.n // 2):
                for j in range(2):
                    if 2 * i + j + 1 < st.n:
                        st.split_hi(nc, c, act, i, j + 1)
                    for m in range(2):
                        g = 2 * j + m
                        act.wait_ge(ready, i * 4 + (g + 1))
                        nc.scalar.activation(halves(L.z[:, 4 * i + g - NQKV]), slot(c, g), ACT.Silu).then_inc(evacuated, 1)

        @block.vector
        def _(dve):
            nc.vector.memset(L.u[:, :, 0:3], 0.0)
            sw = lambda j: L.conv_w[:, j * NQKV:(j + 1) * NQKV].unsqueeze(2).broadcast_to([128, NQKV, TS])
            rows = L.conv_state[:].rearrange("p m (b j) -> p m b j", j=3)
            chain = Chain(dve, own)
            chain.link(nc.vector.tensor_tensor(L.from_state[:], rows[:, :, :, 0], sw(0), ALU.mult))
            for j in (1, 2):
                chain.link(nc.vector.tensor_tensor(L.state_term[:], rows[:, :, :, j], sw(j), ALU.mult))
                chain.link(nc.vector.tensor_tensor(L.from_state[:], L.from_state[:], L.state_term[:], ALU.add))
            st.split_lo(nc, c, dve, 0, 0)
            done = chain.k

            with dve.Fori(0, NQKV // 4) as i:
                chain = Chain(dve, own, i * 20 + done)
                for j in range(2):
                    st.split_lo(nc, c, dve, i, j + 1)
                    for m in range(2):
                        g = 2 * j + m
                        u, y = L.u[:, g % 2], L.y[:, g % 2]
                        tile = lambda t: t[:, ds(i * 4 + g, 1)].rearrange("p a t -> p (a t)")
                        w = lambda tap: L.conv_w[:, ds(i * 4 + (tap * NQKV + g), 1)]
                        dve.wait_ge(evacuated, i * 4 + (g + 5))
                        dve.wait_ge(y_free, i * 4 + (g + 1))
                        chain.link(nc.vector.tensor_scalar(y, u[:, 3:3 + NT], w(3), None, ALU.mult))
                        for tap in (2, 1, 0):
                            chain.link(nc.vector.scalar_tensor_tensor(
                                y[:, 0:TP], u[:, tap:tap + TP], w(tap), y[:, 0:TP], ALU.mult, ALU.add))
                        chain.link(nc.vector.tensor_copy(tile(L.edge), u[:, TP:TP + 11]))
                        nc.vector.tensor_tensor(y[:, TP:NT], y[:, TP:NT], tile(L.from_state), ALU.add).then_inc(convolved, 1)
            for l in range(NQKV // 2 + 1, st.n):
                st.split_lo(nc, c, dve, l // 2, l % 2)


def narrow_product(nc, pe, out, w_hi, w_lo, c):
    for k in range(KT):
        ins = three_products(nc, out, w_hi[:, k], w_lo[:, k], c.x_hi[:, k], c.x_lo[:, k], k == 0, k == KT - 1)
    return ins


def gates_phase(nc, c, io, L):
    sem = lambda s: c.sem(f"gate_{s}")
    cleared, loaded, hi_ready, lo_ready, ab_ready, own_v, own_a = (sem(s) for s in
        ("cleared", "loaded", "hi_ready", "lo_ready", "ab_ready", "own_vector", "own_scalar"))
    act_step, dve_step, turned = (sem(s) for s in ("act_step", "dve_step", "turned"))
    w, w_hi, w_lo = L.ab_raw, L.ab_hi, L.ab_lo
    gb = c.scratch[:, 0]
    t1, t2, t3 = c.pair[0:AH, 0], c.pair[0:AH, 1], c.scratch[0:AH, 1]
    with nc.Block() as block:
        @block.gpsimd
        def _(pool):
            nc.gpsimd.memset(w[:], 0.0).then_inc(cleared, 1)
            nc.gpsimd.memset(gb, 0.0).then_inc(cleared, 1)

        @block.sync
        def _(sp):
            w_in = io["a_w_in"][0].rearrange("(k p) n -> p k n", p=128)
            sp.wait_ge(cleared, 1)
            for at, col in ((0, NQKV * 128 + D), (32, NQKV * 128 + D + AH)):
                sp.dma_start(w[:, :, at:at + AH], w_in[:, :, col:col + AH]).then_inc(loaded, 16)

        @block.tensor
        def _(pe):
            pe.wait_ge(lo_ready, 1)
            narrow_product(nc, pe, slot(c, 0), w_hi, w_lo, c).then_inc(ab_ready, 1)
            pe.wait_ge(dve_step, 5)
            for n in range(NCH):
                ins = pe.transpose(c.P[:, 2, n * 128:(n + 1) * 128], gb[:, n * C:(n + 1) * C], cols(c, CI))
            ins.then_inc(turned, 1)
            pe.wait_ge(dve_step, 7)
            pe.matmul(c.P[:, 3, 0:128], cols(c, CONE), L.spread[:], start=True, stop=True).then_inc(turned, 1)
            pe.wait_ge(dve_step, 8)
            pe.matmul(c.P[:, 4, 0:NCH * AH], cols(c, CU), L.g_tok[:].rearrange("p n h -> p (n h)"),
                      start=True, stop=True).then_inc(turned, 1)

        @block.scalar
        def _(act):
            act.wait_ge(loaded, 32)
            nc.scalar.activation(w_hi[:], w[:], ACT.Copy).then_inc(hi_ready, 1)
            act.wait_ge(ab_ready, 1)
            act.wait_ge(cleared, 2)
            nc.scalar.activation(halves(gb[32:40, :]), c.P[32:40, 0:2, 0:HALF], ACT.Sigmoid).then_inc(act_step, 1)
            nc.scalar.activation(L.a_rate[:], L.a_log[:], ACT.Exp).then_inc(act_step, 1)
            act.wait_ge(dve_step, 3)
            nc.scalar.activation(t2, t2, ACT.Exp).then_inc(own_a, 1)
            act.wait_ge(own_a, 1)
            nc.scalar.activation(t2, t2, ACT.Ln, bias=1.0).then_inc(act_step, 1)

        @block.vector
        def _(dve):
            dve.wait_ge(hi_ready, 1)
            nc.vector.tensor_tensor(w_lo[:], w[:], w_hi[:].bitcast(F32), ALU.subtract).then_inc(lo_ready, 1)
            step = Chain(dve, dve_step)
            dve.wait_ge(act_step, 1)
            step.link(nc.vector.tensor_scalar(halves(t1), c.P[0:AH, 0:2, 0:HALF], L.dt_bias[:], None, ALU.add))
            step.link(nc.vector.tensor_scalar(t2, t1, -1.0, None, ALU.mult))
            step.link(nc.vector.tensor_tensor(t2, t2, t1, ALU.min))
            dve.wait_ge(act_step, 3)
            step.link(nc.vector.scalar_tensor_tensor(t3, t1, 0.0, t2, ALU.max, ALU.add))
            step.link(nc.vector.tensor_scalar(gb[0:AH, :], t3, L.a_rate[:], -1.0, ALU.mult, ALU.mult))
            for w_, row in ((0, 0), (1, 32)):
                step.link(nc.vector.tensor_tensor(
                    L.spread[:, w_ * 64:w_ * 64 + 64].rearrange("p (h b) -> p h b", b=TS),
                    gb[:, TP:NT].unsqueeze(1).broadcast_to([128, AH, TS]),
                    cols(c, CI + row, AH).unsqueeze(2).broadcast_to([128, AH, TS]), ALU.mult))
            dve.wait_ge(turned, 1)
            tok = c.P[:, 2].rearrange("p (n r) -> p n r", n=NCH)
            step.link(nc.vector.tensor_copy(L.g_tok[:], tok[:, :, 0:AH]))
            step.link(nc.vector.tensor_copy(L.b_tok[:], tok[:, :, 32:32 + AH]))
            dve.wait_ge(turned, 2)
            step.link(nc.vector.tensor_copy(L.gb_sample[:], c.P[:, 3, 0:128]))
            dve.wait_ge(turned, 3)
            step.link(nc.vector.tensor_copy(L.G_tok[:].rearrange("p n h -> p (n h)"), c.P[:, 4, 0:NCH * AH]))


def edge_phase(nc, c, io, L):
    sem = lambda s: c.sem(f"edge_{s}")
    turned, read, stored = sem("turned"), sem("read"), sem("stored")
    with nc.Block() as block:
        @block.sync
        def _(sp):
            sp.dma_start(io["new_conv_sample"][0][:, 0:2], io["state_conv"][0][:, 1:3]).then_inc(stored, 16)
            sp.wait_ge(read, 6)
            sp.dma_start(io["new_conv_prompt"][0, 0], L.edge_rows[0:3, :]).then_inc(stored, 16)
            sp.dma_start(io["new_conv_sample"][0, :, 2], L.edge_rows[3:11, :]).then_inc(stored, 16)
            sp.wait_ge(stored, 48)

        @block.tensor
        def _(pe):
            for part in range(6):
                for m in range(4):
                    ins = pe.transpose(c.P[0:11, part, m * 128:(m + 1) * 128], L.edge[:, part * 4 + m], cols(c, CI))
                ins.then_inc(turned, 1)

        @block.scalar
        def _(act):
            for part in range(6):
                act.wait_ge(turned, part + 1)
                nc.scalar.activation(L.edge_rows[:, part * 512:(part + 1) * 512], c.P[0:11, part], ACT.Copy).then_inc(read, 1)


def unit_phase(nc, c, L):
    sem = lambda s: c.sem(f"unit_{s}")
    squared, summed, rooted, own, scaled = (sem(s) for s in ("squared", "summed", "rooted", "own", "scaled"))
    with nc.Block() as block:
        @block.scalar
        def _(act):
            def square(i, g, wait):
                if wait:
                    act.wait_ge(summed, i * 4 + (g - 1))
                nc.scalar.activation(c.pair[:, g % 2], L.qkv[:, i * 4 + g], ACT.Square).then_inc(squared, 1)

            def root(i, g):
                act.wait_ge(summed, i * 4 + (g + 1))
                act.wait_ge(scaled, i * 4 + (g + 1))
                nc.scalar.activation(halves(L.norm[:, g % 2]), slot(c, g), ACT.Sqrt,
                                     bias=cols(c, CEPS, 1)).then_inc(rooted, 1)

            def body(i, first):
                for g in range(4):
                    square(i, g, not (first and g < 2))
                    if not (first and g == 0):
                        root(i if g else i - 1, g - 1 if g else 3)
            body(0, True)
            with act.Fori(1, 2 * AH // 4) as i:
                body(i, False)
            root(2 * AH // 4 - 1, 3)

        @block.tensor
        def _(pe):
            def body(i, first):
                for g in range(4):
                    pe.wait_ge(squared, i * 4 + (g + 1))
                    if not first:
                        pe.wait_ge(rooted, i * 4 + (g - 3))
                    for b in range(2):
                        ins = pe.matmul(slot(c, g)[:, b], cols(c, CONE), c.pair[:, g % 2, b * HALF:(b + 1) * HALF],
                                        start=True, stop=True)
                    ins.then_inc(summed, 1)
            body(0, True)
            with pe.Fori(1, 2 * AH // 4) as i:
                body(i, False)

        @block.vector
        def _(dve):
            dve.sem_inc(scaled, 2)
            for part, scale in ((0, DK ** -0.5), (1, 1.0)):
                with dve.Fori(part * 2, part * 2 + 2) as i:
                    for g in range(4):
                        dve.wait_ge(rooted, i * 4 + (g + 1))
                        nc.vector.reciprocal(L.norm[:, g % 2], L.norm[:, g % 2]).then_inc(own, 1)
                        dve.wait_ge(own, i * 4 + (g + 1))
                        x = L.qkv[:, i * 4 + g]
                        nc.vector.scalar_tensor_tensor(x, x, scale, L.norm[:, g % 2], ALU.mult, ALU.mult)\
                            .then_inc(scaled, 1)


class Steps:

    def __init__(self, c, name, steps):
        self.steps, self.at = steps, {}
        self.sems = {who: c.sem(f"{name}_{who}") for who in steps}
        self.passed = c.sem(f"{name}_passed")

    def begin(self, eng, who, n):
        self.at[who] = 0
        for other, sem in self.sems.items():
            if other != who:
                eng.wait_ge(sem, n * len(self.steps[other]) + 1)

    def done(self, ins, who, step):
        assert self.steps[who][self.at[who]] == step, (who, step)
        self.at[who] += 1
        return ins.then_inc(self.sems[who], 1)

    def after(self, eng, n, **steps):
        for who, step in steps.items():
            eng.wait_ge(self.sems[who], n * len(self.steps[who]) + (self.steps[who].index(step) + 2))

    def stand(self, eng):
        eng.sem_inc(self.passed, 1)


def delta_phase(nc, c, io, L):
    st = Steps(c, "delta", {
        "pe": ["decay", "k_tok", "v_tok", "kk", "qk", "L_T", "B2", "B2_T", "X_B2", "W_B2", "B4", "B4_T",
               "X_B4", "W_B4", "B8", "B8_T", "X_B8", "W_B8", "N", "N_T", "kS", "X_N", "N2", "N2_T", "X_N2", "N4",
               "X_N4", "v_new", "S_add", "out"],
        "act": ["e_last", "e_tok", "e_left", "e_row", "e_L", "e_attn", "L_T", "B2", "B2_T", "B4", "B4_T",
                "B8", "B8_T", "N", "N_T", "N2", "N2_T", "N4", "v_new", "out"],
        "dve": ["g", "G", "beta", "diff", "left", "k_dec", "b_dec", "b_v", "L_raw", "L", "B", "attn", "q_dec", "B_T", "X", "W",
                "X_B2", "W_B2", "X_B4", "W_B4", "X_B8", "W_B8", "R_raw", "R", "X_N", "X_N2", "X_N4", "S"],
        "pool": ["k", "v", "q", "mask_L", "mask_attn", "E_T", "S_dec"],
    })
    stored, cleared = c.sem("delta_stored"), c.sem("delta_cleared")
    B = L.delta
    kc, qc, vc, AT, LM, KD, BV, LT, P1, P1T, X, W, P2, P2T, S = B
    g_c, G_c, b_c, e_tok, e_left, e_last, b_dec = L.small

    def per_head(ap):
        return ap[:].unsqueeze(2).broadcast_to([128, AH, C])

    def both(s):
        return c.P[:, 2 * s:2 * s + 2].rearrange("p b (h x) -> p (b h) x", h=4)

    def for_heads(ap):
        return ap.unsqueeze(1).broadcast_to([128, AH, C])

    ident = cols(c, CI)

    def products(pe, s, lhs, rhs):
        for h in range(AH):
            ins = pe.matmul(both(s)[:, h], lhs[:, h], rhs[:, h], start=True, stop=True)
        return ins

    with nc.Block() as block:
        @block.sync
        def _(sp):
            st.after(sp, NCH - 1, dve="S")
            sp.dma_start(io["new_delta_prompt"][0, 0].rearrange("h k v -> k h v"), S[:]).then_inc(stored, 16)
            sp.wait_ge(stored, 16)

        @block.gpsimd
        def _(pool):
            nc.gpsimd.memset(S[:], 0.0).then_inc(cleared, 1)
            pool.sem_inc(st.sems["pool"], 1)
            high, low = pool.to_reg(-NEG), pool.to_reg(NEG)
            with pool.Fori(0, NCH) as n:
                st.begin(pool, "pool", n)
                for name, to, at in (("k", kc, AH), ("v", vc, 2 * AH), ("q", qc, 0)):
                    st.done(nc.gpsimd.tensor_copy(to[:], L.qkv[:, at:at + AH, ds(n * C, C)]), "pool", name)
                st.after(pool, n, dve="diff")
                st.stand(pool)
                st.done(nc.gpsimd.affine_select(out=LM[:], in_=AT[:], compare_op=ALU.is_gt, fill=high, base=0,
                                                pattern=[[0, AH], [-1, C]], channel_multiplier=1), "pool", "mask_L")
                st.after(pool, n, pool="mask_L")
                st.stand(pool)
                st.done(nc.gpsimd.affine_select(out=AT[:], in_=AT[:], compare_op=ALU.is_ge, fill=low, base=0,
                                                pattern=[[0, AH], [1, C]], channel_multiplier=-1), "pool", "mask_attn")
                st.after(pool, n, act="L_T", dve="B_T")
                st.done(nc.gpsimd.tensor_tensor(LT[:], LT[:], P1T[:], ALU.subtract), "pool", "E_T")
                st.after(pool, n, act="e_last", pe="N4")
                st.done(nc.gpsimd.tensor_tensor(P2[:], S[:], per_head(e_last), ALU.mult), "pool", "S_dec")

        @block.tensor
        def _(pe):
            pe.sem_inc(st.sems["pe"], 1)
            pe.wait_ge(cleared, 1)
            with pe.Fori(0, NCH) as n:
                st.begin(pe, "pe", n)
                st.after(pe, n, dve="g")
                for h in range(AH):
                    ins = pe.matmul(both(0)[:, h], g_c[:, h:h + 1].broadcast_to([128, 128]), cols(c, CU), start=True, stop=True)
                st.done(ins, "pe", "decay")
                for s, x, step in ((1, kc, "k"), (2, vc, "v")):
                    st.after(pe, n, pool=step)
                    for h in range(AH):
                        ins = pe.transpose(both(s)[:, h], x[:, h], ident)
                    st.done(ins, "pe", step + "_tok")
                st.done(products(pe, 3, kc, kc), "pe", "kk")
                st.after(pe, n, pool="q", act="e_row", dve="left")
                st.done(products(pe, 0, kc, qc), "pe", "qk")
                st.after(pe, n, dve="L")
                for h in range(AH):
                    ins = pe.transpose(both(1)[:, h], LM[:, h], ident)
                st.done(ins, "pe", "L_T")
                st.after(pe, n, dve="B_T")
                st.done(products(pe, 2, P1T, P1), "pe", "B2")
                st.done(products(pe, 3, P1, P1T), "pe", "B2_T")
                st.after(pe, n, dve="X", act="B2")
                st.done(products(pe, 0, P2, X), "pe", "X_B2")
                st.after(pe, n, dve="W", act="B2_T")
                st.done(products(pe, 1, P2T, W), "pe", "W_B2")
                st.done(products(pe, 2, P2T, P2), "pe", "B4")
                st.done(products(pe, 3, P2, P2T), "pe", "B4_T")
                st.after(pe, n, dve="X_B2", act="B4")
                st.done(products(pe, 0, P1, X), "pe", "X_B4")
                st.after(pe, n, dve="W_B2", act="B4_T")
                st.done(products(pe, 1, P1T, W), "pe", "W_B4")
                st.done(products(pe, 2, P1T, P1), "pe", "B8")
                st.done(products(pe, 3, P1, P1T), "pe", "B8_T")
                st.after(pe, n, dve="X_B4", act="B8")
                st.done(products(pe, 0, P2, X), "pe", "X_B8")
                st.after(pe, n, dve="W_B4", act="B8_T")
                st.done(products(pe, 1, P2T, W), "pe", "W_B8")
                st.after(pe, n, dve="W_B8", pool="E_T")
                st.done(products(pe, 2, LT, W), "pe", "N")
                st.done(products(pe, 3, W, LT), "pe", "N_T")
                st.done(products(pe, 1, kc, S), "pe", "kS")
                st.after(pe, n, dve="X_B8", act="N")
                st.done(products(pe, 0, P1, X), "pe", "X_N")
                st.after(pe, n, act="N_T")
                st.done(products(pe, 2, P1T, P1), "pe", "N2")
                st.done(products(pe, 3, P1, P1T), "pe", "N2_T")
                st.after(pe, n, dve="X_N", act="N2")
                st.done(products(pe, 0, P2, X), "pe", "X_N2")
                st.after(pe, n, act="N2_T")
                st.done(products(pe, 2, P2T, P2), "pe", "N4")
                st.after(pe, n, dve="X_N2", act="N4")
                st.done(products(pe, 0, P1, X), "pe", "X_N4")
                st.after(pe, n, dve="X_N4")
                st.done(products(pe, 1, X, vc), "pe", "v_new")
                st.after(pe, n, act="v_new")
                st.done(products(pe, 2, KD, P2T), "pe", "S_add")
                for h in range(AH):
                    pe.matmul(both(3)[:, h], S[:, h], qc[:, h], start=True, stop=False)
                    ins = pe.matmul(both(3)[:, h], P2T[:, h], AT[:, h], start=False, stop=True)
                st.done(ins, "pe", "out")

        @block.scalar
        def _(act):
            act.sem_inc(st.sems["act"], 1)
            with act.Fori(0, NCH) as n:
                st.begin(act, "act", n)
                last = both(0)[:, :, C - 1]

                def exp(to, of, step, scale=1.0):
                    st.done(nc.scalar.activation(to, of, ACT.Exp, scale=scale), "act", step)

                def copy(to, s, step):
                    st.after(act, n, pe=step)
                    st.done(nc.scalar.activation(to[:], both(s), ACT.Copy), "act", step)

                st.after(act, n, dve="left")
                exp(e_last[:], last, "e_last")
                exp(e_tok[:], G_c[:], "e_tok")
                exp(e_left[:], e_left[:], "e_left")
                st.after(act, n, pe="v_tok")
                exp(vc[:], both(0), "e_row")
                st.after(act, n, pool="mask_L")
                exp(LM[:], LM[:], "e_L", scale=-1.0)
                st.after(act, n, pool="mask_attn")
                exp(AT[:], AT[:], "e_attn")
                st.after(act, n, dve="B_T")
                copy(LT, 1, "L_T")
                copy(P2, 2, "B2")
                copy(P2T, 3, "B2_T")
                st.after(act, n, pool="E_T", dve="W")
                copy(P1, 2, "B4")
                copy(P1T, 3, "B4_T")
                copy(P2, 2, "B8")
                copy(P2T, 3, "B8_T")
                copy(P1, 2, "N")
                copy(P1T, 3, "N_T")
                copy(P2, 2, "N2")
                copy(P2T, 3, "N2_T")
                copy(P1, 2, "N4")
                copy(P2T, 1, "v_new")
                st.after(act, n, pe="out")
                st.done(nc.scalar.activation(L.qkv[:, 2 * AH:3 * AH, ds(n * C, C)], both(3), ACT.Copy), "act", "out")

        @block.vector
        def _(dve):
            dve.sem_inc(st.sems["dve"], 1)
            with dve.Fori(0, NCH) as n:
                st.begin(dve, "dve", n)

                def tt(step, to, a, b, op):
                    st.done(nc.vector.tensor_tensor(to, a, b, op), "dve", step)

                for name, to, of in (("g", g_c, L.g_tok), ("G", G_c, L.G_tok), ("beta", b_c, L.b_tok)):
                    st.done(nc.vector.tensor_copy(to[:], of[:, n]), "dve", name)
                st.after(dve, n, pe="decay", dve="G")
                tt("diff", AT[:], both(0), per_head(G_c), ALU.subtract)
                tt("left", e_left[:], both(0)[:, :, C - 1], G_c[:], ALU.subtract)
                st.after(dve, n, pe="k_tok", act="e_left")
                tt("k_dec", KD[:], both(1), per_head(e_left), ALU.mult)
                st.done(nc.vector.scalar_tensor_tensor(b_dec[:], e_tok[:], -1.0, b_c[:], ALU.mult, ALU.mult), "dve", "b_dec")
                st.after(dve, n, pe="v_tok", dve="beta")
                tt("b_v", BV[:], both(2), per_head(b_c), ALU.mult)
                st.after(dve, n, pe="kk", act="e_L")
                tt("L_raw", LM[:], both(3), LM[:], ALU.mult)
                st.after(dve, n, dve="L_raw")
                tt("L", LM[:], LM[:], per_head(b_c), ALU.mult)
                st.after(dve, n, dve="L")
                tt("B", P1[:], LM[:], for_heads(cols(c, CM16)), ALU.mult)
                st.after(dve, n, pe="qk", act="e_attn")
                tt("attn", AT[:], both(0), AT[:], ALU.mult)
                tt("q_dec", qc[:], qc[:], vc[:], ALU.mult)
                st.after(dve, n, pe="L_T")
                tt("B_T", P1T[:], both(1), for_heads(cols(c, CM16)), ALU.mult)
                st.after(dve, n, dve="B_T")
                tt("X", X[:], for_heads(ident), P1T[:], ALU.subtract)
                tt("W", W[:], for_heads(ident), P1[:], ALU.subtract)
                for step in ("B2", "B4", "B8"):
                    st.after(dve, n, pe="X_" + step)
                    tt("X_" + step, X[:], X[:], both(0), ALU.add)
                    st.after(dve, n, pe="W_" + step)
                    tt("W_" + step, W[:], W[:], both(1), ALU.add)
                st.after(dve, n, pe="kS", dve="b_dec")
                tt("R_raw", vc[:], both(1), per_head(b_dec), ALU.mult)
                st.after(dve, n, dve="R_raw")
                tt("R", vc[:], vc[:], BV[:], ALU.add)
                for step, op in (("N", ALU.subtract), ("N2", ALU.add), ("N4", ALU.add)):
                    st.after(dve, n, pe="X_" + step)
                    tt("X_" + step, X[:], X[:], both(0), op)
                st.after(dve, n, pe="out", pool="S_dec")
                tt("S", S[:], P2[:], both(2), ALU.add)


def sample_delta_phase(nc, c, io, L):
    sem = lambda s: c.sem(f"step_{s}")
    arrived, stored, pe_step, own, act_step, masked, outer, updated = (sem(s) for s in
        ("arrived", "stored", "pe_step", "own", "act_step", "masked", "outer", "updated"))
    NP = AH * TS
    S, kq, row = L.s_state, L.s_kq, L.s_row
    sm = lambda i: L.s_small[:, i]
    tok = lambda part: L.qkv[:, part * AH:(part + 1) * AH, TP:NT]
    hb = lambda ap: ap.rearrange("p (h b) -> p h b", b=TS)
    E_G, V_MEM, DELTA, DOT, OUT, PROD = range(6)
    with nc.Block() as block:
        @block.sync
        def _(sp):
            for h in range(AH):
                sp.dma_start(S[:, h * TS:(h + 1) * TS], io["state_delta"][0, :, h].rearrange("b k v -> k b v")).then_inc(arrived, 16)
            sp.wait_ge(updated, NP + 8)
            for h in range(AH):
                sp.dma_start(io["new_delta_sample"][0, :, h].rearrange("b k v -> k b v"), S[:, h * TS:(h + 1) * TS])\
                    .then_inc(stored, 16)
            sp.wait_ge(stored, 16 * AH)

        @block.scalar
        def _(act):
            nc.scalar.activation(sm(E_G), L.gb_sample[:, 0:NP], ACT.Exp).then_inc(act_step, 1)

        @block.tensor
        def _(pe):
            pe.wait_ge(own, 3)
            pe.matmul(c.P[:, 1, 0:NP], cols(c, CONE), sm(PROD), start=True, stop=True).then_inc(pe_step, 1)
            pe.transpose(c.P[0:NP, 2, 0:128], L.s_k[:], cols(c, CI)).then_inc(pe_step, 1)
            pe.wait_ge(arrived, 16 * AH)
            for p in range(NP):
                ins = pe.matmul(c.P[:, 0, 2 * p:2 * p + 2], S[:, p], kq[:, p], start=True, stop=True)
            ins.then_inc(pe_step, 1)
            pe.wait_ge(own, 7)
            pe.transpose(c.P[0:NP, 3, 0:128], sm(DELTA), cols(c, CI)).then_inc(pe_step, 1)
            with pe.Fori(0, NP // 8) as i:
                for j in range(2):
                    pe.wait_ge(masked, i * 2 + (j + 1))
                    pe.wait_ge(updated, i * 8 + (4 * j + 1))
                    pe.matmul(c.P[:, 4 + j], row[0:NP, 0, :], L.s_mask[0:NP, j], start=True, stop=True).then_inc(outer, 1)

        @block.vector
        def _(dve):
            chain = Chain(dve, own)
            chain.link(nc.vector.tensor_copy(kq[:, :, 0].rearrange("p (h b) -> p h b", b=TS), tok(1)))
            chain.link(nc.vector.tensor_copy(kq[:, :, 1].rearrange("p (h b) -> p h b", b=TS), tok(0)))
            nc.vector.tensor_copy(hb(L.s_k[:]), tok(1))
            chain.link(nc.vector.tensor_tensor(hb(sm(PROD)), tok(1), tok(0), ALU.mult))
            dve.wait_ge(pe_step, 3)
            dve.wait_ge(act_step, 1)
            chain.link(nc.vector.tensor_copy(sm(DOT), c.P[:, 1, 0:NP]))
            kqS = c.P[:, 0, 0:2 * NP].rearrange("p (n t) -> p n t", t=2)
            chain.link(nc.vector.tensor_tensor(sm(V_MEM), kqS[:, :, 0], sm(E_G), ALU.mult))
            chain.link(nc.vector.tensor_tensor(hb(sm(DELTA)), tok(2), hb(sm(V_MEM)), ALU.subtract))
            chain.link(nc.vector.tensor_tensor(sm(DELTA), sm(DELTA), L.gb_sample[:, NP:2 * NP], ALU.mult))
            chain.link(nc.vector.tensor_tensor(sm(OUT), kqS[:, :, 1], sm(E_G), ALU.mult))
            chain.link(nc.vector.tensor_tensor(sm(V_MEM), sm(DOT), sm(DELTA), ALU.mult))
            chain.link(nc.vector.tensor_tensor(tok(2), hb(sm(OUT)), hb(sm(V_MEM)), ALU.add))
            chain.link(nc.vector.tensor_copy(row[0:NP, 0, :], c.P[0:NP, 2, 0:128]))
            dve.wait_ge(pe_step, 4)
            chain.link(nc.vector.tensor_copy(row[0:NP, 1, :], c.P[0:NP, 3, 0:128]))
            dve.sem_inc(updated, 8)
            with dve.Fori(0, NP // 8) as i:
                for j in range(2):
                    nc.vector.tensor_tensor(L.s_mask[0:NP, j].rearrange("p (n v) -> p n v", n=4),
                                            row[0:NP, 1, :].unsqueeze(1).broadcast_to([NP, 4, 128]),
                                            c.cst[0:NP, ds(i * 8 + (CI + 4 * j), 4)].unsqueeze(2).broadcast_to([NP, 4, 128]),
                                            ALU.mult).then_inc(masked, 1)
                for j in range(2):
                    dve.wait_ge(outer, i * 2 + (j + 1))
                    for q in range(4):
                        p = i * 8 + (4 * j + q)
                        nc.vector.scalar_tensor_tensor(S[:, p], S[:, p], L.s_small[:, E_G, ds(p, 1)],
                                                       c.P[:, 4 + j, q * 128:(q + 1) * 128], ALU.mult, ALU.add).then_inc(updated, 1)


def mixer_out_phase(nc, c, L):
    sem = lambda s: c.sem(f"onorm_{s}")
    squared, summed, rooted, own, gated, hi_ready, freed = (sem(s) for s in
        ("squared", "summed", "rooted", "own", "gated", "hi_ready", "freed"))
    o = lambda h: L.qkv[:, 2 * AH + h]
    with nc.Block() as block:
        @block.scalar
        def _(act):
            def square(h):
                if h >= 2:
                    act.wait_ge(summed, h - 1)
                nc.scalar.activation(c.pair[:, h % 2], o(h), ACT.Square).then_inc(squared, 1)

            square(0)
            for h in range(AH):
                if h + 1 < AH:
                    square(h + 1)
                act.wait_ge(summed, h + 1)
                if h >= 2:
                    act.wait_ge(freed, h - 1)
                nc.scalar.activation(halves(L.norm[:, h % 2]), slot(c, h % 4), ACT.Sqrt, scale=1.0 / DK,
                                     bias=cols(c, CEPS, 1)).then_inc(rooted, 1)
            for h in range(AH):
                act.wait_ge(gated, h + 1)
                nc.scalar.activation(c.x_hi[:, h], o(h), ACT.Copy).then_inc(hi_ready, 1)

        @block.tensor
        def _(pe):
            for h in range(AH):
                pe.wait_ge(squared, h + 1)
                if h >= 4:
                    pe.wait_ge(rooted, h - 3)
                for b in range(2):
                    ins = pe.matmul(slot(c, h % 4)[:, b], cols(c, CONE), c.pair[:, h % 2, b * HALF:(b + 1) * HALF],
                                    start=True, stop=True)
                ins.then_inc(summed, 1)

        @block.vector
        def _(dve):
            chain = Chain(dve, own)
            for h in range(AH):
                r = L.norm[:, h % 2]
                dve.wait_ge(rooted, h + 1)
                chain.link(nc.vector.reciprocal(r, r))
                nc.vector.scalar_tensor_tensor(o(h), o(h), c.vec[:, VO:VO + 1], r, ALU.mult, ALU.mult).then_inc(freed, 1)
                dve.wait_ge(freed, h + 1)
                nc.vector.tensor_tensor(o(h), o(h), L.z[:, h], ALU.mult).then_inc(gated, 1)
            for h in range(AH):
                dve.wait_ge(hi_ready, h + 1)
                nc.vector.tensor_tensor(c.x_lo[:, h], o(h), c.x_hi[:, h].bitcast(F32), ALU.subtract).then_inc(own, 1)


def add_to_residual_phase(nc, c, name, st, sp_next):
    ready, evacuated = c.sem(f"{name}_ready"), c.sem(f"{name}_evacuated")
    with nc.Block() as block:
        @block.sync
        def _(sp):
            st.rest(c, sp)
            sp_next(sp)

        @block.tensor
        def _(pe):
            square_tensor(nc, c, pe, st, ready, evacuated)

        @block.scalar
        def _(act):
            st.split_hi(nc, c, act, 0, 0)

            def body(i, last):
                for j in range(2):
                    if not (last and j == 1):
                        st.split_hi(nc, c, act, i, j + 1)
                    act.wait_ge(ready, i * 4 + (2 * j + 2))
            over(act, st.n // 2, body)

        @block.vector
        def _(dve):
            dve.sem_inc(evacuated, 4)
            st.split_lo(nc, c, dve, 0, 0)

            def body(i, last):
                for j in range(2):
                    if not (last and j == 1):
                        st.split_lo(nc, c, dve, i, j + 1)
                    for m in range(2):
                        g = 2 * j + m
                        dve.wait_ge(ready, i * 4 + (g + 1))
                        hm = halves(c.h[:, i * 4 + g])
                        nc.vector.tensor_tensor(hm, hm, slot(c, g), ALU.add).then_inc(evacuated, 1)
            over(dve, st.n // 2, body)


def gate_up_tensor(nc, c, pe, number, at, ready, gate_read, up_read, j):
    pe.wait_ge(c.lo_done, number + 1)
    for m, read in ((0, gate_read), (1, up_read)):
        pe.wait_ge(read, at + 1)
        for k in range(KT):
            w = k * 256 + m * 128
            ins = three_products(nc, slot(c, 2 * j + m), c.w_hi[:, j, w:w + 128], c.w_lo[:, j, w:w + 128],
                                 c.x_hi[:, k], c.x_lo[:, k], k == 0, k == KT - 1)
        ins.then_inc(ready, 1)


def dense_phase(nc, c, st_gu, st_down, sp_next, L):
    sem = lambda s: c.sem(f"dense_{s}")
    ready, gate_read, up_read, f_hi_ready, f_ready, down_ready, added = (sem(s) for s in
        ("ready", "gate_read", "up_read", "f_hi_ready", "f_ready", "down_ready", "added"))
    with nc.Block() as block:
        @block.sync
        def _(sp):
            st_gu.rest(c, sp)
            st_down.start(c, sp)
            st_down.rest(c, sp)
            sp_next(sp)

        @block.tensor
        def _(pe):
            def gu(i, last):
                for j in range(2):
                    gate_up_tensor(nc, c, pe, st_gu.number(i, j), i * 2 + j, ready, gate_read, up_read, j)
            over(pe, NFF // 2, gu)
            pe.wait_ge(f_ready, NFF)

            def down(i, last):
                for t in range(2):
                    pe.wait_ge(added, i * 2 + (t + 1))
                    for part in range(2):
                        pe.wait_ge(c.lo_done, i * 4 + (st_down.base + 2 * t + part + 1))
                        for k in range(NFF // 2):
                            f = part * (NFF // 2) + k
                            ins = three_products(nc, slot(c, t), c.w_hi[:, part, k * 128:(k + 1) * 128],
                                                 c.w_lo[:, part, k * 128:(k + 1) * 128], L.f_hi[:, f], L.f_lo[:, f],
                                                 f == 0, f == NFF - 1)
                        ins.then_inc(down_ready, 1)
            over(pe, KT // 2, down)

        @block.scalar
        def _(act):
            act.sem_inc(gate_read, 2)
            st_gu.split_hi(nc, c, act, 0, 0)

            def gu(i, last):
                for j in range(2):
                    if last and j == 1:
                        st_down.split_hi(nc, c, act, 0, 0)
                    else:
                        st_gu.split_hi(nc, c, act, i, j + 1)
                    act.wait_ge(ready, i * 4 + (2 * j + 1))
                    nc.scalar.activation(halves(L.sg[:, j]), slot(c, 2 * j), ACT.Silu).then_inc(gate_read, 1)
                    act.wait_ge(up_read, i * 2 + (j + 3))
                    nc.scalar.activation(L.f_hi[:, i * 2 + j], L.sf[:, j], ACT.Copy).then_inc(f_hi_ready, 1)
            over(act, NFF // 2, gu)
            act.wait_ge(ready, 2 * NFF)

            def down(i, last):
                for q in range(4):
                    if not (last and q == 3):
                        st_down.split_hi(nc, c, act, i * 2, q + 1)
                    act.wait_ge(down_ready, i * 4 + (q + 1))
            over(act, KT // 2, down)

        @block.vector
        def _(dve):
            dve.sem_inc(up_read, 2)
            dve.sem_inc(added, 2)
            st_gu.split_lo(nc, c, dve, 0, 0)

            def gu(i, last):
                for j in range(2):
                    if last and j == 1:
                        st_down.split_lo(nc, c, dve, 0, 0)
                    else:
                        st_gu.split_lo(nc, c, dve, i, j + 1)
                    dve.wait_ge(ready, i * 4 + (2 * j + 2))
                    dve.wait_ge(gate_read, i * 2 + (j + 3))
                    nc.vector.tensor_tensor(halves(L.sf[:, j]), halves(L.sg[:, j]), slot(c, 2 * j + 1), ALU.mult)\
                        .then_inc(up_read, 1)
                    dve.wait_ge(f_hi_ready, i * 2 + (j + 1))
                    nc.vector.tensor_tensor(L.f_lo[:, i * 2 + j], L.sf[:, j], L.f_hi[:, i * 2 + j].bitcast(F32),
                                            ALU.subtract).then_inc(f_ready, 1)
            over(dve, NFF // 2, gu)

            def down(i, last):
                for t in range(2):
                    for part in range(2):
                        if not (last and t == 1 and part == 1):
                            st_down.split_lo(nc, c, dve, i * 2, 2 * t + part + 1)
                    dve.wait_ge(down_ready, i * 4 + (2 * t + 2))
                    hm = halves(c.h[:, i * 2 + t])
                    nc.vector.tensor_tensor(hm, hm, slot(c, t), ALU.add).then_inc(added, 1)
            over(dve, KT // 2, down)


class ExpertStream:

    def __init__(self, base, w_gu, w_down):
        self.base, self.gu, self.down = base, w_gu, w_down
        self.per = FE // 128 + 4

    def src(self, e, i, j):
        return gate_and_up(self.gu[e], 128)(i * 256 + j * 128)

    def src_down(self, e, i, j):
        return self.down[e].rearrange("(k p) n -> p k n", p=128)[:, :, ds(i * 512 + j * 256, 256)]

    def start(self, c, sp, wait=True):
        for j in range(2):
            load_chunk(c, sp, self.base + j, j, self.src(0, 0, j), wait)

    def rest(self, c, sp):
        def expert(e, first):
            with sp.Fori(1 if first else 0, FE // 256) as i:
                for j in range(2):
                    load_chunk(c, sp, e * self.per + (i * 2 + (self.base + j)), j, self.src(e, i, j))
            with sp.Fori(0, 2) as i:
                for j in range(2):
                    load_chunk(c, sp, e * self.per + (i * 2 + (self.base + FE // 128 + j)), j, self.src_down(e, i, j))
        expert(0, True)
        with sp.Fori(1, NE) as e:
            expert(e, False)

    def split_hi(self, nc, c, act, e, i, j):
        act.wait_ge(c.raw_loaded[j % 2], e * (16 * self.per) + (i * 32 + 32 * ((self.base + j) // 2 + 1)))
        nc.scalar.activation(c.w_hi[:, j % 2], c.w_raw[:, j % 2], ACT.Copy).then_inc(c.hi_done, 1)

    def split_lo(self, nc, c, dve, e, i, j):
        dve.wait_ge(c.hi_done, e * self.per + (i * 2 + (self.base + j + 1)))
        nc.vector.tensor_tensor(c.w_lo[:, j % 2], c.w_raw[:, j % 2], c.w_hi[:, j % 2].bitcast(F32),
                                ALU.subtract).then_inc(c.lo_done, 1)


def moe_phase(nc, c, st, sp_next, L):
    sem = lambda s: c.sem(f"moe_{s}")
    ready, gate_read, up_read, gated, f_hi_ready, f_ready, down_ready, added, passed = (sem(s) for s in
        ("ready", "gate_read", "up_read", "gated", "f_hi_ready", "f_ready", "down_ready", "added", "passed"))
    NF, ND = FE // 128, 4
    NCK = NF + ND
    with nc.Block() as block:
        @block.sync
        def _(sp):
            st.rest(c, sp)

        @block.tensor
        def _(pe):
            def expert(e, last_expert):
                def gu(i, last):
                    for j in range(2):
                        gate_up_tensor(nc, c, pe, e * NCK + (i * 2 + (st.base + j)), e * NF + (i * 2 + j),
                                       ready, gate_read, up_read, j)
                with pe.Fori(0, NF // 2) as i:
                    gu(i, False)
                pe.wait_ge(f_ready, e * NF + NF)
                pe.sem_inc(passed, 1)

                def down(i, last):
                    for j in range(2):
                        pe.wait_ge(c.lo_done, e * NCK + (i * 2 + (st.base + NF + j + 1)))
                        for m in range(2):
                            g = 2 * j + m
                            pe.wait_ge(added, e * KT + (i * 4 + (g + 1)))
                            for k in range(NF):
                                w = k * 256 + m * 128
                                ins = three_products(nc, slot(c, g), c.w_hi[:, j, w:w + 128], c.w_lo[:, j, w:w + 128],
                                                     L.f_hi[:, k], L.f_lo[:, k], k == 0, k == NF - 1)
                            ins.then_inc(down_ready, 1)
                with pe.Fori(0, ND // 2) as i:
                    down(i, False)
                pe.wait_ge(added, e * KT + (KT + 4))
                pe.sem_inc(passed, 1)
            with pe.Fori(0, NE) as e:
                expert(e, False)

        @block.scalar
        def _(act):
            act.sem_inc(gate_read, 2)
            split = lambda e, i, j: st.split_hi(nc, c, act, e, i, j)
            split(0, 0, 0)

            def expert(e, last_expert):
                def gu(i, last):
                    for j in range(2):
                        split(e, i, j + 1)
                        act.wait_ge(ready, e * (2 * NF) + (i * 4 + (2 * j + 1)))
                        nc.scalar.activation(halves(L.sg[:, j]), slot(c, 2 * j), ACT.Silu).then_inc(gate_read, 1)
                        act.wait_ge(gated, e * NF + (i * 2 + (j + 1)))
                        nc.scalar.activation(L.f_hi[:, i * 2 + j], L.sf[:, j], ACT.Copy).then_inc(f_hi_ready, 1)
                with act.Fori(0, NF // 2) as i:
                    gu(i, False)

                def down(i, last):
                    for j in range(2):
                        if not (last and last_expert and j == 1):
                            split(e, i + NF // 2, j + 1)
                        act.wait_ge(down_ready, e * KT + (i * 4 + (2 * j + 2)))
                over(act, ND // 2, down)
            with act.Fori(0, NE - 1) as e:
                expert(e, False)
            expert(NE - 1, True)

        @block.vector
        def _(dve):
            dve.sem_inc(up_read, 2)
            dve.sem_inc(added, 4)
            split = lambda e, i, j: st.split_lo(nc, c, dve, e, i, j)
            split(0, 0, 0)

            def expert(e, last_expert):
                def gu(i, last):
                    for j in range(2):
                        split(e, i, j + 1)
                        at = e * NF + (i * 2 + j)
                        dve.wait_ge(ready, e * (2 * NF) + (i * 4 + (2 * j + 2)))
                        dve.wait_ge(gate_read, at + 3)
                        nc.vector.tensor_tensor(halves(L.sf[:, j]), halves(L.sg[:, j]), slot(c, 2 * j + 1), ALU.mult)\
                            .then_inc(up_read, 1)
                        dve.wait_ge(up_read, at + 3)
                        nc.vector.tensor_tensor(L.sf[:, j], L.sf[:, j], L.combine[:, e], ALU.mult).then_inc(gated, 1)
                        dve.wait_ge(f_hi_ready, at + 1)
                        nc.vector.tensor_tensor(L.f_lo[:, i * 2 + j], L.sf[:, j], L.f_hi[:, i * 2 + j].bitcast(F32),
                                                ALU.subtract).then_inc(f_ready, 1)
                with dve.Fori(0, NF // 2) as i:
                    gu(i, False)

                def down(i, last):
                    for j in range(2):
                        if not (last and last_expert and j == 1):
                            split(e, i + NF // 2, j + 1)
                        for m in range(2):
                            g = 2 * j + m
                            dve.wait_ge(down_ready, e * KT + (i * 4 + (g + 1)))
                            hm = halves(c.h[:, i * 4 + g])
                            nc.vector.tensor_tensor(hm, hm, slot(c, g), ALU.add).then_inc(added, 1)
                over(dve, ND // 2, down)
            with dve.Fori(0, NE - 1) as e:
                expert(e, False)
            expert(NE - 1, True)


def project_phase(nc, c, name, st, sp_next, out):
    ready, evacuated = c.sem(f"{name}_ready"), c.sem(f"{name}_evacuated")
    with nc.Block() as block:
        @block.sync
        def _(sp):
            if st.n > 2:
                st.rest(c, sp)
            sp_next(sp)

        @block.tensor
        def _(pe):
            square_tensor(nc, c, pe, st, ready, evacuated)

        @block.scalar
        def _(act):
            act.sem_inc(evacuated, 4)
            st.split_hi(nc, c, act, 0, 0)

            def body(i, last):
                for j in range(2):
                    if not (last and j == 1):
                        st.split_hi(nc, c, act, i, j + 1)
                    for m in range(2):
                        g = 2 * j + m
                        act.wait_ge(ready, i * 4 + (g + 1))
                        nc.scalar.activation(halves(out[:, i * 4 + g]), slot(c, g), ACT.Copy).then_inc(evacuated, 1)
            over(act, st.n // 2, body)

        @block.vector
        def _(dve):
            st.split_lo(nc, c, dve, 0, 0)

            def body(i, last):
                for j in range(2):
                    if not (last and j == 1):
                        st.split_lo(nc, c, dve, i, j + 1)
            over(dve, st.n // 2, body)


def head_norm_phase(nc, c, tiles):
    sem = lambda s: c.sem(f"head_{s}")
    squared, summed, rooted, own, scaled = (sem(s) for s in ("squared", "summed", "rooted", "own", "scaled"))
    n = len(tiles)
    with nc.Block() as block:
        @block.scalar
        def _(act):
            def square(t):
                if t >= 2:
                    act.wait_ge(summed, t - 1)
                nc.scalar.activation(c.pair[:, t % 2], tiles[t][0], ACT.Square).then_inc(squared, 1)

            square(0)
            for t in range(n):
                if t + 1 < n:
                    square(t + 1)
                act.wait_ge(summed, t + 1)
                if t >= 2:
                    act.wait_ge(scaled, t - 1)
                nc.scalar.activation(halves(c.scratch[:, t % 2]), slot(c, t % 4), ACT.Sqrt, scale=1.0 / HD,
                                     bias=cols(c, CEPS, 1)).then_inc(rooted, 1)

        @block.tensor
        def _(pe):
            for t in range(n):
                pe.wait_ge(squared, t + 1)
                if t >= 4:
                    pe.wait_ge(rooted, t - 3)
                for b in range(2):
                    ins = pe.matmul(slot(c, t % 4)[:, b], cols(c, CBO), c.pair[:, t % 2, b * HALF:(b + 1) * HALF],
                                    start=True, stop=True)
                ins.then_inc(summed, 1)

        @block.vector
        def _(dve):
            for t, (x, gain) in enumerate(tiles):
                r = c.scratch[:, t % 2]
                dve.wait_ge(rooted, t + 1)
                nc.vector.reciprocal(r, r).then_inc(own, 1)
                dve.wait_ge(own, t + 1)
                nc.vector.scalar_tensor_tensor(x, x, c.vec[:, gain:gain + 1], r, ALU.mult, ALU.mult).then_inc(scaled, 1)


def rotary_phase(nc, c, L):
    sem = lambda s: c.sem(f"rotary_{s}")
    turned, own, done = sem("turned"), sem("own"), sem("done")
    cos, sin = cols(c, CCOS, NT), cols(c, CSIN, NT)
    n_q = BH // 2
    with nc.Block() as block:
        @block.tensor
        def _(pe):
            def product(s, w, x):
                for b in range(2):
                    ins = pe.matmul(slot(c, s)[:, b], w, x[:, b * HALF:(b + 1) * HALF], start=True, stop=True)
                return ins

            for t in range(n_q):
                if t >= 2:
                    pe.wait_ge(done, t - 1)
                product(t % 2, cols(c, CROT), L.q[:, t]).then_inc(turned, 1)
            for kv in range(BKV):
                pe.wait_ge(done, n_q + kv)
                x = L.kv[:, kv // 2]
                product(0, cols(c, CRD0 if kv % 2 == 0 else CRD1), x).then_inc(turned, 1)
                product(1, cols(c, CD0 if kv % 2 == 0 else CD1), x).then_inc(turned, 1)

        @block.vector
        def _(dve):
            chain = Chain(dve, own)
            for t in range(n_q):
                x, r = L.q[:, t], c.scratch[:, t % 2]
                dve.wait_ge(turned, t + 1)
                nc.vector.tensor_tensor(halves(r), slot(c, t % 2), halves(sin), ALU.mult)
                chain.link(nc.vector.tensor_tensor(x, x, cos, ALU.mult))
                nc.vector.tensor_tensor(x, x, r, ALU.add).then_inc(done, 1)
            for kv in range(BKV):
                x, r = L.k2[:, kv], c.scratch[:, kv % 2]
                dve.wait_ge(turned, n_q + 2 * kv + 2)
                nc.vector.tensor_tensor(halves(r), slot(c, 0), halves(sin), ALU.mult)
                chain.link(nc.vector.tensor_tensor(halves(x), slot(c, 1), halves(cos), ALU.mult))
                nc.vector.tensor_tensor(x, x, r, ALU.add).then_inc(done, 1)


def window_phase(nc, c, io, L):
    sem = lambda s: c.sem(f"window_{s}")
    turned, read, stored = sem("turned"), sem("read"), sem("stored")
    row = lambda ap: ap.rearrange("t h d -> t (h d)")
    with nc.Block() as block:
        @block.sync
        def _(sp):
            for name, cache, to in (("k", io["cache_k_win"], L.k_cache), ("v", io["cache_v_win"], L.v_cache)):
                sp.dma_start(to[:], cache.rearrange("b t h d -> t b (h d)")).then_inc(L.cache_loaded, 16)
                sp.dma_start(io[f"new_{name}_win_sample"][:, 0:WIN - 1], cache[:, 1:WIN]).then_inc(stored, 16)
            sp.dma_start(L.sinks[:], io["b_sinks"].broadcast_to([128, BH])).then_inc(L.cache_loaded, 16)
            sp.wait_ge(read, 8)
            sp.dma_start(row(io["new_v_win_prompt"][0]), L.v_tok[:, NCH - 1]).then_inc(stored, 16)
            sp.dma_start(row(io["new_k_win_prompt"][0]), L.k_rows[:, 0]).then_inc(stored, 16)
            for name, rows in (("k", L.k_rows[0:TS, 1]), ("v", L.v_new[0:TS])):
                sp.dma_start(io[f"new_{name}_win_sample"][:, WIN - 1].rearrange("b h d -> b (h d)"), rows).then_inc(stored, 16)
            sp.wait_ge(stored, 96)
            sp.wait_ge(L.cache_loaded, 48)

        @block.tensor
        def _(pe):
            ident = cols(c, CI)
            for n in range(NCH):
                for j in range(2):
                    ins = pe.transpose(c.P[:, n, j * 128:(j + 1) * 128], L.kv[:, 2 + j, n * 128:(n + 1) * 128], ident)
                ins.then_inc(turned, 1)
            for j in range(2):
                ins = pe.transpose(c.P[0:TS, 4, j * 128:(j + 1) * 128], L.kv[:, 2 + j, TP:NT], ident)
            ins.then_inc(turned, 1)
            for kv in range(BKV):
                ins = pe.transpose(c.P[:, 5, kv * 128:(kv + 1) * 128], L.k2[:, kv, TP - WIN:TP], ident)
            ins.then_inc(turned, 1)
            for kv in range(BKV):
                ins = pe.transpose(c.P[0:TS, 6, kv * 128:(kv + 1) * 128], L.k2[:, kv, TP:NT], ident)
            ins.then_inc(turned, 1)

        @block.vector
        def _(dve):
            def take(n, to, of):
                dve.wait_ge(turned, n)
                nc.vector.tensor_copy(to, of).then_inc(read, 1)
            for n in range(NCH):
                take(n + 1, L.v_tok[:, n], c.P[:, n, 0:256])
            take(NCH + 1, L.v_new[0:TS], c.P[0:TS, 4, 0:256])
            once = lambda ap: ap.rearrange("p (h u d) -> p h u d", h=BKV, u=2)[:, :, 0]
            heads = lambda ap: ap.rearrange("p (h d) -> p h d", h=BKV)
            take(NCH + 2, heads(L.k_rows[:, 0]), once(c.P[:, 5]))
            take(NCH + 3, heads(L.k_rows[0:TS, 1]), once(c.P[0:TS, 6]))
            nc.vector.memset(L.p_stat[:], 0.0).then_inc(read, 1)
            dve.wait_ge(L.cache_loaded, 48)
            nc.vector.tensor_tensor(L.sink_pick[:], L.sinks[:], cols(c, CHEAD, BH), ALU.mult).then_inc(read, 1)
            dve.wait_ge(read, 9)
            nc.vector.tensor_reduce(L.sink_rows[:], L.sink_pick[:], AX, ALU.add)


def attend_phase(nc, c, L):
    sem = lambda s: c.sem(f"attend_{s}")
    scored, shifted, weighed, divided, turned, placed, summed, out_hi, out_lo, own = (sem(s) for s in
        ("scored", "shifted", "weighed", "divided", "turned", "placed", "summed", "out_hi", "out_lo", "own"))
    N = NCH * BKV
    at = lambda i: (i // BKV, i % BKV)
    GQ = BH // BKV

    def keys(i):
        return 128 if at(i)[0] == 0 else 256

    def scores(i):
        return c.P[:, 2 * (i % 2):2 * (i % 2) + 2].rearrange("p b (g k) -> p (b g) k", g=2)[:, :, 0:keys(i)]

    probs = lambda i: L.probs[:, i % 2, :, 0:keys(i)]
    turned_probs = c.P[:, 4:6].rearrange("p b (g q) -> p (b g) q", g=4)
    stat = lambda i, n: L.p_stat[:, i % 2, n]
    MAX, NEGM, SINK, DEN = range(4)
    place = lambda g: g % 2 * 2 + g // 2
    by_place = lambda ap: ap.rearrange("p (t u) -> p u t", u=2)
    square = lambda ap: ap.rearrange("p (u t) -> p u t", u=2)
    out = lambda i: c.P[:, 6 + i % 2, 0:256].rearrange("p (t q) -> p t q", t=2)
    with nc.Block() as block:
        @block.tensor
        def _(pe):
            def score(i):
                blk, kv = at(i)
                if i >= 2:
                    pe.wait_ge(shifted, i - 1)
                for g in (0, 2, 1, 3):
                    rows = slice(g % 2 * HD, g % 2 * HD + HD)
                    ins = pe.matmul(scores(i)[:, place(g)], L.q[rows, 2 * kv + g // 2, blk * 128:(blk + 1) * 128],
                                    L.k2[rows, kv, (blk + 1) * 128 - keys(i):(blk + 1) * 128], start=True, stop=True)
                ins.then_inc(scored, 1)

            score(0)
            for i in range(N):
                blk, kv = at(i)
                if i + 1 < N:
                    score(i + 1)
                nb = keys(i) // 128
                pe.wait_ge(divided, i + 1)
                if i >= 1:
                    pe.wait_ge(placed, i)
                for g in range(GQ):
                    for k in range(nb):
                        ins = pe.transpose(turned_probs[:, 2 * g + k], probs(i)[:, g, k * 128:(k + 1) * 128], cols(c, CI))
                ins.then_inc(turned, 1)
                pe.wait_ge(placed, i + 1)
                if i >= 2:
                    pe.wait_ge(out_lo, i - 1)
                for g in range(GQ):
                    rows = slice(g % 2 * HD, g % 2 * HD + HD)
                    for k in range(nb):
                        ins = pe.matmul(out(i)[rows, g // 2], L.v_tok[:, blk - nb + 1 + k, kv * HD:(kv + 1) * HD],
                                        L.probs_t[:, 2 * place(g) + k], start=(k == 0), stop=(k == nb - 1))
                ins.then_inc(summed, 1)

        @block.vector
        def _(dve):
            def shift(i):
                blk, kv = at(i)
                if i >= 2:
                    dve.wait_ge(turned, i - 1)
                dve.wait_ge(scored, i + 1)
                mask = cols(c, CMASK + 256 - keys(i), keys(i)).unsqueeze(1).broadcast_to([128, GQ, keys(i)])
                nc.vector.scalar_tensor_tensor(probs(i), scores(i), HD ** -0.5, mask, ALU.mult, ALU.add).then_inc(shifted, 1)
                dve.wait_ge(shifted, i + 1)
                sink = by_place(L.sinks[:, kv * GQ:(kv + 1) * GQ])
                chain.link(nc.vector.tensor_reduce(stat(i, MAX), probs(i), AX, ALU.max))
                chain.link(nc.vector.tensor_tensor(square(stat(i, MAX)), square(stat(i, MAX)), sink, ALU.max))
                nc.vector.tensor_scalar(stat(i, NEGM), stat(i, MAX), -1.0, None, ALU.mult)
                nc.vector.tensor_tensor(square(stat(i, SINK)), sink, square(stat(i, MAX)), ALU.subtract).then_inc(L.maxed, 1)

            def low(i):
                blk, kv = at(i)
                dve.wait_ge(out_hi, i + 1)
                x = (slice(None), slice(2 * kv, 2 * kv + 2), slice(blk * 128, blk * 128 + 128))
                nc.vector.tensor_tensor(c.x_lo[x], out(i), c.x_hi[x].bitcast(F32), ALU.subtract).then_inc(out_lo, 1)

            chain = Chain(dve, own)
            shift(0)
            for i in range(N):
                if i + 1 < N:
                    shift(i + 1)
                dve.wait_ge(weighed, i + 1)
                chain.link(nc.vector.tensor_tensor(stat(i, DEN), stat(i, DEN), stat(i, SINK), ALU.add))
                chain.link(nc.vector.reciprocal(stat(i, DEN), stat(i, DEN)))
                nc.vector.tensor_tensor(probs(i), probs(i), stat(i, DEN).unsqueeze(2).broadcast_to([128, GQ, keys(i)]),
                                        ALU.mult).then_inc(divided, 1)
                if i >= 1:
                    low(i - 1)
            low(N - 1)

        @block.scalar
        def _(act):
            def weigh(i):
                act.wait_ge(L.maxed, i + 1)
                for g in range(GQ):
                    nc.scalar.activation(probs(i)[:, g], probs(i)[:, g], ACT.Exp, bias=stat(i, NEGM)[:, g:g + 1],
                                         accum_out=stat(i, DEN)[:, g:g + 1])
                nc.scalar.activation(stat(i, SINK), stat(i, SINK), ACT.Exp).then_inc(weighed, 1)

            weigh(0)
            for i in range(N):
                blk, kv = at(i)
                if i + 1 < N:
                    weigh(i + 1)
                act.wait_ge(turned, i + 1)
                if i >= 1:
                    act.wait_ge(summed, i)
                nb = keys(i) // 128
                view = lambda ap: ap.rearrange("p (g k) q -> p g k q", k=2)[:, :, 0:nb]
                nc.scalar.activation(view(L.probs_t[:]), view(turned_probs), ACT.Copy).then_inc(placed, 1)
                act.wait_ge(summed, i + 1)
                nc.scalar.activation(c.x_hi[:, 2 * kv:2 * kv + 2, blk * 128:(blk + 1) * 128], out(i), ACT.Copy)\
                    .then_inc(out_hi, 1)


def sample_attend_phase(nc, c, L):
    sem = lambda s: c.sem(f"one_{s}")
    pe_step, act_step, own = sem("pe_step"), sem("act_step"), sem("own")
    ident = cols(c, CI)
    qz, kT, sT, sT2, p, st = L.qz, L.k_turned, L.scores_t, L.scores_t2, L.one_probs, L.one_stat
    pairs = BH * TS
    hb = lambda ap: ap.rearrange("p (h b) -> p h b", b=TS)
    with nc.Block() as block:
        @block.tensor
        def _(pe):
            for par in range(2):
                ins = pe.matmul(c.P[:, 0, par * 64:par * 64 + 64], cols(c, CD0 if par == 0 else CD1), L.q[:, :, TP:NT],
                                start=True, stop=True)
            ins.then_inc(pe_step, 1)
            for b in range(TS):
                for j in range(2):
                    n = 2 * b + j
                    ins = pe.transpose(c.P[:, 1 + n // 4, n % 4 * 128:n % 4 * 128 + 128],
                                       L.k_cache[:, b, j * 128:(j + 1) * 128], ident)
            ins.then_inc(pe_step, 1)
            pe.wait_ge(own, 8)
            for kv in range(BKV):
                pe.matmul(c.P[0:TS, 6, kv * 32:kv * 32 + 32], L.k2[:, kv, TP:NT], qz[:, 4 * kv:4 * kv + 4, :]
                          .rearrange("p h b -> p (h b)"), start=True, stop=True)
            pe.wait_ge(act_step, 1)
            for b in range(TS):
                for j in range(2):
                    ins = pe.matmul(hb(c.P[:, 5, 0:pairs])[:, 8 * j:8 * j + 8, b], kT[:, 2 * b + j], qz[:, 8 * j:8 * j + 8, b],
                                    start=True, stop=True)
            ins.then_inc(pe_step, 1)
            pe.wait_ge(act_step, 3)
            pe.transpose(c.P[:, 0, 0:128], sT[:], ident)
            pe.transpose(c.P[:, 0, 128:136], sT2[0:TS], cols(c, CI)[0:TS, 0:TS]).then_inc(pe_step, 1)
            pe.wait_ge(own, 17)
            pe.transpose(c.P[:, 1, 0:128], p[:, 0:128], ident)
            pe.transpose(c.P[0:TS, 2, 0:128], p[:, 128:136], ident).then_inc(pe_step, 1)
            pe.wait_ge(act_step, 7)
            for b in range(TS):
                for j in range(2):
                    o = hb(c.P[:, 7, 0:pairs])[:, 8 * j:8 * j + 8, b]
                    pe.matmul(o, L.v_cache[:, b, j * 128:(j + 1) * 128], hb(sT[:])[:, 8 * j:8 * j + 8, b], start=True, stop=False)
                    ins = pe.matmul(o, L.v_new[0:TS, j * 128:(j + 1) * 128], hb(sT2[0:TS])[:, 8 * j:8 * j + 8, b],
                                    start=False, stop=True)
            ins.then_inc(pe_step, 1)
            pe.wait_ge(own, 19)
            pe.matmul(c.P[:, 0, 0:pairs], cols(c, CFOLD), L.one_out[:], start=True, stop=True).then_inc(pe_step, 1)

        @block.scalar
        def _(act):
            act.wait_ge(pe_step, 2)
            nc.scalar.activation(kT[:].rearrange("p (a n) k -> p a (n k)", a=4), c.P[:, 1:5], ACT.Copy).then_inc(act_step, 1)
            act.wait_ge(pe_step, 3)
            nc.scalar.activation(sT[:], c.P[:, 5, 0:pairs], ACT.Copy).then_inc(act_step, 1)
            nc.scalar.activation(sT2[0:TS], c.P[0:TS, 6, 0:pairs], ACT.Copy).then_inc(act_step, 1)
            act.wait_ge(own, 14)
            nc.scalar.activation(p[:], p[:], ACT.Exp, bias=st[:, 1:2], accum_out=st[:, 3:4]).then_inc(act_step, 1)
            nc.scalar.activation(st[:, 2:3], st[:, 2:3], ACT.Exp).then_inc(act_step, 1)
            act.wait_ge(pe_step, 5)
            nc.scalar.activation(sT[:], c.P[:, 1, 0:128], ACT.Copy).then_inc(act_step, 1)
            nc.scalar.activation(sT2[0:TS], c.P[0:TS, 2, 0:128], ACT.Copy).then_inc(act_step, 1)
            act.wait_ge(pe_step, 7)
            o = c.P[:, 0, 0:pairs].rearrange("p (t u b) -> p t u b", u=2, b=TS)
            for par in range(2):
                rows = slice(par * HD, par * HD + HD)
                nc.scalar.activation(c.x_hi[rows, :, TP:NT], o[rows, :, par], ACT.Copy).then_inc(act_step, 1)

        @block.vector
        def _(dve):
            chain = Chain(dve, own)
            dve.wait_ge(pe_step, 1)
            for par in range(2):
                for kp in range(2):
                    for a in range(2):
                        h0 = a * 8 + kp * 4
                        to = qz[:, h0:h0 + 4].rearrange("p (r u) b -> p r u b", u=2)[:, :, par]
                        t0 = par * 64 + (a * 4 + kp * 2) * TS
                        of = c.P[:, 0, t0:t0 + 2 * TS].rearrange("p (r b) -> p r b", r=2)
                        chain.link(nc.vector.tensor_scalar(to, of, cols(c, CHALF + kp, 1), None, ALU.mult))
            dve.wait_ge(pe_step, 4)
            chain.link(nc.vector.tensor_scalar(p[:, 0:128], c.P[:, 0, 0:128], HD ** -0.5, None, ALU.mult))
            chain.link(nc.vector.scalar_tensor_tensor(p[:, 128:136], c.P[:, 0, 128:136], HD ** -0.5, cols(c, CNEW, 8),
                                                      ALU.mult, ALU.add))
            chain.link(nc.vector.tensor_reduce(st[:, 0:1], p[:], AX, ALU.max))
            chain.link(nc.vector.tensor_tensor(st[:, 0:1], st[:, 0:1], L.sink_rows[:], ALU.max))
            chain.link(nc.vector.tensor_scalar(st[:, 1:2], st[:, 0:1], -1.0, None, ALU.mult))
            chain.link(nc.vector.tensor_tensor(st[:, 2:3], L.sink_rows[:], st[:, 0:1], ALU.subtract))
            dve.wait_ge(act_step, 5)
            chain.link(nc.vector.tensor_tensor(st[:, 3:4], st[:, 3:4], st[:, 2:3], ALU.add))
            chain.link(nc.vector.reciprocal(st[:, 3:4], st[:, 3:4]))
            chain.link(nc.vector.tensor_scalar(p[:], p[:], st[:, 3:4], None, ALU.mult))
            dve.wait_ge(pe_step, 6)
            kinds = lambda ap: ap.rearrange("p (a u n) -> p a u n", a=2, u=2)
            for kp in range(2):
                chain.link(nc.vector.tensor_scalar(kinds(L.one_out[:])[:, :, kp], kinds(c.P[:, 7, 0:pairs])[:, :, kp],
                                                   cols(c, CHALF + kp, 1), None, ALU.mult))
            dve.wait_ge(act_step, 9)
            o = c.P[:, 0, 0:pairs].rearrange("p (t u b) -> p t u b", u=2, b=TS)
            for par in range(2):
                rows = slice(par * HD, par * HD + HD)
                chain.link(nc.vector.tensor_tensor(c.x_lo[rows, :, TP:NT], o[rows, :, par],
                                                   c.x_hi[rows, :, TP:NT].bitcast(F32), ALU.subtract))


def route_phase(nc, c, io, L):
    sem = lambda s: c.sem(f"route_{s}")
    cleared, loaded, hi_ready, lo_ready, pe_step, act_step, own, spread, read = (sem(s) for s in
        ("cleared", "loaded", "hi_ready", "lo_ready", "pe_step", "act_step", "own", "spread", "read"))
    w, w_hi, w_lo = L.r_raw, L.r_hi, L.r_lo
    NB = NCH + 1
    lg, one, two, cand, tmp, comb = (L.r_work[:, i] for i in range(6))
    m1, m2, g1, g2 = (L.r_stat[:, i] for i in range(4))
    per_e = lambda ap: ap.unsqueeze(2).broadcast_to([128, NB, NE])
    with nc.Block() as block:
        @block.gpsimd
        def _(pool):
            nc.gpsimd.memset(w[:], 0.0).then_inc(cleared, 1)
            nc.gpsimd.memset(L.r_work[:], 0.0).then_inc(cleared, 1)

        @block.sync
        def _(sp):
            sp.wait_ge(cleared, 1)
            sp.dma_start(w[:, :, 0:NE], io["moe_router"][0].rearrange("(k p) e -> p k e", p=128)).then_inc(loaded, 16)
            sp.dma_start(L.r_bias[:], io["moe_router_b"].broadcast_to([128, NE])).then_inc(loaded, 16)

        @block.tensor
        def _(pe):
            pe.wait_ge(lo_ready, 1)
            narrow_product(nc, pe, slot(c, 0), w_hi, w_lo, c).then_inc(pe_step, 1)
            pe.wait_ge(act_step, 1)
            for n in range(NCH):
                pe.transpose(c.P[:, 2, n * 128:(n + 1) * 128], L.r_logit[:, n * 128:(n + 1) * 128], cols(c, CI))
            pe.transpose(c.P[0:TS, 3, 0:128], L.r_logit[:, TP:NT], cols(c, CI)).then_inc(pe_step, 1)
            pe.wait_ge(own, 22)
            for e in range(NE):
                if e == 4:
                    pe.wait_ge(read, 4)
                for n in range(NCH):
                    ins = pe.matmul(c.P[:, 4 + e % 4, n * 128:(n + 1) * 128], comb[:, n, e:e + 1].broadcast_to([128, 128]),
                                    cols(c, CI), start=True, stop=True)
                ins.then_inc(spread, 1)
            for e in range(NE):
                ins = pe.matmul(c.P[:, 0, e * TS:(e + 1) * TS], comb[0:TS, NCH, e:e + 1].broadcast_to([TS, 128]),
                                cols(c, CI)[0:TS, 0:TS], start=True, stop=True)
            ins.then_inc(spread, 1)

        @block.scalar
        def _(act):
            act.wait_ge(loaded, 32)
            nc.scalar.activation(w_hi[:], w[:], ACT.Copy).then_inc(hi_ready, 1)
            act.wait_ge(pe_step, 1)
            nc.scalar.activation(halves(L.r_logit[:]), slot(c, 0), ACT.Copy).then_inc(act_step, 1)
            act.wait_ge(own, 16)
            nc.scalar.activation(g2, g2, ACT.Exp).then_inc(act_step, 1)
            for e in range(NE):
                act.wait_ge(spread, e + 1)
                nc.scalar.activation(L.combine[:, e, 0:TP], c.P[:, 4 + e % 4], ACT.Copy).then_inc(read, 1)
            act.wait_ge(spread, NE + 1)
            nc.scalar.activation(L.combine[:, :, TP:NT], c.P[:, 0, 0:NE * TS].rearrange("p (e b) -> p e b", b=TS),
                                 ACT.Copy).then_inc(read, 1)

        @block.vector
        def _(dve):
            dve.wait_ge(hi_ready, 1)
            nc.vector.tensor_tensor(w_lo[:], w[:], w_hi[:].bitcast(F32), ALU.subtract).then_inc(lo_ready, 1)
            chain = Chain(dve, own)
            tt = lambda to, a, b, op: chain.link(nc.vector.tensor_tensor(to, a, b, op))
            stt = lambda to, a, s, b, o0, o1: chain.link(nc.vector.scalar_tensor_tensor(to, a, s, b, o0, o1))
            dve.wait_ge(cleared, 2)
            dve.wait_ge(pe_step, 2)
            bias = L.r_bias[:].unsqueeze(1)
            tt(lg[:, 0:NCH], c.P[:, 2].rearrange("p (n r) -> p n r", n=NCH)[:, :, 0:NE], bias.broadcast_to([128, NCH, NE]), ALU.add)
            tt(lg[0:TS, NCH], c.P[0:TS, 3, 0:NE], L.r_bias[0:TS], ALU.add)
            number = cols(c, CEXP, NE).unsqueeze(1).broadcast_to([128, NB, NE])

            def pick(of, m, hot):
                chain.link(nc.vector.tensor_reduce(m, of, AX, ALU.max))
                tt(hot, of, per_e(m), ALU.is_equal)
                stt(cand, hot, -100.0, number, ALU.mult, ALU.add)
                chain.link(nc.vector.tensor_reduce(g1, cand, AX, ALU.min))
                tt(hot, cand, per_e(g1), ALU.is_equal)

            pick(lg, m1, one)
            stt(tmp, one, NEG, lg, ALU.mult, ALU.add)
            pick(tmp, m2, two)
            chain.link(nc.vector.tensor_copy(g1, m1))
            chain.link(nc.vector.tensor_copy(g2, m2))
            tt(g2, m2, m1, ALU.subtract)
            dve.wait_ge(act_step, 2)
            chain.link(nc.vector.tensor_scalar(g1, g2, 1.0, None, ALU.add))
            chain.link(nc.vector.reciprocal(g1, g1))
            tt(g2, g2, g1, ALU.mult)
            tt(one, one, per_e(g1), ALU.mult)
            tt(two, two, per_e(g2), ALU.mult)
            tt(comb, one, two, ALU.add)


def store_phase(nc, c, io, L):
    sem = lambda s: c.sem(f"store_{s}")
    turned, read_a, read_v, stored = sem("turned"), sem("read_act"), sem("read_vector"), sem("stored")
    with nc.Block() as block:
        @block.tensor
        def _(pe):
            for t in range(NCH + 1):
                n = 128 if t < NCH else TS
                if t >= 4:
                    pe.wait_ge(read_a, 1)
                    pe.wait_ge(read_v, 1)
                for k in range(KT):
                    ins = pe.transpose(c.P[0:n, 2 * (t % 4) + k // 4, k % 4 * 128:k % 4 * 128 + 128],
                                       c.h[:, k, t * 128:t * 128 + n], cols(c, CI))
                ins.then_inc(turned, 1)

        @block.scalar
        def _(act):
            for t in range(NCH + 1):
                n = 128 if t < NCH else TS
                act.wait_ge(turned, t + 1)
                nc.scalar.activation(L.y[0:n, t, 0:512], c.P[0:n, 2 * (t % 4)], ACT.Copy).then_inc(read_a, 1)

        @block.vector
        def _(dve):
            for t in range(NCH + 1):
                n = 128 if t < NCH else TS
                dve.wait_ge(turned, t + 1)
                nc.vector.tensor_copy(L.y[0:n, t, 512:1024], c.P[0:n, 2 * (t % 4) + 1]).then_inc(read_v, 1)

        @block.sync
        def _(sp):
            for t in range(NCH + 1):
                sp.wait_ge(read_a, t + 1)
                sp.wait_ge(read_v, t + 1)
                to = io["y_prompt"][0, t * 128:(t + 1) * 128] if t < NCH else io["y_sample"].rearrange("b s d -> (b s) d")
                sp.dma_start(to, L.y[0:128 if t < NCH else TS, t]).then_inc(stored, 16)
            sp.wait_ge(stored, 16 * (NCH + 1))


def decoder_step(nc, io):
    k_p_n = lambda w: w.rearrange("(k p) n -> p k n", p=128)
    wide = lambda w: (lambda i, j: k_p_n(w)[:, :, ds(i * 512 + j * 256, 256)])
    s_in = Stream(0, (NQKV * 128 + D) // 256, wide(io["a_w_in"][0]))
    s_out = Stream(s_in.end, 4, wide(io["a_w_out"][0]))
    gu = gate_and_up(io["dense_w_gu"][0], 128)
    s_gu = Stream(s_out.end, NFF, lambda i, j: gu(i * 256 + j * 128))
    down = io["dense_w_down"][0].rearrange("(s k p) n -> s p k n", s=2, p=128)
    s_down = Stream(s_gu.end, 2 * KT, lambda i, j: down[j, :, :, ds(i * 128, 128)])
    s_kv = Stream(s_down.end, 2, wide(io["w_kv"]))
    s_q = Stream(s_kv.end, 4, wide(io["b_w_q"][0]))
    s_o = Stream(s_q.end, 4, wide(io["b_w_o"][0]))
    s_moe = ExpertStream(s_o.end, io["moe_w_gu"][0], io["moe_w_down"][0])
    with ExitStack() as whole:
        c = shared_buffers(nc, whole)
        L = Layer()

        def alloc(ctx, tag="", **shapes):
            return [ctx.enter_context(nc.sbuf_tensor(name + tag, shape, F32R if name.endswith(("_hi", "_lo")) else F32))
                    for name, shape in shapes.items()]

        nothing = lambda sp: None
        with ExitStack() as layer_a:
            (L.conv_w, L.conv_state, L.a_log, L.dt_bias, L.a_rate, L.qkv,
             L.z, L.edge, L.g_tok, L.b_tok, L.G_tok, L.gb_sample) = alloc(layer_a, conv_w=[128, 4 * NQKV], conv_state=[128, NQKV, 3 * TS], a_log=[AH, 1], dt_bias=[AH, 1],
                  a_rate=[AH, 1], qkv=[128, NQKV, NT], z=[128, AH, NT], edge=[128, NQKV, 11],
                  g_tok=[128, NCH, AH], b_tok=[128, NCH, AH], G_tok=[128, NCH, AH], gb_sample=[128, 2 * AH * TS])
            load_phase(nc, c, io, L, lambda sp: s_in.start(c, sp, wait=False))
            with ExitStack() as ctx:
                c.x_hi, c.x_lo = split_buffers(nc, ctx, "xa")
                with ExitStack() as inner:
                    L.u, L.y, L.from_state, L.state_term = alloc(inner, u=[128, 2, 3 + NT], y=[128, 2, NT], from_state=[128, NQKV, TS], state_term=[128, NQKV, TS])
                    norm_phase(nc, c, VA)
                    project_in_phase(nc, c, s_in, lambda sp: s_out.start(c, sp), L)
                with ExitStack() as inner:
                    L.ab_raw, L.ab_hi, L.ab_lo, L.spread = alloc(inner, ab_raw=[128, KT, 128], ab_hi=[128, KT, 128], ab_lo=[128, KT, 128], spread=[128, 128])
                    gates_phase(nc, c, io, L)
            with ExitStack() as ctx:
                L.edge_rows, L.norm = alloc(ctx, edge_rows=[11, NQKV * 128], norm=[128, 2, NT])
                edge_phase(nc, c, io, L)
                unit_phase(nc, c, L)
            with ExitStack() as ctx:
                as_heads = lambda ap: ap.rearrange("p a t -> p (a t)")[:, 0:AH * C].rearrange("p (h x) -> p h x", h=AH)
                bufs = [ctx.enter_context(nc.sbuf_tensor(f"delta_{i}", [128, AH, C], F32)) for i in range(13)]
                L.delta = bufs[:12] + [as_heads(c.pair[:]), as_heads(c.scratch[:]), bufs[12]]
                L.small = [ctx.enter_context(nc.sbuf_tensor(f"delta_small_{i}", [128, AH], F32)) for i in range(7)]
                delta_phase(nc, c, io, L)
            with ExitStack() as ctx:
                L.s_state, L.s_kq, L.s_k, L.s_row, L.s_small, L.s_mask = alloc(ctx, s_state=[128, AH * TS, 128], s_kq=[128, AH * TS, 2], s_k=[128, AH * TS],
                      s_row=[128, 2, 128], s_small=[128, 6, AH * TS], s_mask=[128, 2, 512])
                sample_delta_phase(nc, c, io, L)
            with ExitStack() as ctx:
                c.x_hi, c.x_lo = split_buffers(nc, ctx, "xo")
                [L.norm] = alloc(ctx, "_o", norm=[128, 2, NT])
                mixer_out_phase(nc, c, L)
                add_to_residual_phase(nc, c, "a_out", s_out, lambda sp: s_gu.start(c, sp))
        with ExitStack() as ctx:
            c.x_hi, c.x_lo = split_buffers(nc, ctx, "xf")
            L.f_hi, L.f_lo = alloc(ctx, f_hi=[128, NFF, NT], f_lo=[128, NFF, NT])
            L.sg, L.sf = c.pair, c.scratch
            norm_phase(nc, c, VF)
            dense_phase(nc, c, s_gu, s_down, lambda sp: s_kv.start(c, sp), L)
        with ExitStack() as ctx:
            c.x_hi, c.x_lo = split_buffers(nc, ctx, "xb")
            (L.q, L.kv, L.k2, L.v_tok, L.v_new, L.k_rows, L.k_cache,
             L.v_cache, L.sinks, L.sink_rows, L.sink_pick, L.probs, L.probs_t, L.p_stat) = alloc(ctx, q=[128, KT, NT], kv=[128, 4, NT], k2=[128, BKV, NT], v_tok=[128, NCH, 256], v_new=[128, 256],
                  k_rows=[128, 2, 256], k_cache=[128, TS, 256], v_cache=[128, TS, 256], sinks=[128, BH], sink_rows=[128, 1], sink_pick=[128, BH],
                  probs=[128, 2, 4, 256], probs_t=[128, 8, 128], p_stat=[128, 2, 4, 4])
            norm_phase(nc, c, VKV)
            project_phase(nc, c, "kv", s_kv, lambda sp: s_q.start(c, sp), L.kv)
            norm_phase(nc, c, VB)
            project_phase(nc, c, "q", s_q, lambda sp: s_o.start(c, sp), L.q)
            head_norm_phase(nc, c, [(L.q[:, t], VQ) for t in range(KT)] + [(L.kv[:, t], VK) for t in range(2)])
            rotary_phase(nc, c, L)
            L.cache_loaded, L.maxed = c.sem("cache_loaded"), c.sem("attend_maxed")
            window_phase(nc, c, io, L)
            attend_phase(nc, c, L)
            with ExitStack() as inner:
                L.qz, L.k_turned, L.scores_t, L.scores_t2, L.one_probs, L.one_stat, L.one_out = alloc(inner, qz=[128, BH, TS], k_turned=[128, 2 * TS, 128], scores_t=[128, 128], scores_t2=[128, 128],
                      one_probs=[128, 136], one_stat=[128, 4], one_out=[128, 128])
                sample_attend_phase(nc, c, L)
            add_to_residual_phase(nc, c, "b_out", s_o, lambda sp: s_moe.start(c, sp))
        with ExitStack() as ctx:
            c.x_hi, c.x_lo = split_buffers(nc, ctx, "xm")
            [L.combine] = alloc(ctx, combine=[128, NE, NT])
            norm_phase(nc, c, VF + 8)
            with ExitStack() as inner:
                L.r_raw, L.r_hi, L.r_lo, L.r_logit, L.r_bias, L.r_work, L.r_stat = alloc(inner, r_raw=[128, KT, 128], r_hi=[128, KT, 128], r_lo=[128, KT, 128], r_logit=[128, NT],
                      r_bias=[128, NE], r_work=[128, 6, NCH + 1, NE], r_stat=[128, 4, NCH + 1])
                route_phase(nc, c, io, L)
            with ExitStack() as inner:
                L.f_hi, L.f_lo = alloc(inner, "_moe", f_hi=[128, FE // 128, NT], f_lo=[128, FE // 128, NT])
                moe_phase(nc, c, s_moe, nothing, L)
        with ExitStack() as ctx:
            [L.y] = alloc(ctx, "_out", y=[128, NCH + 1, D])
            store_phase(nc, c, io, L)


_INS = ["x_prompt", "x_sample", "state_conv", "state_delta", "cache_k_win", "cache_v_win", "a_norm", "a_w_in",
        "a_conv_w", "a_A_log", "a_dt_bias", "a_o_norm", "a_w_out", "kv_norm", "w_kv", "k_norm", "b_norm", "b_w_q",
        "b_q_norm", "b_sinks", "b_w_o", "ffn_norm", "dense_w_gu", "dense_w_down", "moe_router", "moe_router_b",
        "moe_w_gu", "moe_w_down", "constants"]
_OUTS = [("y_prompt", (1, TP, D)), ("y_sample", (TS, 1, D)), ("new_conv_prompt", (1, 1, 3, NQKV * 128)),
         ("new_conv_sample", (1, TS, 3, NQKV * 128)), ("new_delta_prompt", (1, 1, AH, DK, DK)),
         ("new_delta_sample", (1, TS, AH, DK, DK)), ("new_k_win_prompt", (1, WIN, BKV, HD)),
         ("new_k_win_sample", (TS, WIN, BKV, HD)), ("new_v_win_prompt", (1, WIN, BKV, HD)),
         ("new_v_win_sample", (TS, WIN, BKV, HD))]


def kernel(**inputs):
    import numpy as _np
    import concourse.bacc as _bacc
    from concourse.bass_utils import run_bass_kernel_spmd as _run

    nc = _bacc.Bacc("TRN2", target_bir_lowering=False, num_devices=1)
    arrays, io = {}, {}
    given = {**inputs, **constants()}
    for name in _INS:
        a = _np.ascontiguousarray(given[name])
        arrays[f"in_{name}_dram"] = a
        io[name] = nc.dram_tensor(f"in_{name}_dram", a.shape, F32, kind="ExternalInput").ap()
    for i, (name, shape) in enumerate(_OUTS):
        io[name] = nc.dram_tensor(f"out_{i}_dram", shape, F32, kind="ExternalOutput").ap()
    decoder_step(nc, io)
    r = _run(nc, [arrays], core_ids=[0])
    return tuple(r.results[0][f"out_{i}_dram"] for i in range(len(_OUTS)))
```

```python
from contextlib import ExitStack

import numpy as np
import concourse.bass as bass
from concourse import mybir

F32 = mybir.dt.float32
F32R = mybir.dt.float32r
I32 = mybir.dt.int32
ALU = mybir.AluOpType
ACT = mybir.ActivationFunctionType
AX = mybir.AxisListType.X
ds = bass.ds

D = 1024
KT = D // 128
TP, TS = 512, 8
NT = TP + TS
HALF = NT // 2
AH, DK = 8, 128
NQKV = 3 * AH
C = 128
NCH = TP // C
FF = 2816
NFF = FF // 128
NE, FE = 8, 1024
SLOTS = 256
ROUNDS = -(-NT // SLOTS)
BH, BKV, HD = 16, 4, 64
WIN = 128
PAST = 1024
EPS = 1e-6
NEG = -1e30
CHUNK = 2048

CI, CONE, CU, CM16, CBO, CROT, CD0, CD1, CRD0, CRD1, CFOLD = (128 * i for i in range(11))
CCOS = 128 * 11
CSIN = CCOS + NT
CMASK = CSIN + NT
CNEW = CMASK + 256
CEXP = CNEW + 8
CHALF = CEXP + 8
CEPS = CHALF + 2
CHEAD = CEPS + 1
CIOTA = CHEAD + 16
CSLOT = CIOTA + SLOTS
NCST = CSLOT + SLOTS // 128

VA, VKV, VB, VF, VO, VK, VQ = 0, 8, 16, 24, 40, 41, 42
NVEC = 43


def constants():
    t = np.zeros((128, NCST), np.float32)
    i = np.arange(128)
    eye = np.eye(128, dtype=np.float32)
    t[:, CI:CI + 128] = eye
    t[:, CONE:CONE + 128] = 1.0
    t[:, CU:CU + 128] = i[:, None] <= i[None, :]
    t[:, CM16:CM16 + 128] = i[:, None] // 16 == i[None, :] // 16
    t[:, CBO:CBO + 128] = i[:, None] // HD == i[None, :] // HD
    rot_half = HD // 8
    rot = np.zeros((128, 128), np.float32)
    for m in range(128):
        if m % HD < rot_half:
            rot[m + rot_half, m] = -1.0
        elif m % HD < 2 * rot_half:
            rot[m - rot_half, m] = 1.0
    dup = [np.zeros((128, 128), np.float32) for _ in range(2)]
    for m in range(128):
        dup[0][m % HD, m] = 1.0
        dup[1][HD + m % HD, m] = 1.0
    t[:, CROT:CROT + 128] = rot
    t[:, CD0:CD0 + 128] = dup[0]
    t[:, CD1:CD1 + 128] = dup[1]
    t[:, CRD0:CRD0 + 128] = dup[0] @ rot
    t[:, CRD1:CRD1 + 128] = dup[1] @ rot
    t[:, CFOLD:CFOLD + 128] = i[:, None] % HD == i[None, :] % HD
    pos = np.concatenate([np.arange(TP), np.full(TS, PAST)]).astype(np.float32)
    rd = 2 * rot_half
    inv = np.power(np.float32(500000.0), -np.arange(0, rd, 2, dtype=np.float32) / np.float32(rd)).astype(np.float32)
    ang = (pos[None, :] * inv[:, None]).astype(np.float32).astype(np.float64)
    t[:, CCOS:CCOS + NT] = 1.0
    for m in range(128):
        if m % HD < rd:
            t[m, CCOS:CCOS + NT] = np.cos(ang[m % HD % rot_half])
            t[m, CSIN:CSIN + NT] = np.sin(ang[m % HD % rot_half])
    t[:, CMASK:CMASK + 128] = np.where(i[None, :] >= i[:, None], 0.0, NEG)
    t[:, CMASK + 128:CMASK + 256] = np.where(i[None, :] <= i[:, None], 0.0, NEG)
    t[:, CNEW:CNEW + 8] = np.where(np.arange(8)[None, :] == i[:, None] % 8, 0.0, NEG)
    t[:, CEXP:CEXP + 8] = 100 + np.arange(8)[None, :]
    t[:64, CHALF] = 1.0
    t[64:, CHALF + 1] = 1.0
    t[:, CEPS] = EPS
    t[:, CHEAD:CHEAD + 16] = i[:, None] // 8 == np.arange(16)[None, :]
    t[:, CIOTA:CIOTA + SLOTS] = np.arange(SLOTS)[None, :]
    t[:, CSLOT:CSLOT + SLOTS // 128] = i[:, None] + 128 * np.arange(SLOTS // 128)[None, :]
    return {"constants": t}


class Chain:

    def __init__(self, eng, sem, base=0):
        self.eng, self.sem, self.base, self.k = eng, sem, base, 0

    def link(self, ins):
        self.k += 1
        ins.then_inc(self.sem, 1)
        self.eng.wait_ge(self.sem, self.base + self.k)


class Core:
    pass


class Layer:
    pass


def split_buffers(nc, ctx, name):
    return [ctx.enter_context(nc.sbuf_tensor(f"{name}_{part}", [128, KT, NT], F32R)) for part in ("hi", "lo")]


def shared_buffers(nc, ctx):
    c = Core()
    sb = lambda name, shape, dt=F32: ctx.enter_context(nc.sbuf_tensor(name, shape, dt))
    c.sem = lambda name: ctx.enter_context(nc.semaphore(name))
    c.cst = sb("cst", [128, NCST])
    c.vec = sb("vec", [128, NVEC])
    c.h = sb("h", [128, KT, NT])
    c.w_raw = sb("w_raw", [128, 2, CHUNK])
    c.w_hi = sb("w_hi", [128, 2, CHUNK], F32R)
    c.w_lo = sb("w_lo", [128, 2, CHUNK], F32R)
    c.scratch = sb("scratch", [128, 2, NT])
    c.pair = sb("pair", [128, 2, NT])
    c.rstd = c.scratch[:, 0]
    c.P = ctx.enter_context(nc.psum_tensor("P", [128, 8, 512], F32))
    c.raw_loaded = [c.sem("raw_loaded0"), c.sem("raw_loaded1")]
    c.hi_done = c.sem("hi_done")
    c.h_even = c.sem("h_even")
    c.lo_done = c.sem("lo_done")
    c.norm_sems = [c.sem("norm_" + s) for s in ("squared", "summed", "ms_ready", "root_ready", "scaled",
                                                "hi_ready", "low_ready", "own")]
    c.norms = 0
    return c


def cols(c, at, n=128):
    return c.cst[:, at:at + n]


def slot(c, s):
    return c.P[:, 2 * s:2 * s + 2, 0:HALF]


def halves(ap):
    return ap.rearrange("p (b t) -> p b t", b=2)



def load_chunk(c, sp, number, s, src, wait=True):
    if wait:
        sp.wait_ge(c.lo_done, number - 1)
    k_tiles, width = (src[0] if isinstance(src, tuple) else src).shape[1:]
    if isinstance(src, tuple):
        dst = c.w_raw[:, s, 0:k_tiles * 2 * width].rearrange("p (k g f) -> p k g f", k=k_tiles, g=2)
        parts = [(dst[:, :, g], src[g]) for g in range(2)]
    else:
        dst = c.w_raw[:, s, 0:k_tiles * width].rearrange("p (k f) -> p k f", k=k_tiles)
        half = k_tiles // 2
        parts = [(dst[:, 0:half], src[:, 0:half]), (dst[:, half:], src[:, half:])]
    for to, of in parts:
        sp.dma_start(to, of).then_inc(c.raw_loaded[s], 16)


def gate_and_up(w, width):
    w = w.rearrange("(k p) (g f) -> p g k f", p=128, g=2)
    return lambda at: tuple(w[:, g, :, ds(at, width)] for g in range(2))


def three_products(nc, out, w_hi, w_lo, x_hi, x_lo, first, last):
    for n, (w, x) in enumerate(((w_hi, x_hi), (w_hi, x_lo), (w_lo, x_hi))):
        for b in range(2):
            ins = nc.tensor.matmul(out[:, b], w, x[:, b * HALF:(b + 1) * HALF],
                                   start=(first and n == 0), stop=(last and n == 2))
    return ins


class Stream:

    def __init__(self, base, n, src):
        assert base % 2 == 0 and n % 2 == 0
        self.base, self.n, self.src = base, n, src
        self.end = base + n

    def number(self, i, j):
        return i * 2 + (self.base + j)

    def start(self, c, sp, wait=True):
        for j in range(2):
            load_chunk(c, sp, self.base + j, j, self.src(0, j), wait)

    def rest(self, c, sp):
        with sp.Fori(1, self.n // 2) as i:
            for j in range(2):
                load_chunk(c, sp, self.number(i, j), j, self.src(i, j))

    def split_hi(self, nc, c, act, i, j):
        act.wait_ge(c.raw_loaded[j % 2], i * 32 + 32 * ((self.base + j) // 2 + 1))
        nc.scalar.activation(c.w_hi[:, j % 2], c.w_raw[:, j % 2], ACT.Copy).then_inc(c.hi_done, 1)

    def split_lo(self, nc, c, dve, i, j):
        dve.wait_ge(c.hi_done, self.number(i, j) + 1)
        nc.vector.tensor_tensor(c.w_lo[:, j % 2], c.w_raw[:, j % 2], c.w_hi[:, j % 2].bitcast(F32),
                                ALU.subtract).then_inc(c.lo_done, 1)


def over(eng, n, body):
    if n > 1:
        with eng.Fori(0, n - 1) as i:
            body(i, False)
    body(n - 1, True)


def square_tensor(nc, c, pe, st, ready, evacuated):
    def body(i, last):
        for j in range(2):
            pe.wait_ge(c.lo_done, st.number(i, j) + 1)
            for m in range(2):
                g = 2 * j + m
                pe.wait_ge(evacuated, i * 4 + (g + 1))
                for k in range(KT):
                    at = k * 256 + m * 128
                    ins = three_products(nc, slot(c, g), c.w_hi[:, j, at:at + 128], c.w_lo[:, j, at:at + 128],
                                         c.x_hi[:, k], c.x_lo[:, k], k == 0, k == KT - 1)
                ins.then_inc(ready, 1)
    over(pe, st.n // 2, body)


def norm_phase(nc, c, gain):
    squared, summed, ms_ready, root_ready, scaled, hi_ready, low_ready, own = c.norm_sems
    one, all_ = c.norms, c.norms * KT
    c.norms += 1
    with nc.Block() as block:
        @block.scalar
        def _(act):
            for k in range(KT):
                if k >= 2:
                    act.wait_ge(summed, all_ + k - 1)
                nc.scalar.activation(c.pair[:, k % 2], c.h[:, k], ACT.Square).then_inc(squared, 1)
            act.wait_ge(ms_ready, one + 1)
            nc.scalar.activation(c.rstd, c.rstd, ACT.Sqrt).then_inc(root_ready, 1)
            for k in range(KT):
                act.wait_ge(scaled, all_ + k + 1)
                nc.scalar.activation(c.x_hi[:, k], c.pair[:, k % 2], ACT.Copy).then_inc(hi_ready, 1)

        @block.tensor
        def _(pe):
            for k in range(KT):
                pe.wait_ge(squared, all_ + k + 1)
                for b in range(2):
                    ins = pe.matmul(c.P[:, b, 0:HALF], cols(c, CONE), c.pair[:, k % 2, b * HALF:(b + 1) * HALF],
                                    start=(k == 0), stop=(k == KT - 1))
                ins.then_inc(summed, 1)

        @block.vector
        def _(dve):
            dve.wait_ge(summed, all_ + KT)
            nc.vector.tensor_scalar(halves(c.rstd), slot(c, 0), 1.0 / D, EPS, ALU.mult, ALU.add).then_inc(ms_ready, 1)
            dve.wait_ge(root_ready, one + 1)
            nc.vector.reciprocal(c.rstd, c.rstd).then_inc(own, 1)
            dve.wait_ge(own, one + 1)
            for k in range(KT + 1):
                if k < KT:
                    if k >= 2:
                        dve.wait_ge(low_ready, all_ + k - 1)
                    nc.vector.scalar_tensor_tensor(c.pair[:, k % 2], c.h[:, k], c.vec[:, gain + k:gain + k + 1],
                                                   c.rstd, ALU.mult, ALU.mult).then_inc(scaled, 1)
                if k >= 1:
                    dve.wait_ge(hi_ready, all_ + k)
                    nc.vector.tensor_tensor(c.x_lo[:, k - 1], c.pair[:, (k - 1) % 2],
                                            c.x_hi[:, k - 1].bitcast(F32), ALU.subtract).then_inc(low_ready, 1)


def load_phase(nc, c, io, L, sp_work):
    with ExitStack() as ctx:
        xt = ctx.enter_context(nc.sbuf_tensor("x_tokens", [128, 5, D], F32))
        rows = ctx.enter_context(nc.sbuf_tensor("vector_rows", [128, 128], F32))
        crow = ctx.enter_context(nc.sbuf_tensor("conv_rows", [128, 128], F32))
        srow = ctx.enter_context(nc.sbuf_tensor("state_rows", [TS * 3, NQKV * 128], F32))
        in_c, in_v, in_x, in_s = c.sem("in_constants"), c.sem("in_vectors"), c.sem("in_tokens"), c.sem("in_state")
        turned, read = c.sem("load_turned"), c.sem("load_read")
        with nc.Block() as block:
            @block.sync
            def _(sp):
                sp.dma_start(c.cst[:], io["constants"]).then_inc(in_c, 16)
                for t in range(4):
                    sp.dma_start(xt[:, t], io["x_prompt"][0, t * 128:(t + 1) * 128]).then_inc(in_x, 16)
                sp.dma_start(xt[0:TS, 4], io["x_sample"].rearrange("b s d -> (b s) d")).then_inc(in_x, 16)
                sp_work(sp)
                sp.dma_start(srow[:], io["state_conv"][0].rearrange("b j f -> (b j) f")).then_inc(in_s, 16)

            @block.scalar
            def _(act):
                as_rows = lambda v: v.rearrange("(k p) -> k p", p=128)
                parts = [(VA, 8, as_rows(io["a_norm"][0])), (VKV, 8, as_rows(io["kv_norm"])),
                         (VB, 8, as_rows(io["b_norm"][0])), (VF, 8, as_rows(io["ffn_norm"][0])),
                         (VF + 8, 8, as_rows(io["ffn_norm"][1])), (VO, 1, io["a_o_norm"])]
                for at, n, src in parts:
                    act.dma_start(rows[at:at + n, :], src).then_inc(in_v, 16)
                for at, v in ((VK, io["k_norm"].rearrange("(a d) -> a d", a=1)), (VQ, io["b_q_norm"])):
                    for half in range(2):
                        act.dma_start(rows[at:at + 1, half * HD:(half + 1) * HD], v).then_inc(in_v, 16)
                act.dma_start(crow[0:96, :], io["a_conv_w"][0].rearrange("j (m p) -> (j m) p", p=128)).then_inc(in_v, 16)
                act.dma_start(L.a_log[:], io["a_A_log"].rearrange("a h -> h a")).then_inc(in_v, 16)
                act.dma_start(L.dt_bias[:], io["a_dt_bias"].rearrange("a h -> h a")).then_inc(in_v, 16)
                for k in range(1, KT, 2):
                    act.wait_ge(turned, k + 1)
                    nc.scalar.activation(c.h[:, k, 0:TP], c.P[:, k % 4], ACT.Copy).then_inc(read, 1)

            @block.tensor
            def _(pe):
                ident = cols(c, CI)
                pe.wait_ge(in_c, 16)
                pe.wait_ge(in_x, 80)
                for k in range(KT):
                    if k >= 4:
                        pe.wait_ge(c.h_even, (k - 4) // 2 + 1)
                        if k % 2:
                            pe.wait_ge(read, (k - 4) // 2 + 1)
                    for t in range(4):
                        ins = pe.transpose(c.P[:, k % 4, t * 128:(t + 1) * 128], xt[:, t, k * 128:(k + 1) * 128], ident)
                    ins.then_inc(turned, 1)
                for k in range(KT):
                    ins = pe.transpose(c.P[:, 4, k * TS:(k + 1) * TS], xt[0:TS, 4, k * 128:(k + 1) * 128], cols(c, CI)[0:TS, 0:TS])
                ins.then_inc(turned, 1)
                pe.wait_ge(in_v, 16 * 13)
                pe.transpose(c.P[:, 5, 0:NVEC], rows[0:NVEC, :], cols(c, CI)[0:NVEC, 0:NVEC]).then_inc(turned, 1)
                pe.transpose(c.P[:, 6, 0:96], crow[0:96, :], cols(c, CI)[0:96, 0:96]).then_inc(turned, 1)
                pe.wait_ge(in_s, 16)
                for m in range(NQKV):
                    if m == 0:
                        pe.wait_ge(c.h_even, 4)
                        pe.wait_ge(read, 4)
                    ins = pe.transpose(c.P[:, m // AH, (m % AH) * 24:(m % AH) * 24 + 24],
                                       srow[:, m * 128:(m + 1) * 128], cols(c, CI)[0:24, 0:24])
                ins.then_inc(turned, 1)

            @block.vector
            def _(dve):
                for k in range(0, KT, 2):
                    dve.wait_ge(turned, k + 1)
                    nc.vector.tensor_copy(c.h[:, k, 0:TP], c.P[:, k % 4]).then_inc(c.h_even, 1)
                dve.wait_ge(turned, KT + 1)
                nc.vector.tensor_copy(c.h[:, :, TP:NT], c.P[:, 4, 0:KT * TS].rearrange("p (k t) -> p k t", k=KT))
                dve.wait_ge(turned, KT + 2)
                nc.vector.tensor_copy(c.vec[:], c.P[:, 5, 0:NVEC])
                dve.wait_ge(turned, KT + 3)
                nc.vector.tensor_copy(L.conv_w[:], c.P[:, 6, 0:96])
                dve.wait_ge(turned, KT + 4)
                for part in range(3):
                    nc.vector.tensor_copy(L.conv_state[:, part * AH:(part + 1) * AH],
                                          c.P[:, part, 0:192].rearrange("p (m r) -> p m r", m=AH))


def project_in_phase(nc, c, st, sp_next, L):
    sem = lambda s: c.sem(f"in_{s}")
    ready, evacuated, convolved, y_free, own = (sem(s) for s in ("ready", "evacuated", "convolved", "y_free", "own"))
    with nc.Block() as block:
        @block.sync
        def _(sp):
            st.rest(c, sp)
            sp_next(sp)

        @block.tensor
        def _(pe):
            square_tensor(nc, c, pe, st, ready, evacuated)

        @block.scalar
        def _(act):
            act.sem_inc(evacuated, 4)
            act.sem_inc(y_free, 2)
            st.split_hi(nc, c, act, 0, 0)

            def silu(m, y):
                nc.scalar.activation(L.qkv[:, m], L.y[:, y], ACT.Silu).then_inc(y_free, 1)

            def qkv(i, first):
                for j in range(2):
                    st.split_hi(nc, c, act, i, j + 1)
                    for m in range(2):
                        g = 2 * j + m
                        act.wait_ge(ready, i * 4 + (g + 1))
                        nc.scalar.activation(halves(L.u[:, g % 2, 3:3 + NT]), slot(c, g), ACT.Copy).then_inc(evacuated, 1)
                        if not (first and g == 0):
                            act.wait_ge(convolved, i * 4 + g)
                            silu(i * 4 + (g - 1) if g else i * 4 - 1, (g - 1) % 2)
            qkv(0, True)
            with act.Fori(1, NQKV // 4) as i:
                qkv(i, False)
            act.wait_ge(convolved, NQKV)
            silu(NQKV - 1, 1)
            for i in range(NQKV // 4, st.n // 2):
                for j in range(2):
                    if 2 * i + j + 1 < st.n:
                        st.split_hi(nc, c, act, i, j + 1)
                    for m in range(2):
                        g = 2 * j + m
                        act.wait_ge(ready, i * 4 + (g + 1))
                        nc.scalar.activation(halves(L.z[:, 4 * i + g - NQKV]), slot(c, g), ACT.Silu).then_inc(evacuated, 1)

        @block.vector
        def _(dve):
            nc.vector.memset(L.u[:, :, 0:3], 0.0)
            sw = lambda j: L.conv_w[:, j * NQKV:(j + 1) * NQKV].unsqueeze(2).broadcast_to([128, NQKV, TS])
            rows = L.conv_state[:].rearrange("p m (b j) -> p m b j", j=3)
            chain = Chain(dve, own)
            chain.link(nc.vector.tensor_tensor(L.from_state[:], rows[:, :, :, 0], sw(0), ALU.mult))
            for j in (1, 2):
                chain.link(nc.vector.tensor_tensor(L.state_term[:], rows[:, :, :, j], sw(j), ALU.mult))
                chain.link(nc.vector.tensor_tensor(L.from_state[:], L.from_state[:], L.state_term[:], ALU.add))
            st.split_lo(nc, c, dve, 0, 0)
            done = chain.k

            with dve.Fori(0, NQKV // 4) as i:
                chain = Chain(dve, own, i * 20 + done)
                for j in range(2):
                    st.split_lo(nc, c, dve, i, j + 1)
                    for m in range(2):
                        g = 2 * j + m
                        u, y = L.u[:, g % 2], L.y[:, g % 2]
                        tile = lambda t: t[:, ds(i * 4 + g, 1)].rearrange("p a t -> p (a t)")
                        w = lambda tap: L.conv_w[:, ds(i * 4 + (tap * NQKV + g), 1)]
                        dve.wait_ge(evacuated, i * 4 + (g + 5))
                        dve.wait_ge(y_free, i * 4 + (g + 1))
                        chain.link(nc.vector.tensor_scalar(y, u[:, 3:3 + NT], w(3), None, ALU.mult))
                        for tap in (2, 1, 0):
                            chain.link(nc.vector.scalar_tensor_tensor(
                                y[:, 0:TP], u[:, tap:tap + TP], w(tap), y[:, 0:TP], ALU.mult, ALU.add))
                        chain.link(nc.vector.tensor_copy(tile(L.edge), u[:, TP:TP + 11]))
                        nc.vector.tensor_tensor(y[:, TP:NT], y[:, TP:NT], tile(L.from_state), ALU.add).then_inc(convolved, 1)
            for l in range(NQKV // 2 + 1, st.n):
                st.split_lo(nc, c, dve, l // 2, l % 2)


def narrow_product(nc, pe, out, w_hi, w_lo, c):
    for k in range(KT):
        ins = three_products(nc, out, w_hi[:, k], w_lo[:, k], c.x_hi[:, k], c.x_lo[:, k], k == 0, k == KT - 1)
    return ins


def gates_phase(nc, c, io, L):
    sem = lambda s: c.sem(f"gate_{s}")
    cleared, loaded, hi_ready, lo_ready, ab_ready, own_v, own_a = (sem(s) for s in
        ("cleared", "loaded", "hi_ready", "lo_ready", "ab_ready", "own_vector", "own_scalar"))
    act_step, dve_step, turned = (sem(s) for s in ("act_step", "dve_step", "turned"))
    w, w_hi, w_lo = L.ab_raw, L.ab_hi, L.ab_lo
    gb = c.scratch[:, 0]
    t1, t2, t3 = c.pair[0:AH, 0], c.pair[0:AH, 1], c.scratch[0:AH, 1]
    with nc.Block() as block:
        @block.gpsimd
        def _(pool):
            nc.gpsimd.memset(w[:], 0.0).then_inc(cleared, 1)
            nc.gpsimd.memset(gb, 0.0).then_inc(cleared, 1)

        @block.sync
        def _(sp):
            w_in = io["a_w_in"][0].rearrange("(k p) n -> p k n", p=128)
            sp.wait_ge(cleared, 1)
            for at, col in ((0, NQKV * 128 + D), (32, NQKV * 128 + D + AH)):
                sp.dma_start(w[:, :, at:at + AH], w_in[:, :, col:col + AH]).then_inc(loaded, 16)

        @block.tensor
        def _(pe):
            pe.wait_ge(lo_ready, 1)
            narrow_product(nc, pe, slot(c, 0), w_hi, w_lo, c).then_inc(ab_ready, 1)
            pe.wait_ge(dve_step, 5)
            for n in range(NCH):
                ins = pe.transpose(c.P[:, 2, n * 128:(n + 1) * 128], gb[:, n * C:(n + 1) * C], cols(c, CI))
            ins.then_inc(turned, 1)
            pe.wait_ge(dve_step, 7)
            pe.matmul(c.P[:, 3, 0:128], cols(c, CONE), L.spread[:], start=True, stop=True).then_inc(turned, 1)
            pe.wait_ge(dve_step, 8)
            pe.matmul(c.P[:, 4, 0:NCH * AH], cols(c, CU), L.g_tok[:].rearrange("p n h -> p (n h)"),
                      start=True, stop=True).then_inc(turned, 1)

        @block.scalar
        def _(act):
            act.wait_ge(loaded, 32)
            nc.scalar.activation(w_hi[:], w[:], ACT.Copy).then_inc(hi_ready, 1)
            act.wait_ge(ab_ready, 1)
            act.wait_ge(cleared, 2)
            nc.scalar.activation(halves(gb[32:40, :]), c.P[32:40, 0:2, 0:HALF], ACT.Sigmoid).then_inc(act_step, 1)
            nc.scalar.activation(L.a_rate[:], L.a_log[:], ACT.Exp).then_inc(act_step, 1)
            act.wait_ge(dve_step, 3)
            nc.scalar.activation(t2, t2, ACT.Exp).then_inc(own_a, 1)
            act.wait_ge(own_a, 1)
            nc.scalar.activation(t2, t2, ACT.Ln, bias=1.0).then_inc(act_step, 1)

        @block.vector
        def _(dve):
            dve.wait_ge(hi_ready, 1)
            nc.vector.tensor_tensor(w_lo[:], w[:], w_hi[:].bitcast(F32), ALU.subtract).then_inc(lo_ready, 1)
            step = Chain(dve, dve_step)
            dve.wait_ge(act_step, 1)
            step.link(nc.vector.tensor_scalar(halves(t1), c.P[0:AH, 0:2, 0:HALF], L.dt_bias[:], None, ALU.add))
            step.link(nc.vector.tensor_scalar(t2, t1, -1.0, None, ALU.mult))
            step.link(nc.vector.tensor_tensor(t2, t2, t1, ALU.min))
            dve.wait_ge(act_step, 3)
            step.link(nc.vector.scalar_tensor_tensor(t3, t1, 0.0, t2, ALU.max, ALU.add))
            step.link(nc.vector.tensor_scalar(gb[0:AH, :], t3, L.a_rate[:], -1.0, ALU.mult, ALU.mult))
            for w_, row in ((0, 0), (1, 32)):
                step.link(nc.vector.tensor_tensor(
                    L.spread[:, w_ * 64:w_ * 64 + 64].rearrange("p (h b) -> p h b", b=TS),
                    gb[:, TP:NT].unsqueeze(1).broadcast_to([128, AH, TS]),
                    cols(c, CI + row, AH).unsqueeze(2).broadcast_to([128, AH, TS]), ALU.mult))
            dve.wait_ge(turned, 1)
            tok = c.P[:, 2].rearrange("p (n r) -> p n r", n=NCH)
            step.link(nc.vector.tensor_copy(L.g_tok[:], tok[:, :, 0:AH]))
            step.link(nc.vector.tensor_copy(L.b_tok[:], tok[:, :, 32:32 + AH]))
            dve.wait_ge(turned, 2)
            step.link(nc.vector.tensor_copy(L.gb_sample[:], c.P[:, 3, 0:128]))
            dve.wait_ge(turned, 3)
            step.link(nc.vector.tensor_copy(L.G_tok[:].rearrange("p n h -> p (n h)"), c.P[:, 4, 0:NCH * AH]))


def edge_phase(nc, c, io, L):
    sem = lambda s: c.sem(f"edge_{s}")
    turned, read, stored = sem("turned"), sem("read"), sem("stored")
    with nc.Block() as block:
        @block.sync
        def _(sp):
            sp.dma_start(io["new_conv_sample"][0][:, 0:2], io["state_conv"][0][:, 1:3]).then_inc(stored, 16)
            sp.wait_ge(read, 6)
            sp.dma_start(io["new_conv_prompt"][0, 0], L.edge_rows[0:3, :]).then_inc(stored, 16)
            sp.dma_start(io["new_conv_sample"][0, :, 2], L.edge_rows[3:11, :]).then_inc(stored, 16)
            sp.wait_ge(stored, 48)

        @block.tensor
        def _(pe):
            for part in range(6):
                for m in range(4):
                    ins = pe.transpose(c.P[0:11, part, m * 128:(m + 1) * 128], L.edge[:, part * 4 + m], cols(c, CI))
                ins.then_inc(turned, 1)

        @block.scalar
        def _(act):
            for part in range(6):
                act.wait_ge(turned, part + 1)
                nc.scalar.activation(L.edge_rows[:, part * 512:(part + 1) * 512], c.P[0:11, part], ACT.Copy).then_inc(read, 1)


def unit_phase(nc, c, L):
    sem = lambda s: c.sem(f"unit_{s}")
    squared, summed, rooted, own, scaled = (sem(s) for s in ("squared", "summed", "rooted", "own", "scaled"))
    with nc.Block() as block:
        @block.scalar
        def _(act):
            def square(i, g, wait):
                if wait:
                    act.wait_ge(summed, i * 4 + (g - 1))
                nc.scalar.activation(c.pair[:, g % 2], L.qkv[:, i * 4 + g], ACT.Square).then_inc(squared, 1)

            def root(i, g):
                act.wait_ge(summed, i * 4 + (g + 1))
                act.wait_ge(scaled, i * 4 + (g + 1))
                nc.scalar.activation(halves(L.norm[:, g % 2]), slot(c, g), ACT.Sqrt,
                                     bias=cols(c, CEPS, 1)).then_inc(rooted, 1)

            def body(i, first):
                for g in range(4):
                    square(i, g, not (first and g < 2))
                    if not (first and g == 0):
                        root(i if g else i - 1, g - 1 if g else 3)
            body(0, True)
            with act.Fori(1, 2 * AH // 4) as i:
                body(i, False)
            root(2 * AH // 4 - 1, 3)

        @block.tensor
        def _(pe):
            def body(i, first):
                for g in range(4):
                    pe.wait_ge(squared, i * 4 + (g + 1))
                    if not first:
                        pe.wait_ge(rooted, i * 4 + (g - 3))
                    for b in range(2):
                        ins = pe.matmul(slot(c, g)[:, b], cols(c, CONE), c.pair[:, g % 2, b * HALF:(b + 1) * HALF],
                                        start=True, stop=True)
                    ins.then_inc(summed, 1)
            body(0, True)
            with pe.Fori(1, 2 * AH // 4) as i:
                body(i, False)

        @block.vector
        def _(dve):
            dve.sem_inc(scaled, 2)
            for part, scale in ((0, DK ** -0.5), (1, 1.0)):
                with dve.Fori(part * 2, part * 2 + 2) as i:
                    for g in range(4):
                        dve.wait_ge(rooted, i * 4 + (g + 1))
                        nc.vector.reciprocal(L.norm[:, g % 2], L.norm[:, g % 2]).then_inc(own, 1)
                        dve.wait_ge(own, i * 4 + (g + 1))
                        x = L.qkv[:, i * 4 + g]
                        nc.vector.scalar_tensor_tensor(x, x, scale, L.norm[:, g % 2], ALU.mult, ALU.mult)\
                            .then_inc(scaled, 1)


class Steps:

    def __init__(self, c, name, steps):
        self.steps, self.at = steps, {}
        self.sems = {who: c.sem(f"{name}_{who}") for who in steps}
        self.passed = c.sem(f"{name}_passed")

    def begin(self, eng, who, n):
        self.at[who] = 0
        for other, sem in self.sems.items():
            if other != who:
                eng.wait_ge(sem, n * len(self.steps[other]) + 1)

    def done(self, ins, who, step):
        assert self.steps[who][self.at[who]] == step, (who, step)
        self.at[who] += 1
        return ins.then_inc(self.sems[who], 1)

    def after(self, eng, n, **steps):
        for who, step in steps.items():
            eng.wait_ge(self.sems[who], n * len(self.steps[who]) + (self.steps[who].index(step) + 2))

    def stand(self, eng):
        eng.sem_inc(self.passed, 1)


def delta_phase(nc, c, io, L):
    st = Steps(c, "delta", {
        "pe": ["decay", "k_tok", "v_tok", "kk", "qk", "L_T", "B2", "B2_T", "X_B2", "W_B2", "B4", "B4_T",
               "X_B4", "W_B4", "B8", "B8_T", "X_B8", "W_B8", "N", "N_T", "kS", "X_N", "N2", "N2_T", "X_N2", "N4",
               "X_N4", "v_new", "S_add", "out"],
        "act": ["e_last", "e_tok", "e_left", "e_row", "e_L", "e_attn", "L_T", "B2", "B2_T", "B4", "B4_T",
                "B8", "B8_T", "N", "N_T", "N2", "N2_T", "N4", "v_new", "out"],
        "dve": ["g", "G", "beta", "diff", "left", "k_dec", "b_dec", "b_v", "L_raw", "L", "B", "attn", "q_dec", "B_T", "X", "W",
                "X_B2", "W_B2", "X_B4", "W_B4", "X_B8", "W_B8", "R_raw", "R", "X_N", "X_N2", "X_N4", "S"],
        "pool": ["k", "v", "q", "mask_L", "mask_attn", "E_T", "S_dec"],
    })
    stored, cleared = c.sem("delta_stored"), c.sem("delta_cleared")
    B = L.delta
    kc, qc, vc, AT, LM, KD, BV, LT, P1, P1T, X, W, P2, P2T, S = B
    g_c, G_c, b_c, e_tok, e_left, e_last, b_dec = L.small

    def per_head(ap):
        return ap[:].unsqueeze(2).broadcast_to([128, AH, C])

    def both(s):
        return c.P[:, 2 * s:2 * s + 2].rearrange("p b (h x) -> p (b h) x", h=4)

    def for_heads(ap):
        return ap.unsqueeze(1).broadcast_to([128, AH, C])

    ident = cols(c, CI)

    def products(pe, s, lhs, rhs):
        for h in range(AH):
            ins = pe.matmul(both(s)[:, h], lhs[:, h], rhs[:, h], start=True, stop=True)
        return ins

    with nc.Block() as block:
        @block.sync
        def _(sp):
            st.after(sp, NCH - 1, dve="S")
            sp.dma_start(io["new_delta_prompt"][0, 0].rearrange("h k v -> k h v"), S[:]).then_inc(stored, 16)
            sp.wait_ge(stored, 16)

        @block.gpsimd
        def _(pool):
            nc.gpsimd.memset(S[:], 0.0).then_inc(cleared, 1)
            pool.sem_inc(st.sems["pool"], 1)
            high, low = pool.to_reg(-NEG), pool.to_reg(NEG)
            with pool.Fori(0, NCH) as n:
                st.begin(pool, "pool", n)
                for name, to, at in (("k", kc, AH), ("v", vc, 2 * AH), ("q", qc, 0)):
                    st.done(nc.gpsimd.tensor_copy(to[:], L.qkv[:, at:at + AH, ds(n * C, C)]), "pool", name)
                st.after(pool, n, dve="diff")
                st.stand(pool)
                st.done(nc.gpsimd.affine_select(out=LM[:], in_=AT[:], compare_op=ALU.is_gt, fill=high, base=0,
                                                pattern=[[0, AH], [-1, C]], channel_multiplier=1), "pool", "mask_L")
                st.after(pool, n, pool="mask_L")
                st.stand(pool)
                st.done(nc.gpsimd.affine_select(out=AT[:], in_=AT[:], compare_op=ALU.is_ge, fill=low, base=0,
                                                pattern=[[0, AH], [1, C]], channel_multiplier=-1), "pool", "mask_attn")
                st.after(pool, n, act="L_T", dve="B_T")
                st.done(nc.gpsimd.tensor_tensor(LT[:], LT[:], P1T[:], ALU.subtract), "pool", "E_T")
                st.after(pool, n, act="e_last", pe="N4")
                st.done(nc.gpsimd.tensor_tensor(P2[:], S[:], per_head(e_last), ALU.mult), "pool", "S_dec")

        @block.tensor
        def _(pe):
            pe.sem_inc(st.sems["pe"], 1)
            pe.wait_ge(cleared, 1)
            with pe.Fori(0, NCH) as n:
                st.begin(pe, "pe", n)
                st.after(pe, n, dve="g")
                for h in range(AH):
                    ins = pe.matmul(both(0)[:, h], g_c[:, h:h + 1].broadcast_to([128, 128]), cols(c, CU), start=True, stop=True)
                st.done(ins, "pe", "decay")
                for s, x, step in ((1, kc, "k"), (2, vc, "v")):
                    st.after(pe, n, pool=step)
                    for h in range(AH):
                        ins = pe.transpose(both(s)[:, h], x[:, h], ident)
                    st.done(ins, "pe", step + "_tok")
                st.done(products(pe, 3, kc, kc), "pe", "kk")
                st.after(pe, n, pool="q", act="e_row", dve="left")
                st.done(products(pe, 0, kc, qc), "pe", "qk")
                st.after(pe, n, dve="L")
                for h in range(AH):
                    ins = pe.transpose(both(1)[:, h], LM[:, h], ident)
                st.done(ins, "pe", "L_T")
                st.after(pe, n, dve="B_T")
                st.done(products(pe, 2, P1T, P1), "pe", "B2")
                st.done(products(pe, 3, P1, P1T), "pe", "B2_T")
                st.after(pe, n, dve="X", act="B2")
                st.done(products(pe, 0, P2, X), "pe", "X_B2")
                st.after(pe, n, dve="W", act="B2_T")
                st.done(products(pe, 1, P2T, W), "pe", "W_B2")
                st.done(products(pe, 2, P2T, P2), "pe", "B4")
                st.done(products(pe, 3, P2, P2T), "pe", "B4_T")
                st.after(pe, n, dve="X_B2", act="B4")
                st.done(products(pe, 0, P1, X), "pe", "X_B4")
                st.after(pe, n, dve="W_B2", act="B4_T")
                st.done(products(pe, 1, P1T, W), "pe", "W_B4")
                st.done(products(pe, 2, P1T, P1), "pe", "B8")
                st.done(products(pe, 3, P1, P1T), "pe", "B8_T")
                st.after(pe, n, dve="X_B4", act="B8")
                st.done(products(pe, 0, P2, X), "pe", "X_B8")
                st.after(pe, n, dve="W_B4", act="B8_T")
                st.done(products(pe, 1, P2T, W), "pe", "W_B8")
                st.after(pe, n, dve="W_B8", pool="E_T")
                st.done(products(pe, 2, LT, W), "pe", "N")
                st.done(products(pe, 3, W, LT), "pe", "N_T")
                st.done(products(pe, 1, kc, S), "pe", "kS")
                st.after(pe, n, dve="X_B8", act="N")
                st.done(products(pe, 0, P1, X), "pe", "X_N")
                st.after(pe, n, act="N_T")
                st.done(products(pe, 2, P1T, P1), "pe", "N2")
                st.done(products(pe, 3, P1, P1T), "pe", "N2_T")
                st.after(pe, n, dve="X_N", act="N2")
                st.done(products(pe, 0, P2, X), "pe", "X_N2")
                st.after(pe, n, act="N2_T")
                st.done(products(pe, 2, P2T, P2), "pe", "N4")
                st.after(pe, n, dve="X_N2", act="N4")
                st.done(products(pe, 0, P1, X), "pe", "X_N4")
                st.after(pe, n, dve="X_N4")
                st.done(products(pe, 1, X, vc), "pe", "v_new")
                st.after(pe, n, act="v_new")
                st.done(products(pe, 2, KD, P2T), "pe", "S_add")
                for h in range(AH):
                    pe.matmul(both(3)[:, h], S[:, h], qc[:, h], start=True, stop=False)
                    ins = pe.matmul(both(3)[:, h], P2T[:, h], AT[:, h], start=False, stop=True)
                st.done(ins, "pe", "out")

        @block.scalar
        def _(act):
            act.sem_inc(st.sems["act"], 1)
            with act.Fori(0, NCH) as n:
                st.begin(act, "act", n)
                last = both(0)[:, :, C - 1]

                def exp(to, of, step, scale=1.0):
                    st.done(nc.scalar.activation(to, of, ACT.Exp, scale=scale), "act", step)

                def copy(to, s, step):
                    st.after(act, n, pe=step)
                    st.done(nc.scalar.activation(to[:], both(s), ACT.Copy), "act", step)

                st.after(act, n, dve="left")
                exp(e_last[:], last, "e_last")
                exp(e_tok[:], G_c[:], "e_tok")
                exp(e_left[:], e_left[:], "e_left")
                st.after(act, n, pe="v_tok")
                exp(vc[:], both(0), "e_row")
                st.after(act, n, pool="mask_L")
                exp(LM[:], LM[:], "e_L", scale=-1.0)
                st.after(act, n, pool="mask_attn")
                exp(AT[:], AT[:], "e_attn")
                st.after(act, n, dve="B_T")
                copy(LT, 1, "L_T")
                copy(P2, 2, "B2")
                copy(P2T, 3, "B2_T")
                st.after(act, n, pool="E_T", dve="W")
                copy(P1, 2, "B4")
                copy(P1T, 3, "B4_T")
                copy(P2, 2, "B8")
                copy(P2T, 3, "B8_T")
                copy(P1, 2, "N")
                copy(P1T, 3, "N_T")
                copy(P2, 2, "N2")
                copy(P2T, 3, "N2_T")
                copy(P1, 2, "N4")
                copy(P2T, 1, "v_new")
                st.after(act, n, pe="out")
                st.done(nc.scalar.activation(L.qkv[:, 2 * AH:3 * AH, ds(n * C, C)], both(3), ACT.Copy), "act", "out")

        @block.vector
        def _(dve):
            dve.sem_inc(st.sems["dve"], 1)
            with dve.Fori(0, NCH) as n:
                st.begin(dve, "dve", n)

                def tt(step, to, a, b, op):
                    st.done(nc.vector.tensor_tensor(to, a, b, op), "dve", step)

                for name, to, of in (("g", g_c, L.g_tok), ("G", G_c, L.G_tok), ("beta", b_c, L.b_tok)):
                    st.done(nc.vector.tensor_copy(to[:], of[:, n]), "dve", name)
                st.after(dve, n, pe="decay", dve="G")
                tt("diff", AT[:], both(0), per_head(G_c), ALU.subtract)
                tt("left", e_left[:], both(0)[:, :, C - 1], G_c[:], ALU.subtract)
                st.after(dve, n, pe="k_tok", act="e_left")
                tt("k_dec", KD[:], both(1), per_head(e_left), ALU.mult)
                st.done(nc.vector.scalar_tensor_tensor(b_dec[:], e_tok[:], -1.0, b_c[:], ALU.mult, ALU.mult), "dve", "b_dec")
                st.after(dve, n, pe="v_tok", dve="beta")
                tt("b_v", BV[:], both(2), per_head(b_c), ALU.mult)
                st.after(dve, n, pe="kk", act="e_L")
                tt("L_raw", LM[:], both(3), LM[:], ALU.mult)
                st.after(dve, n, dve="L_raw")
                tt("L", LM[:], LM[:], per_head(b_c), ALU.mult)
                st.after(dve, n, dve="L")
                tt("B", P1[:], LM[:], for_heads(cols(c, CM16)), ALU.mult)
                st.after(dve, n, pe="qk", act="e_attn")
                tt("attn", AT[:], both(0), AT[:], ALU.mult)
                tt("q_dec", qc[:], qc[:], vc[:], ALU.mult)
                st.after(dve, n, pe="L_T")
                tt("B_T", P1T[:], both(1), for_heads(cols(c, CM16)), ALU.mult)
                st.after(dve, n, dve="B_T")
                tt("X", X[:], for_heads(ident), P1T[:], ALU.subtract)
                tt("W", W[:], for_heads(ident), P1[:], ALU.subtract)
                for step in ("B2", "B4", "B8"):
                    st.after(dve, n, pe="X_" + step)
                    tt("X_" + step, X[:], X[:], both(0), ALU.add)
                    st.after(dve, n, pe="W_" + step)
                    tt("W_" + step, W[:], W[:], both(1), ALU.add)
                st.after(dve, n, pe="kS", dve="b_dec")
                tt("R_raw", vc[:], both(1), per_head(b_dec), ALU.mult)
                st.after(dve, n, dve="R_raw")
                tt("R", vc[:], vc[:], BV[:], ALU.add)
                for step, op in (("N", ALU.subtract), ("N2", ALU.add), ("N4", ALU.add)):
                    st.after(dve, n, pe="X_" + step)
                    tt("X_" + step, X[:], X[:], both(0), op)
                st.after(dve, n, pe="out", pool="S_dec")
                tt("S", S[:], P2[:], both(2), ALU.add)


def sample_delta_phase(nc, c, io, L):
    sem = lambda s: c.sem(f"step_{s}")
    arrived, stored, pe_step, own, act_step, masked, outer, updated = (sem(s) for s in
        ("arrived", "stored", "pe_step", "own", "act_step", "masked", "outer", "updated"))
    NP = AH * TS
    S, kq, row = L.s_state, L.s_kq, L.s_row
    sm = lambda i: L.s_small[:, i]
    tok = lambda part: L.qkv[:, part * AH:(part + 1) * AH, TP:NT]
    hb = lambda ap: ap.rearrange("p (h b) -> p h b", b=TS)
    E_G, V_MEM, DELTA, DOT, OUT, PROD = range(6)
    with nc.Block() as block:
        @block.sync
        def _(sp):
            for h in range(AH):
                sp.dma_start(S[:, h * TS:(h + 1) * TS], io["state_delta"][0, :, h].rearrange("b k v -> k b v")).then_inc(arrived, 16)
            sp.wait_ge(updated, NP + 8)
            for h in range(AH):
                sp.dma_start(io["new_delta_sample"][0, :, h].rearrange("b k v -> k b v"), S[:, h * TS:(h + 1) * TS])\
                    .then_inc(stored, 16)
            sp.wait_ge(stored, 16 * AH)

        @block.scalar
        def _(act):
            nc.scalar.activation(sm(E_G), L.gb_sample[:, 0:NP], ACT.Exp).then_inc(act_step, 1)

        @block.tensor
        def _(pe):
            pe.wait_ge(own, 3)
            pe.matmul(c.P[:, 1, 0:NP], cols(c, CONE), sm(PROD), start=True, stop=True).then_inc(pe_step, 1)
            pe.transpose(c.P[0:NP, 2, 0:128], L.s_k[:], cols(c, CI)).then_inc(pe_step, 1)
            pe.wait_ge(arrived, 16 * AH)
            for p in range(NP):
                ins = pe.matmul(c.P[:, 0, 2 * p:2 * p + 2], S[:, p], kq[:, p], start=True, stop=True)
            ins.then_inc(pe_step, 1)
            pe.wait_ge(own, 7)
            pe.transpose(c.P[0:NP, 3, 0:128], sm(DELTA), cols(c, CI)).then_inc(pe_step, 1)
            with pe.Fori(0, NP // 8) as i:
                for j in range(2):
                    pe.wait_ge(masked, i * 2 + (j + 1))
                    pe.wait_ge(updated, i * 8 + (4 * j + 1))
                    pe.matmul(c.P[:, 4 + j], row[0:NP, 0, :], L.s_mask[0:NP, j], start=True, stop=True).then_inc(outer, 1)

        @block.vector
        def _(dve):
            chain = Chain(dve, own)
            chain.link(nc.vector.tensor_copy(kq[:, :, 0].rearrange("p (h b) -> p h b", b=TS), tok(1)))
            chain.link(nc.vector.tensor_copy(kq[:, :, 1].rearrange("p (h b) -> p h b", b=TS), tok(0)))
            nc.vector.tensor_copy(hb(L.s_k[:]), tok(1))
            chain.link(nc.vector.tensor_tensor(hb(sm(PROD)), tok(1), tok(0), ALU.mult))
            dve.wait_ge(pe_step, 3)
            dve.wait_ge(act_step, 1)
            chain.link(nc.vector.tensor_copy(sm(DOT), c.P[:, 1, 0:NP]))
            kqS = c.P[:, 0, 0:2 * NP].rearrange("p (n t) -> p n t", t=2)
            chain.link(nc.vector.tensor_tensor(sm(V_MEM), kqS[:, :, 0], sm(E_G), ALU.mult))
            chain.link(nc.vector.tensor_tensor(hb(sm(DELTA)), tok(2), hb(sm(V_MEM)), ALU.subtract))
            chain.link(nc.vector.tensor_tensor(sm(DELTA), sm(DELTA), L.gb_sample[:, NP:2 * NP], ALU.mult))
            chain.link(nc.vector.tensor_tensor(sm(OUT), kqS[:, :, 1], sm(E_G), ALU.mult))
            chain.link(nc.vector.tensor_tensor(sm(V_MEM), sm(DOT), sm(DELTA), ALU.mult))
            chain.link(nc.vector.tensor_tensor(tok(2), hb(sm(OUT)), hb(sm(V_MEM)), ALU.add))
            chain.link(nc.vector.tensor_copy(row[0:NP, 0, :], c.P[0:NP, 2, 0:128]))
            dve.wait_ge(pe_step, 4)
            chain.link(nc.vector.tensor_copy(row[0:NP, 1, :], c.P[0:NP, 3, 0:128]))
            dve.sem_inc(updated, 8)
            with dve.Fori(0, NP // 8) as i:
                for j in range(2):
                    nc.vector.tensor_tensor(L.s_mask[0:NP, j].rearrange("p (n v) -> p n v", n=4),
                                            row[0:NP, 1, :].unsqueeze(1).broadcast_to([NP, 4, 128]),
                                            c.cst[0:NP, ds(i * 8 + (CI + 4 * j), 4)].unsqueeze(2).broadcast_to([NP, 4, 128]),
                                            ALU.mult).then_inc(masked, 1)
                for j in range(2):
                    dve.wait_ge(outer, i * 2 + (j + 1))
                    for q in range(4):
                        p = i * 8 + (4 * j + q)
                        nc.vector.scalar_tensor_tensor(S[:, p], S[:, p], L.s_small[:, E_G, ds(p, 1)],
                                                       c.P[:, 4 + j, q * 128:(q + 1) * 128], ALU.mult, ALU.add).then_inc(updated, 1)


def mixer_out_phase(nc, c, L):
    sem = lambda s: c.sem(f"onorm_{s}")
    squared, summed, rooted, own, gated, hi_ready, freed = (sem(s) for s in
        ("squared", "summed", "rooted", "own", "gated", "hi_ready", "freed"))
    o = lambda h: L.qkv[:, 2 * AH + h]
    with nc.Block() as block:
        @block.scalar
        def _(act):
            def square(h):
                if h >= 2:
                    act.wait_ge(summed, h - 1)
                nc.scalar.activation(c.pair[:, h % 2], o(h), ACT.Square).then_inc(squared, 1)

            square(0)
            for h in range(AH):
                if h + 1 < AH:
                    square(h + 1)
                act.wait_ge(summed, h + 1)
                if h >= 2:
                    act.wait_ge(freed, h - 1)
                nc.scalar.activation(halves(L.norm[:, h % 2]), slot(c, h % 4), ACT.Sqrt, scale=1.0 / DK,
                                     bias=cols(c, CEPS, 1)).then_inc(rooted, 1)
            for h in range(AH):
                act.wait_ge(gated, h + 1)
                nc.scalar.activation(c.x_hi[:, h], o(h), ACT.Copy).then_inc(hi_ready, 1)

        @block.tensor
        def _(pe):
            for h in range(AH):
                pe.wait_ge(squared, h + 1)
                if h >= 4:
                    pe.wait_ge(rooted, h - 3)
                for b in range(2):
                    ins = pe.matmul(slot(c, h % 4)[:, b], cols(c, CONE), c.pair[:, h % 2, b * HALF:(b + 1) * HALF],
                                    start=True, stop=True)
                ins.then_inc(summed, 1)

        @block.vector
        def _(dve):
            chain = Chain(dve, own)
            for h in range(AH):
                r = L.norm[:, h % 2]
                dve.wait_ge(rooted, h + 1)
                chain.link(nc.vector.reciprocal(r, r))
                nc.vector.scalar_tensor_tensor(o(h), o(h), c.vec[:, VO:VO + 1], r, ALU.mult, ALU.mult).then_inc(freed, 1)
                dve.wait_ge(freed, h + 1)
                nc.vector.tensor_tensor(o(h), o(h), L.z[:, h], ALU.mult).then_inc(gated, 1)
            for h in range(AH):
                dve.wait_ge(hi_ready, h + 1)
                nc.vector.tensor_tensor(c.x_lo[:, h], o(h), c.x_hi[:, h].bitcast(F32), ALU.subtract).then_inc(own, 1)


def add_to_residual_phase(nc, c, name, st, sp_next):
    ready, evacuated = c.sem(f"{name}_ready"), c.sem(f"{name}_evacuated")
    with nc.Block() as block:
        @block.sync
        def _(sp):
            st.rest(c, sp)
            sp_next(sp)

        @block.tensor
        def _(pe):
            square_tensor(nc, c, pe, st, ready, evacuated)

        @block.scalar
        def _(act):
            st.split_hi(nc, c, act, 0, 0)

            def body(i, last):
                for j in range(2):
                    if not (last and j == 1):
                        st.split_hi(nc, c, act, i, j + 1)
                    act.wait_ge(ready, i * 4 + (2 * j + 2))
            over(act, st.n // 2, body)

        @block.vector
        def _(dve):
            dve.sem_inc(evacuated, 4)
            st.split_lo(nc, c, dve, 0, 0)

            def body(i, last):
                for j in range(2):
                    if not (last and j == 1):
                        st.split_lo(nc, c, dve, i, j + 1)
                    for m in range(2):
                        g = 2 * j + m
                        dve.wait_ge(ready, i * 4 + (g + 1))
                        hm = halves(c.h[:, i * 4 + g])
                        nc.vector.tensor_tensor(hm, hm, slot(c, g), ALU.add).then_inc(evacuated, 1)
            over(dve, st.n // 2, body)


def gate_up_tensor(nc, c, pe, number, at, ready, gate_read, up_read, j):
    pe.wait_ge(c.lo_done, number + 1)
    for m, read in ((0, gate_read), (1, up_read)):
        pe.wait_ge(read, at + 1)
        for k in range(KT):
            w = k * 256 + m * 128
            ins = three_products(nc, slot(c, 2 * j + m), c.w_hi[:, j, w:w + 128], c.w_lo[:, j, w:w + 128],
                                 c.x_hi[:, k], c.x_lo[:, k], k == 0, k == KT - 1)
        ins.then_inc(ready, 1)


def dense_phase(nc, c, st_gu, st_down, sp_next, L):
    sem = lambda s: c.sem(f"dense_{s}")
    ready, gate_read, up_read, f_hi_ready, f_ready, down_ready, added = (sem(s) for s in
        ("ready", "gate_read", "up_read", "f_hi_ready", "f_ready", "down_ready", "added"))
    with nc.Block() as block:
        @block.sync
        def _(sp):
            st_gu.rest(c, sp)
            st_down.start(c, sp)
            st_down.rest(c, sp)
            sp_next(sp)

        @block.tensor
        def _(pe):
            def gu(i, last):
                for j in range(2):
                    gate_up_tensor(nc, c, pe, st_gu.number(i, j), i * 2 + j, ready, gate_read, up_read, j)
            over(pe, NFF // 2, gu)
            pe.wait_ge(f_ready, NFF)

            def down(i, last):
                for t in range(2):
                    pe.wait_ge(added, i * 2 + (t + 1))
                    for part in range(2):
                        pe.wait_ge(c.lo_done, i * 4 + (st_down.base + 2 * t + part + 1))
                        for k in range(NFF // 2):
                            f = part * (NFF // 2) + k
                            ins = three_products(nc, slot(c, t), c.w_hi[:, part, k * 128:(k + 1) * 128],
                                                 c.w_lo[:, part, k * 128:(k + 1) * 128], L.f_hi[:, f], L.f_lo[:, f],
                                                 f == 0, f == NFF - 1)
                        ins.then_inc(down_ready, 1)
            over(pe, KT // 2, down)

        @block.scalar
        def _(act):
            act.sem_inc(gate_read, 2)
            nc.scalar.activation(L.table[:], cols(c, CONE, 1), ACT.Silu)
            st_gu.split_hi(nc, c, act, 0, 0)

            def gu(i, last):
                for j in range(2):
                    if last and j == 1:
                        st_down.split_hi(nc, c, act, 0, 0)
                    else:
                        st_gu.split_hi(nc, c, act, i, j + 1)
                    act.wait_ge(ready, i * 4 + (2 * j + 1))
                    nc.scalar.activation(halves(L.sg[:, j]), slot(c, 2 * j), ACT.Silu).then_inc(gate_read, 1)
                    act.wait_ge(up_read, i * 2 + (j + 3))
                    nc.scalar.activation(L.f_hi[:, i * 2 + j], L.sf[:, j], ACT.Copy).then_inc(f_hi_ready, 1)
            over(act, NFF // 2, gu)
            act.wait_ge(ready, 2 * NFF)

            def down(i, last):
                for q in range(4):
                    if not (last and q == 3):
                        st_down.split_hi(nc, c, act, i * 2, q + 1)
                    act.wait_ge(down_ready, i * 4 + (q + 1))
            over(act, KT // 2, down)

        @block.vector
        def _(dve):
            dve.sem_inc(up_read, 2)
            dve.sem_inc(added, 2)
            st_gu.split_lo(nc, c, dve, 0, 0)

            def gu(i, last):
                for j in range(2):
                    if last and j == 1:
                        st_down.split_lo(nc, c, dve, 0, 0)
                    else:
                        st_gu.split_lo(nc, c, dve, i, j + 1)
                    dve.wait_ge(ready, i * 4 + (2 * j + 2))
                    dve.wait_ge(gate_read, i * 2 + (j + 3))
                    nc.vector.tensor_tensor(halves(L.sf[:, j]), halves(L.sg[:, j]), slot(c, 2 * j + 1), ALU.mult)\
                        .then_inc(up_read, 1)
                    dve.wait_ge(f_hi_ready, i * 2 + (j + 1))
                    nc.vector.tensor_tensor(L.f_lo[:, i * 2 + j], L.sf[:, j], L.f_hi[:, i * 2 + j].bitcast(F32),
                                            ALU.subtract).then_inc(f_ready, 1)
            over(dve, NFF // 2, gu)

            def down(i, last):
                for t in range(2):
                    for part in range(2):
                        if not (last and t == 1 and part == 1):
                            st_down.split_lo(nc, c, dve, i * 2, 2 * t + part + 1)
                    dve.wait_ge(down_ready, i * 4 + (2 * t + 2))
                    hm = halves(c.h[:, i * 2 + t])
                    nc.vector.tensor_tensor(hm, hm, slot(c, t), ALU.add).then_inc(added, 1)
            over(dve, KT // 2, down)


class ExpertStream:

    def __init__(self, base, w_gu, w_down):
        assert base % 2 == 0
        self.base, self.gu, self.down = base, w_gu, w_down
        self.n_gu = FE // 128
        self.per = self.n_gu + FE // 256

    def number(self, v, n):
        return v * self.per + (self.base + n)

    def load(self, c, sp, v, e, n, wait=True):
        if n < self.n_gu:
            src = gate_and_up(self.gu[e], 128)(n * 128)
        else:
            at = (n - self.n_gu) * 256
            src = self.down[e][at:at + 256].rearrange("(k p) f -> p k f", p=128)
        load_chunk(c, sp, self.number(v, n), n % 2, src, wait)

    def start(self, c, sp, wait=True):
        for n in range(2):
            self.load(c, sp, 0, 0, n, wait)

    def rest(self, c, sp, rounds):
        def visit(r, e, following):
            for n in range(2, self.per):
                self.load(c, sp, r * NE + e, e, n)
            for n in range(2):
                self.load(c, sp, r * NE + (e + 1), following, n)
        with sp.Fori(0, rounds) as r:
            with sp.Fori(0, NE - 1) as e:
                visit(r, e, e + 1)
            visit(r, NE - 1, 0)

    def split_hi(self, nc, c, act, v, n):
        act.wait_ge(c.raw_loaded[n % 2], v * (16 * self.per) + 32 * ((self.base + n) // 2 + 1))
        nc.scalar.activation(c.w_hi[:, n % 2], c.w_raw[:, n % 2], ACT.Copy).then_inc(c.hi_done, 1)

    def split_lo(self, nc, c, dve, v, n):
        dve.wait_ge(c.hi_done, self.number(v, n) + 1)
        nc.vector.tensor_tensor(c.w_lo[:, n % 2], c.w_raw[:, n % 2], c.w_hi[:, n % 2].bitcast(F32),
                                ALU.subtract).then_inc(c.lo_done, 1)


def visits(eng, rounds, body):
    with eng.Fori(0, rounds) as r:
        with eng.Fori(0, NE) as e:
            body(r * NE + e, e)


def moe_phase(nc, c, st, L):
    sem = lambda s: c.sem(f"moe_{s}")
    (ready, gate_read, up_read, f_hi_ready, f_ready, picked, gathered, xg_hi_done, xg_lo_done, slot_gated, gates_read,
     diag_ready, spread, placed, down_used, y_ready, y_hi_done, y_lo_done, scattered, added, own) = (sem(s) for s in
        ("ready", "gate_read", "up_read", "f_hi_ready", "f_ready", "picked", "gathered", "xg_hi_done", "xg_lo_done",
         "slot_gated", "gates_read", "diag_ready", "spread", "placed", "down_used", "y_ready", "y_hi_done", "y_lo_done",
         "scattered", "added", "own"))
    NF, ND = st.n_gu, st.per - st.n_gu
    ST = SLOTS // 128
    gate_bank = lambda j: c.P[:, 2 * j, 0:SLOTS]
    up_bank = lambda j: c.P[:, 2 * j + 1, 0:SLOTS]
    y_bank = lambda b, t: c.P[:, 4 + 2 * b + t]
    load_rounds = lambda eng: eng.value_load(L.rounds[0:1, 0:1], min_val=1, max_val=ROUNDS)
    blocks = [(n, 128 if n < NCH else TS) for n in range(NCH + 1)]
    with nc.Block() as block:
        @block.sync
        def _(sp):
            st.rest(c, sp, load_rounds(sp))

        @block.tensor
        def _(pe):
            def gather(v, e):
                pe.wait_ge(picked, v + 1)
                for k in range(KT):
                    j = k % 2
                    if k >= 2:
                        pe.wait_ge(xg_hi_done, v * KT + (k - 1))
                        pe.wait_ge(xg_lo_done, v * KT + (k - 1))
                    for out, x in ((gate_bank(j), L.xt_hi), (up_bank(j), L.xt_lo)):
                        for n, rows in blocks:
                            ins = nc.tensor.matmul(out, x[0:rows, n, k * 128:(k + 1) * 128], L.pick_hi[0:rows, n],
                                                   start=(n == 0), stop=(n == NCH))
                    ins.then_inc(gathered, 1)
                for t in range(ST):
                    for n, rows in blocks:
                        ins = nc.tensor.matmul(c.P[:, 6, t:t + 1], L.pick_hi[0:rows, n, t * 128:(t + 1) * 128].bitcast(F32),
                                               L.comb[0:rows, n, ds(e, 1)], start=(n == 0), stop=(n == NCH))
                ins.then_inc(slot_gated, 1)

            def visit(v, e):
                pe.wait_ge(xg_hi_done, v * KT + KT)
                pe.wait_ge(xg_lo_done, v * KT + KT)
                pe.wait_ge(added, v * KT + KT)
                pe.sem_inc(L.passed, 1)
                with pe.Fori(0, NF // 2) as i:
                    for j in range(2):
                        pe.wait_ge(c.lo_done, v * st.per + (i * 2 + (st.base + j + 1)))
                        for m, out, read in ((0, gate_bank(j), gate_read), (1, up_bank(j), up_read)):
                            pe.wait_ge(read, v * NF + (i * 2 + (j + 1)))
                            for k in range(KT):
                                w = k * 256 + m * 128
                                w_hi, w_lo = c.w_hi[:, j, w:w + 128], c.w_lo[:, j, w:w + 128]
                                for n, (a, x) in enumerate(((w_hi, L.xg_hi), (w_hi, L.xg_lo), (w_lo, L.xg_hi))):
                                    ins = nc.tensor.matmul(out, a, x[:, k], start=(k == 0 and n == 0),
                                                           stop=(k == KT - 1 and n == 2))
                            ins.then_inc(ready, 1)
                pe.wait_ge(diag_ready, v + 1)
                pe.wait_ge(y_lo_done, v * (2 * ST) + 2 * ST)
                nc.tensor.matmul(c.P[:, 4], cols(c, CONE), L.diag[:, 0:NCH].rearrange("p n t -> p (n t)"), start=True, stop=True)
                nc.tensor.matmul(c.P[:, 5, 0:TS], cols(c, CONE)[0:TS], L.diag[0:TS, NCH, 0:TS],
                                 start=True, stop=True).then_inc(spread, 1)
                pe.wait_ge(gate_read, v * NF + (NF + 2))
                pe.wait_ge(up_read, v * NF + (NF + 2))
                gather(v + 1, e + 1)
                pe.wait_ge(f_ready, v * NF + NF)
                pe.wait_ge(placed, v * (2 * ST) + 2 * ST)
                pe.wait_ge(gates_read, v + 2)
                for q in range(ND):
                    pe.wait_ge(c.lo_done, v * st.per + (st.base + NF + q + 1))
                    for b in range(2):
                        for t in range(ST):
                            for k in range(2):
                                f, w = 2 * q + k, k * D + b * 512
                                f_hi, f_lo = (x[:, f, t * 128:(t + 1) * 128] for x in (L.f_hi, L.f_lo))
                                w_hi, w_lo = (x[:, q % 2, w:w + 512] for x in (c.w_hi, c.w_lo))
                                for n, (a, x) in enumerate(((f_hi, w_hi), (f_hi, w_lo), (f_lo, w_hi))):
                                    ins = nc.tensor.matmul(y_bank(b, t), a, x, start=(f == 0 and n == 0),
                                                           stop=(f == NF - 1 and n == 2))
                            if q == ND - 1:
                                ins.then_inc(y_ready, 1)
                    if q < ND - 1:
                        ins.then_inc(down_used, 1)
                pe.wait_ge(xg_hi_done, v * KT + 2 * KT)
                pe.wait_ge(xg_lo_done, v * KT + 2 * KT)
                for k in range(KT):
                    if k % 4 == 0:
                        pe.wait_ge(y_lo_done, v * (2 * ST) + (2 * ST + (k // 4 + 1) * ST))
                    if k >= 2:
                        pe.wait_ge(added, v * KT + (KT + k - 1))
                    for n, (y, t) in enumerate((y, t) for y in (L.y_hi, L.y_lo) for t in range(ST)):
                        for b in range(2):
                            ins = nc.tensor.matmul(slot(c, k % 2)[:, b], y[:, t, k * 128:(k + 1) * 128],
                                                   L.place_hi[:, t, b * HALF:(b + 1) * HALF],
                                                   start=(n == 0), stop=(n == 2 * ST - 1))
                    ins.then_inc(scattered, 1)

            rounds = load_rounds(pe)
            gather(0, 0)
            visits(pe, rounds, visit)

        @block.scalar
        def _(act):
            rounds = load_rounds(act)
            act.sem_inc(gate_read, 2)
            nc.scalar.activation(L.table[:], cols(c, CONE, 1), ACT.Silu)
            st.split_hi(nc, c, act, 0, 0)

            def gathered_high(v):
                for k in range(KT):
                    act.wait_ge(gathered, v * KT + (k + 1))
                    nc.scalar.activation(L.xg_hi[:, k], gate_bank(k % 2), ACT.Copy).then_inc(xg_hi_done, 1)

            def visit(v, e):
                with act.Fori(0, NF // 2) as i:
                    for j in range(2):
                        act.wait_ge(c.raw_loaded[(j + 1) % 2], v * (16 * st.per) + (i * 32 + 32 * ((st.base + j + 1) // 2 + 1)))
                        nc.scalar.activation(c.w_hi[:, (j + 1) % 2], c.w_raw[:, (j + 1) % 2], ACT.Copy).then_inc(c.hi_done, 1)
                        act.wait_ge(ready, v * (2 * NF) + (i * 4 + (2 * j + 1)))
                        nc.scalar.activation(L.sg[:, j, 0:SLOTS], gate_bank(j), ACT.Silu).then_inc(gate_read, 1)
                        act.wait_ge(up_read, v * NF + (i * 2 + (j + 3)))
                        nc.scalar.activation(L.f_hi[:, i * 2 + j], L.sf[:, j, 0:SLOTS], ACT.Copy).then_inc(f_hi_ready, 1)
                gathered_high(v + 1)
                for q in range(ND):
                    if q:
                        act.wait_ge(down_used, v * (ND - 1) + q)
                    st.split_hi(nc, c, act, v, NF + q + 1)
                act.wait_ge(gates_read, v + 2)
                for n, (b, t) in enumerate((b, t) for b in range(2) for t in range(ST)):
                    act.wait_ge(y_ready, v * (2 * ST) + (n + 1))
                    nc.scalar.activation(L.y_hi[:, t, b * 512:(b + 1) * 512], y_bank(b, t), ACT.Copy,
                                         scale=L.gate[:, t:t + 1]).then_inc(y_hi_done, 1)
            gathered_high(0)
            visits(act, rounds, visit)

        @block.vector
        def _(dve):
            rounds = load_rounds(dve)
            dve.sem_inc(up_read, 2)
            dve.sem_inc(added, KT)
            dve.sem_inc(y_lo_done, 2 * ST)
            st.split_lo(nc, c, dve, 0, 0)

            def pick(v):
                nc.vector.tensor_tensor(L.pick_hi[:], cols(c, CIOTA, SLOTS).unsqueeze(1).broadcast_to([128, NCH + 1, SLOTS]),
                                        L.number[:, :, ds(v, 1)].broadcast_to([128, NCH + 1, SLOTS]),
                                        ALU.is_equal).then_inc(picked, 1)

            def gathered_low(v):
                for k in range(KT):
                    dve.wait_ge(gathered, v * KT + (k + 1))
                    nc.vector.tensor_copy(L.xg_lo[:, k], up_bank(k % 2)).then_inc(xg_lo_done, 1)
                dve.wait_ge(slot_gated, v + 1)
                nc.vector.tensor_copy(L.next_gate[:], c.P[:, 6, 0:ST]).then_inc(gates_read, 1)

            def visit(v, e):
                dve.wait_ge(gates_read, v + 1)
                nc.vector.tensor_copy(L.gate[:], L.next_gate[:]).then_inc(own, 1)
                nc.vector.tensor_tensor(L.diag[:], cols(c, CI).unsqueeze(1).broadcast_to([128, NCH + 1, 128]),
                                        L.number[:, :, ds(v, 1)].broadcast_to([128, NCH + 1, 128]),
                                        ALU.mult).then_inc(diag_ready, 1)
                pick(v + 1)
                with dve.Fori(0, NF // 2) as i:
                    for j in range(2):
                        dve.wait_ge(c.hi_done, v * st.per + (i * 2 + (st.base + j + 2)))
                        nc.vector.tensor_tensor(c.w_lo[:, (j + 1) % 2], c.w_raw[:, (j + 1) % 2],
                                                c.w_hi[:, (j + 1) % 2].bitcast(F32), ALU.subtract).then_inc(c.lo_done, 1)
                        at = v * NF + (i * 2 + j)
                        dve.wait_ge(ready, v * (2 * NF) + (i * 4 + (2 * j + 2)))
                        dve.wait_ge(gate_read, at + 3)
                        nc.vector.tensor_tensor(L.sf[:, j, 0:SLOTS], L.sg[:, j, 0:SLOTS], up_bank(j), ALU.mult).then_inc(up_read, 1)
                        dve.wait_ge(f_hi_ready, at + 1)
                        nc.vector.tensor_tensor(L.f_lo[:, i * 2 + j], L.sf[:, j, 0:SLOTS], L.f_hi[:, i * 2 + j].bitcast(F32),
                                                ALU.subtract).then_inc(f_ready, 1)
                dve.wait_ge(spread, v + 1)
                for t in range(ST):
                    for bank, at, n in ((4, 0, TP), (5, TP, TS)):
                        nc.vector.tensor_scalar(L.place_hi[:, t, at:at + n], c.P[:, bank, 0:n], cols(c, CSLOT + t, 1), None,
                                                ALU.is_equal).then_inc(placed, 1)
                gathered_low(v + 1)
                for q in range(ND):
                    st.split_lo(nc, c, dve, v, NF + q + 1)
                dve.wait_ge(own, v + 1)
                for n, (b, t) in enumerate((b, t) for b in range(2) for t in range(ST)):
                    half = slice(b * 512, (b + 1) * 512)
                    dve.wait_ge(y_hi_done, v * (2 * ST) + (n + 1))
                    nc.vector.scalar_tensor_tensor(L.y_lo[:, t, half], y_bank(b, t), L.gate[:, t:t + 1],
                                                   L.y_hi[:, t, half].bitcast(F32), ALU.mult, ALU.subtract).then_inc(y_lo_done, 1)
                for k in range(KT):
                    dve.wait_ge(scattered, v * KT + (k + 1))
                    hk = halves(c.h[:, k])
                    nc.vector.tensor_tensor(hk, hk, slot(c, k % 2), ALU.add).then_inc(added, 1)
            pick(0)
            gathered_low(0)
            visits(dve, rounds, visit)




def project_phase(nc, c, name, st, sp_next, out):
    ready, evacuated = c.sem(f"{name}_ready"), c.sem(f"{name}_evacuated")
    with nc.Block() as block:
        @block.sync
        def _(sp):
            if st.n > 2:
                st.rest(c, sp)
            sp_next(sp)

        @block.tensor
        def _(pe):
            square_tensor(nc, c, pe, st, ready, evacuated)

        @block.scalar
        def _(act):
            act.sem_inc(evacuated, 4)
            st.split_hi(nc, c, act, 0, 0)

            def body(i, last):
                for j in range(2):
                    if not (last and j == 1):
                        st.split_hi(nc, c, act, i, j + 1)
                    for m in range(2):
                        g = 2 * j + m
                        act.wait_ge(ready, i * 4 + (g + 1))
                        nc.scalar.activation(halves(out[:, i * 4 + g]), slot(c, g), ACT.Copy).then_inc(evacuated, 1)
            over(act, st.n // 2, body)

        @block.vector
        def _(dve):
            st.split_lo(nc, c, dve, 0, 0)

            def body(i, last):
                for j in range(2):
                    if not (last and j == 1):
                        st.split_lo(nc, c, dve, i, j + 1)
            over(dve, st.n // 2, body)


def head_norm_phase(nc, c, tiles):
    sem = lambda s: c.sem(f"head_{s}")
    squared, summed, rooted, own, scaled = (sem(s) for s in ("squared", "summed", "rooted", "own", "scaled"))
    n = len(tiles)
    with nc.Block() as block:
        @block.scalar
        def _(act):
            def square(t):
                if t >= 2:
                    act.wait_ge(summed, t - 1)
                nc.scalar.activation(c.pair[:, t % 2], tiles[t][0], ACT.Square).then_inc(squared, 1)

            square(0)
            for t in range(n):
                if t + 1 < n:
                    square(t + 1)
                act.wait_ge(summed, t + 1)
                if t >= 2:
                    act.wait_ge(scaled, t - 1)
                nc.scalar.activation(halves(c.scratch[:, t % 2]), slot(c, t % 4), ACT.Sqrt, scale=1.0 / HD,
                                     bias=cols(c, CEPS, 1)).then_inc(rooted, 1)

        @block.tensor
        def _(pe):
            for t in range(n):
                pe.wait_ge(squared, t + 1)
                if t >= 4:
                    pe.wait_ge(rooted, t - 3)
                for b in range(2):
                    ins = pe.matmul(slot(c, t % 4)[:, b], cols(c, CBO), c.pair[:, t % 2, b * HALF:(b + 1) * HALF],
                                    start=True, stop=True)
                ins.then_inc(summed, 1)

        @block.vector
        def _(dve):
            for t, (x, gain) in enumerate(tiles):
                r = c.scratch[:, t % 2]
                dve.wait_ge(rooted, t + 1)
                nc.vector.reciprocal(r, r).then_inc(own, 1)
                dve.wait_ge(own, t + 1)
                nc.vector.scalar_tensor_tensor(x, x, c.vec[:, gain:gain + 1], r, ALU.mult, ALU.mult).then_inc(scaled, 1)


def rotary_phase(nc, c, L):
    sem = lambda s: c.sem(f"rotary_{s}")
    turned, own, done = sem("turned"), sem("own"), sem("done")
    cos, sin = cols(c, CCOS, NT), cols(c, CSIN, NT)
    n_q = BH // 2
    with nc.Block() as block:
        @block.tensor
        def _(pe):
            def product(s, w, x):
                for b in range(2):
                    ins = pe.matmul(slot(c, s)[:, b], w, x[:, b * HALF:(b + 1) * HALF], start=True, stop=True)
                return ins

            for t in range(n_q):
                if t >= 2:
                    pe.wait_ge(done, t - 1)
                product(t % 2, cols(c, CROT), L.q[:, t]).then_inc(turned, 1)
            for kv in range(BKV):
                pe.wait_ge(done, n_q + kv)
                x = L.kv[:, kv // 2]
                product(0, cols(c, CRD0 if kv % 2 == 0 else CRD1), x).then_inc(turned, 1)
                product(1, cols(c, CD0 if kv % 2 == 0 else CD1), x).then_inc(turned, 1)

        @block.vector
        def _(dve):
            chain = Chain(dve, own)
            for t in range(n_q):
                x, r = L.q[:, t], c.scratch[:, t % 2]
                dve.wait_ge(turned, t + 1)
                nc.vector.tensor_tensor(halves(r), slot(c, t % 2), halves(sin), ALU.mult)
                chain.link(nc.vector.tensor_tensor(x, x, cos, ALU.mult))
                nc.vector.tensor_tensor(x, x, r, ALU.add).then_inc(done, 1)
            for kv in range(BKV):
                x, r = L.k2[:, kv], c.scratch[:, kv % 2]
                dve.wait_ge(turned, n_q + 2 * kv + 2)
                nc.vector.tensor_tensor(halves(r), slot(c, 0), halves(sin), ALU.mult)
                chain.link(nc.vector.tensor_tensor(halves(x), slot(c, 1), halves(cos), ALU.mult))
                nc.vector.tensor_tensor(x, x, r, ALU.add).then_inc(done, 1)


def window_phase(nc, c, io, L):
    sem = lambda s: c.sem(f"window_{s}")
    turned, read, stored = sem("turned"), sem("read"), sem("stored")
    row = lambda ap: ap.rearrange("t h d -> t (h d)")
    with nc.Block() as block:
        @block.sync
        def _(sp):
            for name, cache, to in (("k", io["cache_k_win"], L.k_cache), ("v", io["cache_v_win"], L.v_cache)):
                sp.dma_start(to[:], cache.rearrange("b t h d -> t b (h d)")).then_inc(L.cache_loaded, 16)
                sp.dma_start(io[f"new_{name}_win_sample"][:, 0:WIN - 1], cache[:, 1:WIN]).then_inc(stored, 16)
            sp.dma_start(L.sinks[:], io["b_sinks"].broadcast_to([128, BH])).then_inc(L.cache_loaded, 16)
            sp.wait_ge(read, 8)
            sp.dma_start(row(io["new_v_win_prompt"][0]), L.v_tok[:, NCH - 1]).then_inc(stored, 16)
            sp.dma_start(row(io["new_k_win_prompt"][0]), L.k_rows[:, 0]).then_inc(stored, 16)
            for name, rows in (("k", L.k_rows[0:TS, 1]), ("v", L.v_new[0:TS])):
                sp.dma_start(io[f"new_{name}_win_sample"][:, WIN - 1].rearrange("b h d -> b (h d)"), rows).then_inc(stored, 16)
            sp.wait_ge(stored, 96)
            sp.wait_ge(L.cache_loaded, 48)

        @block.tensor
        def _(pe):
            ident = cols(c, CI)
            for n in range(NCH):
                for j in range(2):
                    ins = pe.transpose(c.P[:, n, j * 128:(j + 1) * 128], L.kv[:, 2 + j, n * 128:(n + 1) * 128], ident)
                ins.then_inc(turned, 1)
            for j in range(2):
                ins = pe.transpose(c.P[0:TS, 4, j * 128:(j + 1) * 128], L.kv[:, 2 + j, TP:NT], ident)
            ins.then_inc(turned, 1)
            for kv in range(BKV):
                ins = pe.transpose(c.P[:, 5, kv * 128:(kv + 1) * 128], L.k2[:, kv, TP - WIN:TP], ident)
            ins.then_inc(turned, 1)
            for kv in range(BKV):
                ins = pe.transpose(c.P[0:TS, 6, kv * 128:(kv + 1) * 128], L.k2[:, kv, TP:NT], ident)
            ins.then_inc(turned, 1)

        @block.vector
        def _(dve):
            def take(n, to, of):
                dve.wait_ge(turned, n)
                nc.vector.tensor_copy(to, of).then_inc(read, 1)
            for n in range(NCH):
                take(n + 1, L.v_tok[:, n], c.P[:, n, 0:256])
            take(NCH + 1, L.v_new[0:TS], c.P[0:TS, 4, 0:256])
            once = lambda ap: ap.rearrange("p (h u d) -> p h u d", h=BKV, u=2)[:, :, 0]
            heads = lambda ap: ap.rearrange("p (h d) -> p h d", h=BKV)
            take(NCH + 2, heads(L.k_rows[:, 0]), once(c.P[:, 5]))
            take(NCH + 3, heads(L.k_rows[0:TS, 1]), once(c.P[0:TS, 6]))
            nc.vector.memset(L.p_stat[:], 0.0).then_inc(read, 1)
            dve.wait_ge(L.cache_loaded, 48)
            nc.vector.tensor_tensor(L.sink_pick[:], L.sinks[:], cols(c, CHEAD, BH), ALU.mult).then_inc(read, 1)
            dve.wait_ge(read, 9)
            nc.vector.tensor_reduce(L.sink_rows[:], L.sink_pick[:], AX, ALU.add)


def attend_phase(nc, c, L):
    sem = lambda s: c.sem(f"attend_{s}")
    scored, shifted, weighed, divided, turned, placed, summed, out_hi, out_lo, own = (sem(s) for s in
        ("scored", "shifted", "weighed", "divided", "turned", "placed", "summed", "out_hi", "out_lo", "own"))
    N = NCH * BKV
    at = lambda i: (i // BKV, i % BKV)
    GQ = BH // BKV

    def keys(i):
        return 128 if at(i)[0] == 0 else 256

    def scores(i):
        return c.P[:, 2 * (i % 2):2 * (i % 2) + 2].rearrange("p b (g k) -> p (b g) k", g=2)[:, :, 0:keys(i)]

    probs = lambda i: L.probs[:, i % 2, :, 0:keys(i)]
    turned_probs = c.P[:, 4:6].rearrange("p b (g q) -> p (b g) q", g=4)
    stat = lambda i, n: L.p_stat[:, i % 2, n]
    MAX, NEGM, SINK, DEN = range(4)
    place = lambda g: g % 2 * 2 + g // 2
    by_place = lambda ap: ap.rearrange("p (t u) -> p u t", u=2)
    square = lambda ap: ap.rearrange("p (u t) -> p u t", u=2)
    out = lambda i: c.P[:, 6 + i % 2, 0:256].rearrange("p (t q) -> p t q", t=2)
    with nc.Block() as block:
        @block.tensor
        def _(pe):
            def score(i):
                blk, kv = at(i)
                if i >= 2:
                    pe.wait_ge(shifted, i - 1)
                for g in (0, 2, 1, 3):
                    rows = slice(g % 2 * HD, g % 2 * HD + HD)
                    ins = pe.matmul(scores(i)[:, place(g)], L.q[rows, 2 * kv + g // 2, blk * 128:(blk + 1) * 128],
                                    L.k2[rows, kv, (blk + 1) * 128 - keys(i):(blk + 1) * 128], start=True, stop=True)
                ins.then_inc(scored, 1)

            score(0)
            for i in range(N):
                blk, kv = at(i)
                if i + 1 < N:
                    score(i + 1)
                nb = keys(i) // 128
                pe.wait_ge(divided, i + 1)
                if i >= 1:
                    pe.wait_ge(placed, i)
                for g in range(GQ):
                    for k in range(nb):
                        ins = pe.transpose(turned_probs[:, 2 * g + k], probs(i)[:, g, k * 128:(k + 1) * 128], cols(c, CI))
                ins.then_inc(turned, 1)
                pe.wait_ge(placed, i + 1)
                if i >= 2:
                    pe.wait_ge(out_lo, i - 1)
                for g in range(GQ):
                    rows = slice(g % 2 * HD, g % 2 * HD + HD)
                    for k in range(nb):
                        ins = pe.matmul(out(i)[rows, g // 2], L.v_tok[:, blk - nb + 1 + k, kv * HD:(kv + 1) * HD],
                                        L.probs_t[:, 2 * place(g) + k], start=(k == 0), stop=(k == nb - 1))
                ins.then_inc(summed, 1)

        @block.vector
        def _(dve):
            def shift(i):
                blk, kv = at(i)
                if i >= 2:
                    dve.wait_ge(turned, i - 1)
                dve.wait_ge(scored, i + 1)
                mask = cols(c, CMASK + 256 - keys(i), keys(i)).unsqueeze(1).broadcast_to([128, GQ, keys(i)])
                nc.vector.scalar_tensor_tensor(probs(i), scores(i), HD ** -0.5, mask, ALU.mult, ALU.add).then_inc(shifted, 1)
                dve.wait_ge(shifted, i + 1)
                sink = by_place(L.sinks[:, kv * GQ:(kv + 1) * GQ])
                chain.link(nc.vector.tensor_reduce(stat(i, MAX), probs(i), AX, ALU.max))
                chain.link(nc.vector.tensor_tensor(square(stat(i, MAX)), square(stat(i, MAX)), sink, ALU.max))
                nc.vector.tensor_scalar(stat(i, NEGM), stat(i, MAX), -1.0, None, ALU.mult)
                nc.vector.tensor_tensor(square(stat(i, SINK)), sink, square(stat(i, MAX)), ALU.subtract).then_inc(L.maxed, 1)

            def low(i):
                blk, kv = at(i)
                dve.wait_ge(out_hi, i + 1)
                x = (slice(None), slice(2 * kv, 2 * kv + 2), slice(blk * 128, blk * 128 + 128))
                nc.vector.tensor_tensor(c.x_lo[x], out(i), c.x_hi[x].bitcast(F32), ALU.subtract).then_inc(out_lo, 1)

            chain = Chain(dve, own)
            shift(0)
            for i in range(N):
                if i + 1 < N:
                    shift(i + 1)
                dve.wait_ge(weighed, i + 1)
                chain.link(nc.vector.tensor_tensor(stat(i, DEN), stat(i, DEN), stat(i, SINK), ALU.add))
                chain.link(nc.vector.reciprocal(stat(i, DEN), stat(i, DEN)))
                nc.vector.tensor_tensor(probs(i), probs(i), stat(i, DEN).unsqueeze(2).broadcast_to([128, GQ, keys(i)]),
                                        ALU.mult).then_inc(divided, 1)
                if i >= 1:
                    low(i - 1)
            low(N - 1)

        @block.scalar
        def _(act):
            def weigh(i):
                act.wait_ge(L.maxed, i + 1)
                for g in range(GQ):
                    nc.scalar.activation(probs(i)[:, g], probs(i)[:, g], ACT.Exp, bias=stat(i, NEGM)[:, g:g + 1],
                                         accum_out=stat(i, DEN)[:, g:g + 1])
                nc.scalar.activation(stat(i, SINK), stat(i, SINK), ACT.Exp).then_inc(weighed, 1)

            weigh(0)
            for i in range(N):
                blk, kv = at(i)
                if i + 1 < N:
                    weigh(i + 1)
                act.wait_ge(turned, i + 1)
                if i >= 1:
                    act.wait_ge(summed, i)
                nb = keys(i) // 128
                view = lambda ap: ap.rearrange("p (g k) q -> p g k q", k=2)[:, :, 0:nb]
                nc.scalar.activation(view(L.probs_t[:]), view(turned_probs), ACT.Copy).then_inc(placed, 1)
                act.wait_ge(summed, i + 1)
                nc.scalar.activation(c.x_hi[:, 2 * kv:2 * kv + 2, blk * 128:(blk + 1) * 128], out(i), ACT.Copy)\
                    .then_inc(out_hi, 1)


def sample_attend_phase(nc, c, L):
    sem = lambda s: c.sem(f"one_{s}")
    pe_step, act_step, own = sem("pe_step"), sem("act_step"), sem("own")
    ident = cols(c, CI)
    qz, kT, sT, sT2, p, st = L.qz, L.k_turned, L.scores_t, L.scores_t2, L.one_probs, L.one_stat
    pairs = BH * TS
    hb = lambda ap: ap.rearrange("p (h b) -> p h b", b=TS)
    with nc.Block() as block:
        @block.tensor
        def _(pe):
            for par in range(2):
                ins = pe.matmul(c.P[:, 0, par * 64:par * 64 + 64], cols(c, CD0 if par == 0 else CD1), L.q[:, :, TP:NT],
                                start=True, stop=True)
            ins.then_inc(pe_step, 1)
            for b in range(TS):
                for j in range(2):
                    n = 2 * b + j
                    ins = pe.transpose(c.P[:, 1 + n // 4, n % 4 * 128:n % 4 * 128 + 128],
                                       L.k_cache[:, b, j * 128:(j + 1) * 128], ident)
            ins.then_inc(pe_step, 1)
            pe.wait_ge(own, 8)
            for kv in range(BKV):
                pe.matmul(c.P[0:TS, 6, kv * 32:kv * 32 + 32], L.k2[:, kv, TP:NT], qz[:, 4 * kv:4 * kv + 4, :]
                          .rearrange("p h b -> p (h b)"), start=True, stop=True)
            pe.wait_ge(act_step, 1)
            for b in range(TS):
                for j in range(2):
                    ins = pe.matmul(hb(c.P[:, 5, 0:pairs])[:, 8 * j:8 * j + 8, b], kT[:, 2 * b + j], qz[:, 8 * j:8 * j + 8, b],
                                    start=True, stop=True)
            ins.then_inc(pe_step, 1)
            pe.wait_ge(act_step, 3)
            pe.transpose(c.P[:, 0, 0:128], sT[:], ident)
            pe.transpose(c.P[:, 0, 128:136], sT2[0:TS], cols(c, CI)[0:TS, 0:TS]).then_inc(pe_step, 1)
            pe.wait_ge(own, 17)
            pe.transpose(c.P[:, 1, 0:128], p[:, 0:128], ident)
            pe.transpose(c.P[0:TS, 2, 0:128], p[:, 128:136], ident).then_inc(pe_step, 1)
            pe.wait_ge(act_step, 7)
            for b in range(TS):
                for j in range(2):
                    o = hb(c.P[:, 7, 0:pairs])[:, 8 * j:8 * j + 8, b]
                    pe.matmul(o, L.v_cache[:, b, j * 128:(j + 1) * 128], hb(sT[:])[:, 8 * j:8 * j + 8, b], start=True, stop=False)
                    ins = pe.matmul(o, L.v_new[0:TS, j * 128:(j + 1) * 128], hb(sT2[0:TS])[:, 8 * j:8 * j + 8, b],
                                    start=False, stop=True)
            ins.then_inc(pe_step, 1)
            pe.wait_ge(own, 19)
            pe.matmul(c.P[:, 0, 0:pairs], cols(c, CFOLD), L.one_out[:], start=True, stop=True).then_inc(pe_step, 1)

        @block.scalar
        def _(act):
            act.wait_ge(pe_step, 2)
            nc.scalar.activation(kT[:].rearrange("p (a n) k -> p a (n k)", a=4), c.P[:, 1:5], ACT.Copy).then_inc(act_step, 1)
            act.wait_ge(pe_step, 3)
            nc.scalar.activation(sT[:], c.P[:, 5, 0:pairs], ACT.Copy).then_inc(act_step, 1)
            nc.scalar.activation(sT2[0:TS], c.P[0:TS, 6, 0:pairs], ACT.Copy).then_inc(act_step, 1)
            act.wait_ge(own, 14)
            nc.scalar.activation(p[:], p[:], ACT.Exp, bias=st[:, 1:2], accum_out=st[:, 3:4]).then_inc(act_step, 1)
            nc.scalar.activation(st[:, 2:3], st[:, 2:3], ACT.Exp).then_inc(act_step, 1)
            act.wait_ge(pe_step, 5)
            nc.scalar.activation(sT[:], c.P[:, 1, 0:128], ACT.Copy).then_inc(act_step, 1)
            nc.scalar.activation(sT2[0:TS], c.P[0:TS, 2, 0:128], ACT.Copy).then_inc(act_step, 1)
            act.wait_ge(pe_step, 7)
            o = c.P[:, 0, 0:pairs].rearrange("p (t u b) -> p t u b", u=2, b=TS)
            for par in range(2):
                rows = slice(par * HD, par * HD + HD)
                nc.scalar.activation(c.x_hi[rows, :, TP:NT], o[rows, :, par], ACT.Copy).then_inc(act_step, 1)

        @block.vector
        def _(dve):
            chain = Chain(dve, own)
            dve.wait_ge(pe_step, 1)
            for par in range(2):
                for kp in range(2):
                    for a in range(2):
                        h0 = a * 8 + kp * 4
                        to = qz[:, h0:h0 + 4].rearrange("p (r u) b -> p r u b", u=2)[:, :, par]
                        t0 = par * 64 + (a * 4 + kp * 2) * TS
                        of = c.P[:, 0, t0:t0 + 2 * TS].rearrange("p (r b) -> p r b", r=2)
                        chain.link(nc.vector.tensor_scalar(to, of, cols(c, CHALF + kp, 1), None, ALU.mult))
            dve.wait_ge(pe_step, 4)
            chain.link(nc.vector.tensor_scalar(p[:, 0:128], c.P[:, 0, 0:128], HD ** -0.5, None, ALU.mult))
            chain.link(nc.vector.scalar_tensor_tensor(p[:, 128:136], c.P[:, 0, 128:136], HD ** -0.5, cols(c, CNEW, 8),
                                                      ALU.mult, ALU.add))
            chain.link(nc.vector.tensor_reduce(st[:, 0:1], p[:], AX, ALU.max))
            chain.link(nc.vector.tensor_tensor(st[:, 0:1], st[:, 0:1], L.sink_rows[:], ALU.max))
            chain.link(nc.vector.tensor_scalar(st[:, 1:2], st[:, 0:1], -1.0, None, ALU.mult))
            chain.link(nc.vector.tensor_tensor(st[:, 2:3], L.sink_rows[:], st[:, 0:1], ALU.subtract))
            dve.wait_ge(act_step, 5)
            chain.link(nc.vector.tensor_tensor(st[:, 3:4], st[:, 3:4], st[:, 2:3], ALU.add))
            chain.link(nc.vector.reciprocal(st[:, 3:4], st[:, 3:4]))
            chain.link(nc.vector.tensor_scalar(p[:], p[:], st[:, 3:4], None, ALU.mult))
            dve.wait_ge(pe_step, 6)
            kinds = lambda ap: ap.rearrange("p (a u n) -> p a u n", a=2, u=2)
            for kp in range(2):
                chain.link(nc.vector.tensor_scalar(kinds(L.one_out[:])[:, :, kp], kinds(c.P[:, 7, 0:pairs])[:, :, kp],
                                                   cols(c, CHALF + kp, 1), None, ALU.mult))
            dve.wait_ge(act_step, 9)
            o = c.P[:, 0, 0:pairs].rearrange("p (t u b) -> p t u b", u=2, b=TS)
            for par in range(2):
                rows = slice(par * HD, par * HD + HD)
                chain.link(nc.vector.tensor_tensor(c.x_lo[rows, :, TP:NT], o[rows, :, par],
                                                   c.x_hi[rows, :, TP:NT].bitcast(F32), ALU.subtract))


def route_phase(nc, c, io, L):
    sem = lambda s: c.sem(f"route_{s}")
    cleared, loaded, hi_ready, lo_ready, pe_step, act_step, own, turned, read = (sem(s) for s in
        ("cleared", "loaded", "hi_ready", "lo_ready", "pe_step", "act_step", "own", "turned", "read"))
    w, w_hi, w_lo = L.r_raw, L.r_hi, L.r_lo
    NB = NCH + 1
    lg, one, two, cand, tmp, chosen = (L.r_work[:, i] for i in range(6))
    m1, m2, g1, g2 = (L.r_stat[:, i] for i in range(4))
    per_e = lambda ap: ap.unsqueeze(2).broadcast_to([128, NB, NE])
    with nc.Block() as block:
        @block.gpsimd
        def _(pool):
            nc.gpsimd.memset(w[:], 0.0).then_inc(cleared, 1)
            nc.gpsimd.memset(L.r_work[:], 0.0).then_inc(cleared, 1)

        @block.sync
        def _(sp):
            sp.wait_ge(cleared, 1)
            sp.dma_start(w[:, :, 0:NE], io["moe_router"][0].rearrange("(k p) e -> p k e", p=128)).then_inc(loaded, 16)
            sp.dma_start(L.r_bias[:], io["moe_router_b"].broadcast_to([128, NE])).then_inc(loaded, 16)

        @block.tensor
        def _(pe):
            pe.wait_ge(lo_ready, 1)
            narrow_product(nc, pe, slot(c, 0), w_hi, w_lo, c).then_inc(pe_step, 1)
            pe.wait_ge(act_step, 1)
            for n in range(NCH):
                pe.transpose(c.P[:, 2, n * 128:(n + 1) * 128], L.r_logit[:, n * 128:(n + 1) * 128], cols(c, CI))
            pe.transpose(c.P[0:TS, 3, 0:128], L.r_logit[:, TP:NT], cols(c, CI)).then_inc(pe_step, 1)
            for n in range(NCH + 1):
                at, rows = n * 128, 128 if n < NCH else TS
                for part, x in enumerate((c.x_hi, c.x_lo)):
                    for b in range(2):
                        if n:
                            pe.wait_ge(read, 4 * n + 2 * part + b - 3)
                        for k in range(4):
                            ins = pe.transpose(c.P[0:rows, 4 + 2 * part + b, k * 128:(k + 1) * 128],
                                               x[:, 4 * b + k, at:at + rows].bitcast(F32), cols(c, CI))
                        ins.then_inc(turned, 1)
            pe.wait_ge(own, 21)
            chosen_flat = chosen.rearrange("p n e -> p (n e)")
            pe.matmul(c.P[:, 2, 0:NB * NE], cols(c, CU), chosen_flat, start=True, stop=True)
            pe.matmul(c.P[:, 3, 0:NB * NE], cols(c, CONE), chosen_flat, start=True, stop=True).then_inc(pe_step, 1)

        @block.scalar
        def _(act):
            act.wait_ge(loaded, 32)
            nc.scalar.activation(w_hi[:], w[:], ACT.Copy).then_inc(hi_ready, 1)
            act.wait_ge(pe_step, 1)
            nc.scalar.activation(halves(L.r_logit[:]), slot(c, 0), ACT.Copy).then_inc(act_step, 1)
            def token_major(n):
                rows = 128 if n < NCH else TS
                for part, to in enumerate((L.xt_hi, L.xt_lo)):
                    for b in range(2):
                        act.wait_ge(turned, 4 * n + 2 * part + b + 1)
                        nc.scalar.activation(to[0:rows, n, b * 512:(b + 1) * 512], c.P[0:rows, 4 + 2 * part + b],
                                             ACT.Copy).then_inc(read, 1)

            for n in range(3):
                token_major(n)
            act.wait_ge(own, 16)
            nc.scalar.activation(g2, g2, ACT.Exp).then_inc(act_step, 1)
            for n in range(3, NB):
                token_major(n)

        @block.vector
        def _(dve):
            dve.wait_ge(hi_ready, 1)
            nc.vector.tensor_tensor(w_lo[:], w[:], w_hi[:].bitcast(F32), ALU.subtract).then_inc(lo_ready, 1)
            chain = Chain(dve, own)
            tt = lambda to, a, b, op: chain.link(nc.vector.tensor_tensor(to, a, b, op))
            stt = lambda to, a, s, b, o0, o1: chain.link(nc.vector.scalar_tensor_tensor(to, a, s, b, o0, o1))
            dve.wait_ge(cleared, 2)
            dve.wait_ge(pe_step, 2)
            bias = L.r_bias[:].unsqueeze(1)
            tt(lg[:, 0:NCH], c.P[:, 2].rearrange("p (n r) -> p n r", n=NCH)[:, :, 0:NE], bias.broadcast_to([128, NCH, NE]), ALU.add)
            tt(lg[0:TS, NCH], c.P[0:TS, 3, 0:NE], L.r_bias[0:TS], ALU.add)
            number = cols(c, CEXP, NE).unsqueeze(1).broadcast_to([128, NB, NE])

            def pick(of, m, hot):
                chain.link(nc.vector.tensor_reduce(m, of, AX, ALU.max))
                tt(hot, of, per_e(m), ALU.is_equal)
                stt(cand, hot, -100.0, number, ALU.mult, ALU.add)
                chain.link(nc.vector.tensor_reduce(g1, cand, AX, ALU.min))
                tt(hot, cand, per_e(g1), ALU.is_equal)

            pick(lg, m1, one)
            stt(tmp, one, NEG, lg, ALU.mult, ALU.add)
            pick(tmp, m2, two)
            chain.link(nc.vector.tensor_copy(g1, m1))
            chain.link(nc.vector.tensor_copy(g2, m2))
            tt(g2, m2, m1, ALU.subtract)
            dve.wait_ge(act_step, 2)
            chain.link(nc.vector.tensor_scalar(g1, g2, 1.0, None, ALU.add))
            chain.link(nc.vector.reciprocal(g1, g1))
            tt(g2, g2, g1, ALU.mult)
            tt(chosen, one, two, ALU.add)
            chain.link(nc.vector.tensor_scalar(chosen[:, NCH], chosen[:, NCH], cols(c, CHEAD, 1), None, ALU.mult))
            tt(one, one, per_e(g1), ALU.mult)
            tt(two, two, per_e(g2), ALU.mult)
            tt(L.comb[:, :, 0:NE], one, two, ALU.add)
            chain.link(nc.vector.tensor_copy(L.comb[:, :, NE:NE + 1], L.comb[:, :, 0:1]))
            dve.wait_ge(pe_step, 3)
            of_block = lambda bank: c.P[:, bank, 0:NB * NE].rearrange("p (n e) -> p n e", n=NB)
            for n in range(NB):
                if n == 0:
                    chain.link(nc.vector.tensor_copy(tmp[:, 0], of_block(2)[:, 0]))
                    chain.link(nc.vector.tensor_copy(cand[:, 0], of_block(3)[:, 0]))
                else:
                    tt(tmp[:, n], cand[:, n - 1], of_block(2)[:, n], ALU.add)
                    tt(cand[:, n], cand[:, n - 1], of_block(3)[:, n], ALU.add)
            tt(tmp, tmp, chosen, ALU.mult)
            chain.link(nc.vector.memset(L.number[:], -1.0))
            for r in range(ROUNDS):
                nc.vector.tensor_scalar(L.number[:, :, r * NE:(r + 1) * NE], tmp, -1.0 - SLOTS * r, None, ALU.add)
            most, more = m1[:, 0:1], m2[:, 0:1]
            chain.link(nc.vector.tensor_reduce(most, cand[:, NCH], AX, ALU.max))
            chain.link(nc.vector.tensor_scalar(more, most, float(SLOTS), 1.0, ALU.is_gt, ALU.add))
            for r in range(2, ROUNDS):
                to = L.rounds[:] if r == ROUNDS - 1 else more
                chain.link(nc.vector.scalar_tensor_tensor(to, most, float(SLOTS * r), more, ALU.is_gt, ALU.add))


def store_phase(nc, c, io, L):
    sem = lambda s: c.sem(f"store_{s}")
    turned, read_a, read_v, stored = sem("turned"), sem("read_act"), sem("read_vector"), sem("stored")
    with nc.Block() as block:
        @block.tensor
        def _(pe):
            for t in range(NCH + 1):
                n = 128 if t < NCH else TS
                if t >= 4:
                    pe.wait_ge(read_a, 1)
                    pe.wait_ge(read_v, 1)
                for k in range(KT):
                    ins = pe.transpose(c.P[0:n, 2 * (t % 4) + k // 4, k % 4 * 128:k % 4 * 128 + 128],
                                       c.h[:, k, t * 128:t * 128 + n], cols(c, CI))
                ins.then_inc(turned, 1)

        @block.scalar
        def _(act):
            for t in range(NCH + 1):
                n = 128 if t < NCH else TS
                act.wait_ge(turned, t + 1)
                nc.scalar.activation(L.y[0:n, t, 0:512], c.P[0:n, 2 * (t % 4)], ACT.Copy).then_inc(read_a, 1)

        @block.vector
        def _(dve):
            for t in range(NCH + 1):
                n = 128 if t < NCH else TS
                dve.wait_ge(turned, t + 1)
                nc.vector.tensor_copy(L.y[0:n, t, 512:1024], c.P[0:n, 2 * (t % 4) + 1]).then_inc(read_v, 1)

        @block.sync
        def _(sp):
            for t in range(NCH + 1):
                sp.wait_ge(read_a, t + 1)
                sp.wait_ge(read_v, t + 1)
                to = io["y_prompt"][0, t * 128:(t + 1) * 128] if t < NCH else io["y_sample"].rearrange("b s d -> (b s) d")
                sp.dma_start(to, L.y[0:128 if t < NCH else TS, t]).then_inc(stored, 16)
            sp.wait_ge(stored, 16 * (NCH + 1))


def decoder_step(nc, io):
    k_p_n = lambda w: w.rearrange("(k p) n -> p k n", p=128)
    wide = lambda w: (lambda i, j: k_p_n(w)[:, :, ds(i * 512 + j * 256, 256)])
    s_in = Stream(0, (NQKV * 128 + D) // 256, wide(io["a_w_in"][0]))
    s_out = Stream(s_in.end, 4, wide(io["a_w_out"][0]))
    gu = gate_and_up(io["dense_w_gu"][0], 128)
    s_gu = Stream(s_out.end, NFF, lambda i, j: gu(i * 256 + j * 128))
    down = io["dense_w_down"][0].rearrange("(s k p) n -> s p k n", s=2, p=128)
    s_down = Stream(s_gu.end, 2 * KT, lambda i, j: down[j, :, :, ds(i * 128, 128)])
    s_kv = Stream(s_down.end, 2, wide(io["w_kv"]))
    s_q = Stream(s_kv.end, 4, wide(io["b_w_q"][0]))
    s_o = Stream(s_q.end, 4, wide(io["b_w_o"][0]))
    s_moe = ExpertStream(s_o.end, io["moe_w_gu"][0], io["moe_w_down"][0])
    with ExitStack() as whole:
        c = shared_buffers(nc, whole)
        L = Layer()

        def alloc(ctx, tag="", **shapes):
            return [ctx.enter_context(nc.sbuf_tensor(name + tag, shape, F32R if name.endswith(("_hi", "_lo")) else F32))
                    for name, shape in shapes.items()]

        nothing = lambda sp: None
        with ExitStack() as layer_a:
            (L.conv_w, L.conv_state, L.a_log, L.dt_bias, L.a_rate, L.qkv,
             L.z, L.edge, L.g_tok, L.b_tok, L.G_tok, L.gb_sample) = alloc(layer_a, conv_w=[128, 4 * NQKV], conv_state=[128, NQKV, 3 * TS], a_log=[AH, 1], dt_bias=[AH, 1],
                  a_rate=[AH, 1], qkv=[128, NQKV, NT], z=[128, AH, NT], edge=[128, NQKV, 11],
                  g_tok=[128, NCH, AH], b_tok=[128, NCH, AH], G_tok=[128, NCH, AH], gb_sample=[128, 2 * AH * TS])
            load_phase(nc, c, io, L, lambda sp: s_in.start(c, sp, wait=False))
            with ExitStack() as ctx:
                c.x_hi, c.x_lo = split_buffers(nc, ctx, "xa")
                with ExitStack() as inner:
                    L.u, L.y, L.from_state, L.state_term = alloc(inner, u=[128, 2, 3 + NT], y=[128, 2, NT], from_state=[128, NQKV, TS], state_term=[128, NQKV, TS])
                    norm_phase(nc, c, VA)
                    project_in_phase(nc, c, s_in, lambda sp: s_out.start(c, sp), L)
                with ExitStack() as inner:
                    L.ab_raw, L.ab_hi, L.ab_lo, L.spread = alloc(inner, ab_raw=[128, KT, 128], ab_hi=[128, KT, 128], ab_lo=[128, KT, 128], spread=[128, 128])
                    gates_phase(nc, c, io, L)
            with ExitStack() as ctx:
                L.edge_rows, L.norm = alloc(ctx, edge_rows=[11, NQKV * 128], norm=[128, 2, NT])
                edge_phase(nc, c, io, L)
                unit_phase(nc, c, L)
            with ExitStack() as ctx:
                as_heads = lambda ap: ap.rearrange("p a t -> p (a t)")[:, 0:AH * C].rearrange("p (h x) -> p h x", h=AH)
                bufs = [ctx.enter_context(nc.sbuf_tensor(f"delta_{i}", [128, AH, C], F32)) for i in range(13)]
                L.delta = bufs[:12] + [as_heads(c.pair[:]), as_heads(c.scratch[:]), bufs[12]]
                L.small = [ctx.enter_context(nc.sbuf_tensor(f"delta_small_{i}", [128, AH], F32)) for i in range(7)]
                delta_phase(nc, c, io, L)
            with ExitStack() as ctx:
                L.s_state, L.s_kq, L.s_k, L.s_row, L.s_small, L.s_mask = alloc(ctx, s_state=[128, AH * TS, 128], s_kq=[128, AH * TS, 2], s_k=[128, AH * TS],
                      s_row=[128, 2, 128], s_small=[128, 6, AH * TS], s_mask=[128, 2, 512])
                sample_delta_phase(nc, c, io, L)
            with ExitStack() as ctx:
                c.x_hi, c.x_lo = split_buffers(nc, ctx, "xo")
                [L.norm] = alloc(ctx, "_o", norm=[128, 2, NT])
                mixer_out_phase(nc, c, L)
                add_to_residual_phase(nc, c, "a_out", s_out, lambda sp: s_gu.start(c, sp))
        with ExitStack() as ctx:
            c.x_hi, c.x_lo = split_buffers(nc, ctx, "xf")
            L.f_hi, L.f_lo, L.table = alloc(ctx, f_hi=[128, NFF, NT], f_lo=[128, NFF, NT], table=[128, 1])
            L.sg, L.sf = c.pair, c.scratch
            norm_phase(nc, c, VF)
            dense_phase(nc, c, s_gu, s_down, lambda sp: s_kv.start(c, sp), L)
        with ExitStack() as ctx:
            c.x_hi, c.x_lo = split_buffers(nc, ctx, "xb")
            (L.q, L.kv, L.k2, L.v_tok, L.v_new, L.k_rows, L.k_cache,
             L.v_cache, L.sinks, L.sink_rows, L.sink_pick, L.probs, L.probs_t, L.p_stat) = alloc(ctx, q=[128, KT, NT], kv=[128, 4, NT], k2=[128, BKV, NT], v_tok=[128, NCH, 256], v_new=[128, 256],
                  k_rows=[128, 2, 256], k_cache=[128, TS, 256], v_cache=[128, TS, 256], sinks=[128, BH], sink_rows=[128, 1], sink_pick=[128, BH],
                  probs=[128, 2, 4, 256], probs_t=[128, 8, 128], p_stat=[128, 2, 4, 4])
            norm_phase(nc, c, VKV)
            project_phase(nc, c, "kv", s_kv, lambda sp: s_q.start(c, sp), L.kv)
            norm_phase(nc, c, VB)
            project_phase(nc, c, "q", s_q, lambda sp: s_o.start(c, sp), L.q)
            head_norm_phase(nc, c, [(L.q[:, t], VQ) for t in range(KT)] + [(L.kv[:, t], VK) for t in range(2)])
            rotary_phase(nc, c, L)
            L.cache_loaded, L.maxed = c.sem("cache_loaded"), c.sem("attend_maxed")
            window_phase(nc, c, io, L)
            attend_phase(nc, c, L)
            with ExitStack() as inner:
                L.qz, L.k_turned, L.scores_t, L.scores_t2, L.one_probs, L.one_stat, L.one_out = alloc(inner, qz=[128, BH, TS], k_turned=[128, 2 * TS, 128], scores_t=[128, 128], scores_t2=[128, 128],
                      one_probs=[128, 136], one_stat=[128, 4], one_out=[128, 128])
                sample_attend_phase(nc, c, L)
            add_to_residual_phase(nc, c, "b_out", s_o, lambda sp: s_moe.start(c, sp))
        with ExitStack() as ctx:
            L.xt_hi, L.xt_lo, L.number, L.comb = alloc(
                ctx, xt_hi=[128, NCH + 1, D], xt_lo=[128, NCH + 1, D], number=[128, NCH + 1, ROUNDS * NE + 1],
                comb=[128, NCH + 1, NE + 1])
            L.rounds = ctx.enter_context(nc.sbuf_tensor("rounds", [128, 1], I32))
            with ExitStack() as inner:
                c.x_hi, c.x_lo = split_buffers(nc, inner, "xm")
                L.r_raw, L.r_hi, L.r_lo, L.r_logit, L.r_bias, L.r_work, L.r_stat = alloc(
                    inner, r_raw=[128, KT, 128], r_hi=[128, KT, 128], r_lo=[128, KT, 128], r_logit=[128, NT],
                    r_bias=[128, NE], r_work=[128, 6, NCH + 1, NE], r_stat=[128, 4, NCH + 1])
                norm_phase(nc, c, VF + 8)
                route_phase(nc, c, io, L)
            with ExitStack() as inner:
                (L.xg_hi, L.xg_lo, L.f_hi, L.f_lo, L.pick_hi, L.place_hi, L.y_hi, L.y_lo, L.diag, L.gate, L.next_gate,
                 L.table) = alloc(
                    inner, "_moe", xg_hi=[128, KT, SLOTS], xg_lo=[128, KT, SLOTS], f_hi=[128, FE // 128, SLOTS],
                    f_lo=[128, FE // 128, SLOTS], pick_hi=[128, NCH + 1, SLOTS], place_hi=[128, SLOTS // 128, NT],
                    y_hi=[128, SLOTS // 128, D], y_lo=[128, SLOTS // 128, D], diag=[128, NCH + 1, 128],
                    gate=[128, SLOTS // 128], next_gate=[128, SLOTS // 128], table=[128, 1])
                L.passed = c.sem("moe_passed")
                moe_phase(nc, c, s_moe, L)
        with ExitStack() as ctx:
            [L.y] = alloc(ctx, "_out", y=[128, NCH + 1, D])
            store_phase(nc, c, io, L)


_INS = ["x_prompt", "x_sample", "state_conv", "state_delta", "cache_k_win", "cache_v_win", "a_norm", "a_w_in",
        "a_conv_w", "a_A_log", "a_dt_bias", "a_o_norm", "a_w_out", "kv_norm", "w_kv", "k_norm", "b_norm", "b_w_q",
        "b_q_norm", "b_sinks", "b_w_o", "ffn_norm", "dense_w_gu", "dense_w_down", "moe_router", "moe_router_b",
        "moe_w_gu", "moe_w_down", "constants"]
_OUTS = [("y_prompt", (1, TP, D)), ("y_sample", (TS, 1, D)), ("new_conv_prompt", (1, 1, 3, NQKV * 128)),
         ("new_conv_sample", (1, TS, 3, NQKV * 128)), ("new_delta_prompt", (1, 1, AH, DK, DK)),
         ("new_delta_sample", (1, TS, AH, DK, DK)), ("new_k_win_prompt", (1, WIN, BKV, HD)),
         ("new_k_win_sample", (TS, WIN, BKV, HD)), ("new_v_win_prompt", (1, WIN, BKV, HD)),
         ("new_v_win_sample", (TS, WIN, BKV, HD))]


def kernel(**inputs):
    import numpy as _np
    import concourse.bacc as _bacc
    from concourse.bass_utils import run_bass_kernel_spmd as _run

    nc = _bacc.Bacc("TRN2", target_bir_lowering=False, num_devices=1)
    arrays, io = {}, {}
    given = {**inputs, **constants()}
    for name in _INS:
        a = _np.ascontiguousarray(given[name])
        arrays[f"in_{name}_dram"] = a
        io[name] = nc.dram_tensor(f"in_{name}_dram", a.shape, F32, kind="ExternalInput").ap()
    for i, (name, shape) in enumerate(_OUTS):
        io[name] = nc.dram_tensor(f"out_{i}_dram", shape, F32, kind="ExternalOutput").ap()
    decoder_step(nc, io)
    r = _run(nc, [arrays], core_ids=[0])
    return tuple(r.results[0][f"out_{i}_dram"] for i in range(len(_OUTS)))
```
